# Optimizing a Trainium2 kernel written in Bass

```python
import math, functools
import jax, jax.numpy as jnp
from jax import lax
import numpy as np

D_MODEL = 1024
BATCH = 1
SEQ = 128
DEPTH = 2
DEC_BATCH = 1
DEC_SEQ = 256
PAST_LEN = 128

GRID_W = 64
N_EVEN = (DEPTH + 1) // 2
N_ODD = DEPTH // 2
D_CONV = D_MODEL // 2
CONV_W = 3
MLA_HEADS = 8
NOPE_DIM = 64
ROPE_DIM = 32
V_DIM = (D_MODEL // 2) // MLA_HEADS
QK_DIM = NOPE_DIM + ROPE_DIM
Q_RANK = 3 * D_MODEL // 8
KV_RANK = D_MODEL // 4
AX_FREQS = ROPE_DIM // 4
ROPE_BASE = 10000.0
Q_BLOCK = 128
EV_SPLITS = [D_CONV, 2 * D_CONV, 3 * D_CONV, 3 * D_CONV + Q_RANK, 3 * D_CONV + Q_RANK + KV_RANK]
EV_IN = 3 * D_CONV + Q_RANK + KV_RANK + ROPE_DIM
EV_MIX = D_CONV + MLA_HEADS * V_DIM
CHUNK = 128
D_GM = D_MODEL
GM_GROUPS = 8
GM_CH = D_GM // GM_GROUPS
N_EXPERTS = 16
N_GROUPS = 4
EXP_PER_GROUP = N_EXPERTS // N_GROUPS
TOP_K = 2
D_EXPERT = D_MODEL // 4
EPS = 1e-6

kernel_name = "hybrid_flow_prefix_conv_mla_gmlp_moe"

def rmsnorm(x, g):
    xf = x.astype(jnp.float32)
    y = xf * lax.rsqrt(jnp.mean(xf * xf, axis=-1, keepdims=True) + EPS)
    return y.astype(x.dtype) * g

def modulate(h, shift, scale):
    return h * (1 + scale) + shift

def short_conv(v, w):
    vp = jnp.pad(v, ((0, 0), (1, 1), (0, 0)))
    return vp[:, :-2] * w[0] + vp[:, 1:-1] * w[1] + vp[:, 2:] * w[2]

def axial_rope_tables(n_tokens, dtype):
    rows = n_tokens // GRID_W
    r = jnp.repeat(jnp.arange(rows, dtype=jnp.float32), GRID_W)
    col = jnp.tile(jnp.arange(GRID_W, dtype=jnp.float32), rows)
    inv = ROPE_BASE ** (-jnp.arange(AX_FREQS, dtype=jnp.float32) / AX_FREQS)
    ang = jnp.stack([r[:, None] * inv, col[:, None] * inv], axis=1)
    return jnp.cos(ang)[:, :, None, :].astype(dtype), jnp.sin(ang)[:, :, None, :].astype(dtype)

def axial_rope(x, cos, sin):
    xs = x.reshape(x.shape[:-1] + (2, 2, AX_FREQS))
    rot = jnp.stack([-xs[..., 1, :], xs[..., 0, :]], axis=-2)
    return (xs * cos + rot * sin).reshape(x.shape)

def block_attention(q, k, v):
    b, sq, h, dq = q.shape
    nb = sq // Q_BLOCK
    scale = QK_DIM ** -0.5
    qb = q.reshape(b, nb, Q_BLOCK, h, dq).transpose(1, 0, 2, 3, 4)

    def one(qi):
        s = jnp.einsum('bqhd,bkhd->bhqk', qi, k).astype(jnp.float32) * scale
        p = jax.nn.softmax(s, axis=-1).astype(v.dtype)
        return jnp.einsum('bhqk,bkhd->bqhd', p, v)

    o = lax.map(one, qb)
    return o.transpose(1, 0, 2, 3, 4).reshape(b, sq, h * v.shape[-1])

def even_mixer(h, w_in, conv_w, q_norm_g, w_q_up, kv_norm_g, w_kv_up, w_out, rope=None, ctx=None):
    bsz, s, _ = h.shape
    proj = h @ w_in
    b_g, c_g, v_in, q_a, kv_a, k_rope = jnp.split(proj, EV_SPLITS, axis=-1)
    y_conv = b_g * short_conv(c_g * v_in, conv_w)
    q = (rmsnorm(q_a, q_norm_g) @ w_q_up).reshape(bsz, s, MLA_HEADS, QK_DIM)
    q_nope, q_rope = q[..., :NOPE_DIM], q[..., NOPE_DIM:]
    ckv = rmsnorm(kv_a, kv_norm_g)
    if rope is not None:
        cos, sin = rope
        q_rope = axial_rope(q_rope, cos[:, None], sin[:, None])
        k_rope_used = axial_rope(k_rope, cos, sin)
    else:
        k_rope_used = k_rope
    keys_ckv, keys_kr = ckv, k_rope_used
    if ctx is not None:
        keys_ckv = jnp.concatenate([ckv, ctx[0]], axis=1)
        keys_kr = jnp.concatenate([k_rope_used, ctx[1]], axis=1)
    sk = keys_ckv.shape[1]
    kv = (keys_ckv @ w_kv_up).reshape(bsz, sk, MLA_HEADS, NOPE_DIM + V_DIM)
    k = jnp.concatenate([kv[..., :NOPE_DIM],
                         jnp.broadcast_to(keys_kr[:, :, None, :], (bsz, sk, MLA_HEADS, ROPE_DIM))], axis=-1)
    v = kv[..., NOPE_DIM:]
    attn = block_attention(jnp.concatenate([q_nope, q_rope], axis=-1), k, v)
    out = jnp.concatenate([y_conv, attn], axis=-1) @ w_out
    return out, ckv, k_rope

def odd_mixer(h, w_in, v_g, w_s, b_s, w_out):
    bsz, s, _ = h.shape
    z = jax.nn.gelu(h @ w_in, approximate=False)
    u, v = jnp.split(z, 2, axis=-1)
    v = rmsnorm(v, v_g)
    vc = v.reshape(bsz, s // CHUNK, CHUNK, GM_GROUPS, GM_CH)
    sg = jnp.einsum('gpq,bnqgc->bnpgc', w_s, vc) + b_s.T[None, None, :, :, None]
    return (u * sg.reshape(bsz, s, D_GM)) @ w_out

def moe(h, router_w, router_b, w1, w3, w2):
    bsz, s, d = h.shape
    t = h.reshape(-1, d)
    n = t.shape[0]
    scores = jax.nn.sigmoid((t @ router_w).astype(jnp.float32))
    sel = scores + router_b.astype(jnp.float32)
    grp = sel.reshape(n, N_GROUPS, EXP_PER_GROUP)
    gscore = lax.top_k(grp, TOP_K)[0].sum(-1)
    g_idx = jnp.argmax(gscore, axis=-1)
    sel_g = jnp.take_along_axis(grp, g_idx[:, None, None], axis=1)[:, 0]
    _, loc = lax.top_k(sel_g, TOP_K)
    e_idx = g_idx[:, None] * EXP_PER_GROUP + loc
    wts = jnp.take_along_axis(scores, e_idx, axis=1)
    wts = wts / jnp.sum(wts, axis=-1, keepdims=True)
    combine = jnp.sum(jax.nn.one_hot(e_idx, N_EXPERTS, dtype=jnp.float32) * wts[..., None], axis=1).astype(t.dtype)
    hid = jax.nn.silu(jnp.einsum('td,edf->tef', t, w1)) * jnp.einsum('td,edf->tef', t, w3)
    hid = hid * combine[:, :, None]
    return jnp.einsum('tef,efd->td', hid, w2).reshape(bsz, s, d)

def setup_inputs(seed: int = 0) -> dict:
    key = jax.random.key(seed)
    ks = iter(jax.random.split(key, 40))
    nrm = lambda shape, sc: jax.random.normal(next(ks), shape, jnp.float32) * sc
    D = D_MODEL
    return {
        "x_prompt": nrm((BATCH, SEQ, D), 1.0),
        "x_sample": nrm((DEC_BATCH, DEC_SEQ, D), 1.0),
        "cache_ckv": nrm((DEC_BATCH, N_EVEN, PAST_LEN, KV_RANK), 1.0),
        "cache_krope": nrm((DEC_BATCH, N_EVEN, PAST_LEN, ROPE_DIM), 1.0),
        "c": nrm((DEC_BATCH, D), 1.0),
        "c_ctx": nrm((D,), 1.0),
        "w_ada": nrm((DEPTH, D, 6 * D), 0.5 * D ** -0.5),
        "b_ada": nrm((DEPTH, 6 * D), 0.02),
        "g_mix": 1.0 + nrm((DEPTH, D), 0.02),
        "g_ffn": 1.0 + nrm((DEPTH, D), 0.02),
        "g_final": 1.0 + nrm((D,), 0.02),
        "ev_w_in": nrm((N_EVEN, D, EV_IN), D ** -0.5),
        "conv_w": nrm((N_EVEN, CONV_W, D_CONV), CONV_W ** -0.5),
        "q_norm_g": 1.0 + nrm((N_EVEN, Q_RANK), 0.02),
        "w_q_up": nrm((N_EVEN, Q_RANK, MLA_HEADS * QK_DIM), Q_RANK ** -0.5),
        "kv_norm_g": 1.0 + nrm((N_EVEN, KV_RANK), 0.02),
        "w_kv_up": nrm((N_EVEN, KV_RANK, MLA_HEADS * (NOPE_DIM + V_DIM)), KV_RANK ** -0.5),
        "ev_w_out": nrm((N_EVEN, EV_MIX, D), EV_MIX ** -0.5),
        "gm_w_in": nrm((N_ODD, D, 2 * D_GM), D ** -0.5),
        "gm_v_g": 1.0 + nrm((N_ODD, D_GM), 0.02),
        "gm_w_s": nrm((N_ODD, GM_GROUPS, CHUNK, CHUNK), CHUNK ** -0.5),
        "gm_b_s": 1.0 + nrm((N_ODD, GM_GROUPS, CHUNK), 0.02),
        "gm_w_out": nrm((N_ODD, D_GM, D), D_GM ** -0.5),
        "router_w": nrm((D, N_EXPERTS), D ** -0.5),
        "router_b": nrm((N_EXPERTS,), 0.01),
        "moe_w1": nrm((DEPTH, N_EXPERTS, D, D_EXPERT), D ** -0.5),
        "moe_w3": nrm((DEPTH, N_EXPERTS, D, D_EXPERT), D ** -0.5),
        "moe_w2": nrm((DEPTH, N_EXPERTS, D_EXPERT, D), D_EXPERT ** -0.5),
    }

def reference(x_prompt, x_sample, cache_ckv, cache_krope, c, c_ctx, w_ada, b_ada, g_mix, g_ffn, g_final,
              ev_w_in, conv_w, q_norm_g, w_q_up, kv_norm_g, w_kv_up, ev_w_out,
              gm_w_in, gm_v_g, gm_w_s, gm_b_s, gm_w_out, router_w, router_b, moe_w1, moe_w3, moe_w2):
    cos, sin = axial_rope_tables(x_sample.shape[1], x_sample.dtype)
    xp, xs = x_prompt, x_sample
    ckv_states, kr_states = [], []
    for l in range(DEPTH):
        mp = jnp.split((jax.nn.silu(c_ctx) @ w_ada[l] + b_ada[l])[None, None, :], 6, axis=-1)
        ms = jnp.split((jax.nn.silu(c) @ w_ada[l] + b_ada[l])[:, None, :], 6, axis=-1)
        hp = modulate(rmsnorm(xp, g_mix[l]), mp[0], mp[1])
        hs = modulate(rmsnorm(xs, g_mix[l]), ms[0], ms[1])
        i = l // 2
        if l % 2 == 0:
            ev = (ev_w_in[i], conv_w[i], q_norm_g[i], w_q_up[i], kv_norm_g[i], w_kv_up[i], ev_w_out[i])
            op, ckv, kr = even_mixer(hp, *ev)
            os_, _, _ = even_mixer(hs, *ev, rope=(cos, sin), ctx=(cache_ckv[:, i], cache_krope[:, i]))
            ckv_states.append(ckv)
            kr_states.append(kr)
        else:
            od = (gm_w_in[i], gm_v_g[i], gm_w_s[i], gm_b_s[i], gm_w_out[i])
            op = odd_mixer(hp, *od)
            os_ = odd_mixer(hs, *od)
        xp = xp + mp[2] * op
        xs = xs + ms[2] * os_
        hp = modulate(rmsnorm(xp, g_ffn[l]), mp[3], mp[4])
        hs = modulate(rmsnorm(xs, g_ffn[l]), ms[3], ms[4])
        xp = xp + mp[5] * moe(hp, router_w, router_b, moe_w1[l], moe_w3[l], moe_w2[l])
        xs = xs + ms[5] * moe(hs, router_w, router_b, moe_w1[l], moe_w3[l], moe_w2[l])
    y_prompt = rmsnorm(xp, g_final)
    y_sample = rmsnorm(xs, g_final)
    state_ckv = jnp.stack(ckv_states, axis=1)
    state_krope = jnp.stack(kr_states, axis=1)
    return (y_prompt, y_sample, state_ckv, state_krope)


_drawn_inputs = setup_inputs


def setup_inputs(seed=0):
    import zlib

    import numpy as np

    out = dict(_drawn_inputs(seed))
    spreads = {}
    factors = {'cache_krope': 3.249,
     'g_final': 2.916,
     'q_norm_g': 8.0,
     'kv_norm_g': 3.053,
     'gm_v_g': 2.997,
     'gm_b_s': 3.735}
    for name, (base, spread) in spreads.items():
        noise = np.random.default_rng([zlib.crc32(name.encode()), seed]).standard_normal(out[name].shape)
        drawn = base * np.exp(spread * noise) if base else spread * noise
        out[name] = __import__('jax').numpy.asarray(drawn.astype(out[name].dtype))
    for name, factor in factors.items():
        out[name] = (out[name] * factor).astype(out[name].dtype)
    return out
```

```python
from contextlib import ExitStack

import numpy as np
import concourse.bass as bass
from concourse import mybir

F32 = mybir.dt.float32
ALU = mybir.AluOpType
ACT = mybir.ActivationFunctionType
AX = mybir.AxisListType

P = 128
D = 1024
KD = D // P
TP, TS = 128, 256
T = TP + TS
NT = T // P
PAST = 128
NKEY = T + PAST
LAYERS = 2
HEADS, NOPE, ROPE, VD = 8, 64, 32, 64
QK = NOPE + ROPE
QR, KVR = 384, 256
NQ, NKV = QR // P, KVR // P
NE, NG, EPG = 16, 4, 4
F = 256
EPS = 1e-6
SCALE = QK ** -0.5

SLOTS = 4
SLOT = 6144
ADA_COLS = 768
ADA_TILES = ADA_COLS // P
HALF_TILES = 3 * KD
EV_TILES = 18
EV_ORDER = (["qa"] * 3 + ["kv"] * 2 + ["rope"] + ["c", "v"] * 4 + ["b"] * 4)

CHUNKS = ([("ada", (0, 0, c)) for c in range(4)] + [("ev_in", c) for c in range(3)] + [("qkv", 0)]
          + [("ev_out", c) for c in range(2)] + [("ada", (0, 1, c)) for c in range(4)]
          + [("moe", (0, e)) for e in range(NE)]
          + [("ada", (1, 0, c)) for c in range(4)] + [("gm_in", c) for c in range(4)]
          + [("gm_out", c) for c in range(2)] + [("ada", (1, 1, c)) for c in range(4)]
          + [("moe", (1, e)) for e in range(NE)])
CHUNK_AT = {key: n for n, key in enumerate(CHUNKS)}

PRODUCTS = (
    [("ada", 0, 0), ("norm", 0)] + [("ev_in", n) for n in range(6)] + [("q_norm",), ("kv_norm",)]
    + [("ev_in", n) for n in range(6, EV_TILES)]
    + [("q_up", h) for h in range(HEADS)] + [("k_up", j) for j in range(HEADS // 2)]
    + [("v_up", t) for t in range(NKEY // P)]
    + [key for s in range(HEADS + 2)
       for key in ([("score", s, 0), ("score", s, 1)] if s < HEADS else [])
       + ([("probs_t", s - 1, 0), ("probs_t", s - 1, 1)] if 1 <= s <= HEADS else [])
       + ([("attend", s - 2)] if s >= 2 else [])]
    + [("mix_out", 0, d) for d in range(KD)] + [("ada", 0, 1), ("norm", 1), ("router", 0)]
    + [("moe_t", 0, d) for d in range(KD)]
    + [("ada", 1, 0), ("norm", 2)] + [("gm_v", t, c) for c in range(2) for t in range(NT)]
    + [("gm_u", j) for j in range(KD)] + [("spatial", g) for g in range(KD)]
    + [("mix_out", 1, d) for d in range(KD)] + [("ada", 1, 1), ("norm", 3), ("router", 1)]
    + [("moe_t", 1, d) for d in range(KD)] + [("norm", 4)])
PRODUCT_AT = {key: n for n, key in enumerate(PRODUCTS)}
BANKS = 8


ROOTS = ("norm", "q_norm", "kv_norm")
RESIDUALS = ("mix_out", "moe_t")


def bank_of(key):
    return PRODUCT_AT[key] % BANKS, PRODUCT_AT[key] // BANKS


def takes(key):
    n = PRODUCT_AT[key]
    return sum(k[0] not in ROOTS + RESIDUALS for k in PRODUCTS[n % BANKS:n + 1:BANKS])


def roots(key):
    return sum(k[0] in ROOTS for k in PRODUCTS[:PRODUCT_AT[key] + 1])


def residuals(key):
    return sum(k[0] in RESIDUALS for k in PRODUCTS[:PRODUCT_AT[key] + 1])


def last_user(chunk):
    kind, i = chunk
    if kind == "ada":
        return ("ada", i[0], i[1])
    if kind == "ev_in":
        return ("ev_in", 6 * i + 5)
    if kind == "qkv":
        return ("v_up", NKEY // P - 1)
    if kind == "gm_in":
        return ("gm_v", NT - 1, i) if i < 2 else ("gm_u", 4 * (i - 2) + 3)
    return ("mix_out", 0 if kind == "ev_out" else 1, 4 * i + 3)


def build(nc, a, out):
    ctx = ExitStack()
    with ctx:
        def sb(name, shape):
            return ctx.enter_context(nc.sbuf_tensor(name, shape, F32))

        def sem(name):
            return ctx.enter_context(nc.semaphore(name))

        bank = [ctx.enter_context(nc.psum_tensor(f"bank{b}", [P, 512], F32)) for b in range(BANKS)]

        ring = sb("ring", [P, SLOTS, SLOT])
        xT = sb("xT", [P, KD, T])
        hT = sb("hT", [P, KD, T])
        qT = hT
        sq = sb("sq", [P, 4, T])
        rstd = sb("rstd", [P, T])
        rms = sb("rms", [P, T])
        cvec = sb("cvec", [P, KD, 2])
        csil = sb("csil", [P, KD, 2])
        b_ada = sb("b_ada_sb", [P, LAYERS * 2, HALF_TILES])
        gains = sb("gains_sb", [P, 5, KD])
        mod = sb("mod", [P, LAYERS * 2, HALF_TILES, 2])
        gain1 = sb("gain1", [P, LAYERS * 2, KD, 2])
        conv_w = sb("conv_w_sb", [P, 4, 3])
        qkv_g = sb("qkv_g_sb", [P, NQ + NKV])
        rope = sb("rope_sb", [P, T])
        ident = sb("ident_sb", [P, P])
        ones = sb("ones", [P, P])
        eps = sb("eps", [P, 1])
        router_w = sb("router_w_sb", [P, KD, NE])
        router_b = sb("router_b_sb", [P, NE])
        before = sb("before_sb", [P, EPG * EPG])
        work = sb("work", [P, 15744])

        at = [0]

        def carve(*shape):
            n = int(np.prod(shape))
            view = work[:, at[0]:at[0] + n]
            at[0] += n
            if len(shape) == 2:
                view = view.rearrange("p (a b) -> p a b", b=shape[1])
            return view

        mixT = carve(KD, T)
        q_a = carve(NQ, T)
        ckvT = carve(NKV, NKEY)
        k_rope = carve(T)
        rope_t = carve(T)
        values = carve(NKEY // P, 512)
        probs = carve(2, 7 * P)
        probs_t = carve(2, 7 * P)
        keys_at = at[0]
        kT = carve(HEADS, NKEY)
        at[0] = keys_at
        c_gate = carve(4, T)
        u_pad = carve(4, T + 4)
        conv_t = carve(T + 4)
        q_rstd = carve(T)
        at[0] = KD * T
        v_rows = carve(NT, D)
        uT = carve(KD, T)
        sg_t = carve(2, T)
        at[0] = 12672
        v_gain = carve(D)
        b_s = carve(KD, P)
        w_sT = carve(KD, P)
        at[0] = 0
        moe_out = carve(NT, D)
        silu = carve(2, F)
        hidden = carve(2, F)
        hiddenT = carve(2, F)
        weight_e = carve(SLOTS, NT)
        ss = sb("ss", [P, 8])
        s_score = sb("s_score", [P, NT * NE])
        s_sel = sb("s_sel", [P, NT * NE])
        s_gt = sb("s_gt", [P, NT * NE, EPG])
        s_ge = sb("s_ge", [P, NT * NE, EPG])
        s_top = sb("s_top", [P, NT * NE])
        s_g = sb("s_g", [P, NT * NG])
        s_ggt = sb("s_ggt", [P, NT * NG, NG])
        s_gge = sb("s_gge", [P, NT * NG, NG])
        s_den = sb("s_den", [P, NT])
        s_g4 = sb("s_g4", [P, NT * NG])
        combine = sb("combine", [P, NT, NE])
        sm_max = sb("sm_max", [P, 2, 4])
        sm_neg = sb("sm_neg", [P, 2, 4])
        sm_sum = sb("sm_sum", [P, 2, 4])
        sm_inv = sb("sm_inv", [P, 2, 4])

        ring_full = [sem(f"ring_full{s}") for s in range(SLOTS)]
        full = [sem(f"bank_full{b}") for b in range(BANKS)]
        taken = [sem(f"bank_taken{b}") for b in range(BANKS)]
        s_c, s_consts, s_x, s_cache, s_odd = (sem(n) for n in ("c_in", "consts_in", "x_in", "cache_in", "odd_in"))
        s_ones, s_csil = sem("ones_set"), sem("silu_c")
        s_mod = sem("mod_ready")
        s_sq, s_squ = sem("square_ready"), sem("square_used")
        s_rms, s_rstd, s_norm, s_hs, s_hp = (sem(n) for n in ("rms_ready", "rstd_ready", "norm_ready", "h_sample", "h_prompt"))
        s_qn, s_kn = sem("q_normed"), sem("kv_normed")
        s_qnope, s_qrope, s_krope, s_kropes = (sem(n) for n in ("q_nope", "q_rope", "k_rope_ready", "k_rope_spread"))
        s_even_key = sem("even_key")
        s_max, s_exp, s_prob = sem("neg_max"), sem("exp_done"), sem("probs_ready")
        s_res = sem("residual")
        s_vss, s_vrms, s_vn, s_sg = sem("v_squares"), sem("v_rms"), sem("v_normed"), sem("spatial_gated")
        s_ep, s_comb, s_we = sem("exp_router"), sem("combine_ready"), sem("expert_weight")
        s_up, s_silu, s_hid, s_tr, s_ht, s_dn, s_dt = (sem(n) for n in (
            "up_ready", "silu_ready", "hidden_ready", "hidden_t", "hidden_t_copied", "down_ready", "down_taken"))
        s_chain = sem("vector_step")
        s_achain = sem("scalar_step")
        s_out = sem("stored")
        s_y = sem("y_ready")
        s_ada = sem("ada_chunk_used")

        TOK = [(0, 0, TP), (1, TP, T)]

        def slot(chunk):
            return CHUNK_AT[chunk] % SLOTS, CHUNK_AT[chunk] // SLOTS

        block = ctx.enter_context(nc.Block())

        @block.sync
        def _(sp):
            def load(n):
                kind, i = CHUNKS[n]
                src = a["ada_w"][i[0], i[1], i[2]] if kind == "ada" else a[kind][i]
                if n >= SLOTS:
                    gone = CHUNKS[n - SLOTS]
                    if gone[0] == "moe":
                        sp.wait_ge(s_dn, (gone[1][0] * NE + gone[1][1] + 1) * NT)
                    elif gone[0] == "ada" and gone[1][2] < 3:
                        sp.wait_ge(s_ada, 3 * (2 * gone[1][0] + gone[1][1]) + gone[1][2] + 1)
                    else:
                        b, turn = bank_of(last_user(gone))
                        sp.wait_ge(full[b], turn + 1)
                sp.dma_start(ring[:, n % SLOTS, 0:src.shape[-1]], src).then_inc(ring_full[n % SLOTS], 16)

            def load_experts(l):
                base = CHUNK_AT[("moe", (l, 0))]
                for n in range(base, base + SLOTS):
                    kind, (_, e) = CHUNKS[n]
                    gone = last_user(CHUNKS[n - SLOTS])
                    b, turn = bank_of(gone)
                    if CHUNKS[n - SLOTS][1][2] < 3:
                        sp.wait_ge(s_ada, 3 * (2 * l + 1) + CHUNKS[n - SLOTS][1][2] + 1)
                    else:
                        sp.wait_ge(full[b], turn + 1)
                    sp.dma_start(ring[:, n % SLOTS, :], a["moe"][l, e]).then_inc(ring_full[n % SLOTS], 16)
                with sp.Fori(0, NE // SLOTS - 1) as i:
                    for j in range(SLOTS):
                        s = (base + j) % SLOTS
                        sp.wait_ge(s_dn, i * (SLOTS * NT) + (l * NE + j + 1) * NT)
                        sp.dma_start(ring[:, s, :], a["moe"][l, i * SLOTS + (SLOTS + j)]).then_inc(ring_full[s], 16)

            for l in range(LAYERS):
                first = 0 if l == 0 else CHUNK_AT[("moe", (0, NE - 1))] + 1
                for n in range(first, CHUNK_AT[("moe", (l, 0))]):
                    load(n)
                load_experts(l)

        @block.gpsimd
        def _(pool):
            pool.memset(ones[:, :], 1.0).then_inc(s_ones, 1)
            pool.memset(eps[:, :], EPS).then_inc(s_ones, 1)
            pool.memset(u_pad, 0.0).then_inc(s_ones, 1)

        @block.scalar
        def _(act):
            chain = [0]

            def step(ins):
                ins.then_inc(s_achain, 1)
                chain[0] += 1
                act.wait_ge(s_achain, chain[0])

            def product(*key):
                b, turn = bank_of(key)
                act.wait_ge(full[b], turn + 1)
                return bank[b]

            def take(ins, *key):
                ins.then_inc(taken[bank_of(key)[0]], 1)

            def wait_taken(*key):
                act.wait_ge(taken[bank_of(key)[0]], takes(key))

            act.dma_start(cvec[:], a["cvec"]).then_inc(s_c, 16)
            act.dma_start(xT[:], a["xT"]).then_inc(s_x, 16)
            smalls = [(b_ada, "b_ada"), (gains, "gains"), (conv_w, "conv_w"), (qkv_g, "qkv_g"), (rope, "rope"),
                      (ident, "ident"), (router_w, "router_w"), (router_b, "router_b"), (before, "before")]
            for tile, name in smalls:
                act.dma_start(tile[:], a[name]).then_inc(s_consts, 16)
            act.dma_start(ckvT[:, :, T:NKEY], a["cache_ckv"]).then_inc(s_cache, 16)

            act.wait_ge(s_c, 16)
            act.activation(csil[:], cvec[:], ACT.Silu).then_inc(s_csil, 1)

            def squares(q):
                for k in range(KD):
                    if q == 0 and k == 0:
                        act.wait_ge(s_x, 16)
                    elif q > 0:
                        act.wait_ge(s_res, (q - 1) * KD + k + 1)
                    if k >= 4:
                        act.wait_ge(s_squ, squ_n[0] + k - 3)
                    act.activation(sq[:, k % 4, :], xT[:, k, :], ACT.Square).then_inc(s_sq, 1)
                squ_n[0] += KD - 1

            def root(key, width):
                ps = product(*key)
                rms_n[0] += 1
                if rms_n[0] > 1:
                    act.wait_ge(s_rstd, rms_n[0] - 1)
                act.activation(rms[:, :], ps[:, 0:T], ACT.Sqrt, bias=eps[:, 0:1], scale=1.0 / width).then_inc(s_rms, 1)
                act.wait_ge(s_rms, rms_n[0])

            squ_n, rms_n = [0], [0]

            def norm(q):
                squares(q)
                if q == 0:
                    act.wait_ge(s_ones, 3)
                root(("norm", q), D)

            def modulate(q):
                act.wait_ge(s_mod, q + 1)
                for k in range(KD):
                    act.wait_ge(s_norm, q * KD + k + 1)
                    act.activation(hT[:, k, 0:TP], hT[:, k, 0:TP], ACT.Identity, bias=mod[:, q, k, 0:1],
                                   scale=gain1[:, q, k, 0:1]).then_inc(s_hp, 1)

            norm(0)
            modulate(0)

            act.wait_ge(s_consts, 16 * len(smalls))
            for j in range(NQ + NKV):
                wait_taken("ev_in", j)
                src = q_a[:, j, :] if j < NQ else ckvT[:, j - NQ, 0:T]
                if j == 4:
                    act.wait_ge(s_squ, squ_n[0] + 1)
                act.activation(sq[:, j % 4, :], src, ACT.Square).then_inc(s_sq, 1)
            squ_n[0] += NQ - 1 + NKV - 1
            root(("q_norm",), QR)
            root(("kv_norm",), KVR)
            act.wait_ge(s_kn, NKV)
            act.dma_start(out["state_ckv"], ckvT[:, :, 0:TP]).then_inc(s_out, 16)
            act.wait_ge(s_krope, 1)
            act.dma_start(out["state_krope"], k_rope[NOPE:QK, 0:TP]).then_inc(s_out, 16)
            for j in range(4):
                n = 6 + 2 * j
                take(act.activation(c_gate[:, j, :], product("ev_in", n)[:, 0:T], ACT.Identity), "ev_in", n)
            for h in range(HEADS):
                ps = product("q_up", h)
                act.activation(qT[0:NOPE, h, :], ps[0:NOPE, 0:T], ACT.Identity).then_inc(s_qnope, 1)
            wait_taken("ev_in", EV_TILES - 1)
            act.dma_start(kT[NOPE:QK, :, T:NKEY], a["cache_krope"]).then_inc(s_cache, 16)
            act.activation(kT[NOPE:QK, :, 0:T],
                           k_rope[NOPE:QK, :].rearrange("p (a t) -> p a t", a=1).to_broadcast([ROPE, HEADS, T]),
                           ACT.Identity).then_inc(s_kropes, 1)
            for j in range(HEADS // 2):
                ps = product("k_up", j)
                act.activation(kT[0:NOPE, 2 * j, :], ps[0:NOPE, :], ACT.Identity).then_inc(s_even_key, 1)
            for t in range(NKEY // P):
                take(act.activation(values[:, t, :], product("v_up", t)[:, :], ACT.Identity), "v_up", t)

            def exps(h):
                b = h % 2
                act.wait_ge(s_max, h + 1)
                if h >= 2:
                    product("probs_t", h - 2, 1)
                p0, p1 = product("score", h, 0), product("score", h, 1)
                for c, (ps, lo, hi, dst) in enumerate([(p0, 0, P, 0), (p0, P, 512, P), (p1, 0, 384, 512)]):
                    act.activation(probs[:, b, dst:dst + hi - lo], ps[:, lo:hi], ACT.Exp, bias=sm_neg[:, b, c:c + 1],
                                   scale=SCALE, accum_out=sm_sum[:, b, c:c + 1]).then_inc(s_exp, 1)

            for s in range(HEADS + 3):
                if s < HEADS:
                    exps(s)
                if 2 <= s < HEADS + 2:
                    h = s - 2
                    if h >= 2:
                        product("attend", h - 2)
                    take(act.activation(probs_t[:, h % 2, 0:512], product("probs_t", h, 0)[:, :], ACT.Identity),
                         "probs_t", h, 0)
                if s >= 3:
                    h = s - 3
                    take(act.activation(mixT[(h % 2) * VD:(h % 2) * VD + VD, 4 + h // 2, :],
                                        product("attend", h)[0:VD, 0:T], ACT.Identity), "attend", h)

            def experts_act(l):
                with act.Fori(0, NE // SLOTS) as i:
                    for j in range(SLOTS):
                        for t in range(NT):
                            n = j * NT + t
                            b = n % 2
                            base = l * NE * NT
                            act.wait_ge(s_up, i * (SLOTS * NT) + base + n + 1)
                            act.activation(silu[:, b, :], bank[b][:, 0:F], ACT.Silu).then_inc(s_silu, 1)
                            act.wait_ge(s_tr, i * (SLOTS * NT) + base + n + 1)
                            act.activation(hiddenT[:, b, :], bank[2 + b][:, 0:F], ACT.Identity).then_inc(s_ht, 1)

            def moe(l):
                take(act.activation(s_score[:, :], product("router", l)[:, 0:NT * NE], ACT.Exp, scale=-1.0), "router", l)
                experts_act(l)

            norm(1)
            modulate(1)
            product("mix_out", 0, KD - 1)
            act.dma_start(v_gain, a["v_gain"].to_broadcast([P, D])).then_inc(s_odd, 16)
            act.dma_start(b_s, a["b_s"].to_broadcast([P, KD, P])).then_inc(s_odd, 16)
            act.dma_start(w_sT, a["w_sT"]).then_inc(s_odd, 16)
            moe(0)
            norm(2)
            modulate(2)

            for c in range(2):
                for t in range(NT):
                    take(act.activation(v_rows[:, t, c * 512:c * 512 + 512], product("gm_v", t, c)[:, :], ACT.Gelu),
                         "gm_v", t, c)
            for j in range(KD):
                take(act.activation(uT[:, j, :], product("gm_u", j)[:, 0:T], ACT.Gelu), "gm_u", j)
                if j == 0:
                    wait_taken("gm_v", NT - 1, 1)
                    for t in range(NT):
                        step(act.activation(sq[:, :, :].rearrange("p a b -> p (a b)")[:, 0:D], v_rows[:, t, :],
                                            ACT.Square, accum_out=ss[:, t:t + 1]))
                    act.activation(ss[:, 3:3 + NT], ss[:, 0:NT], ACT.Sqrt, bias=eps[:, 0:1],
                                   scale=1.0 / D).then_inc(s_vrms, 1)

            norm(3)
            modulate(3)
            moe(1)
            norm(4)
            for k in range(KD):
                act.wait_ge(s_y, k + 1)
                act.dma_start(out["y"][:, k, :], hT[:, k, :]).then_inc(s_out, 16)
            act.wait_ge(s_out, 16 * (KD + 2))

        @block.vector
        def _(dve):
            chain = [0]

            def step(ins):
                ins.then_inc(s_chain, 1)
                chain[0] += 1
                dve.wait_ge(s_chain, chain[0])

            def product(*key):
                b, turn = bank_of(key)
                dve.wait_ge(full[b], turn + 1)
                return bank[b]

            def take(ins, *key):
                ins.then_inc(taken[bank_of(key)[0]], 1)

            def wait_taken(*key):
                dve.wait_ge(taken[bank_of(key)[0]], takes(key))

            def tt(o, x, y, op):
                return dve.tensor_tensor(o, x, y, op)

            def stt(o, x, s, y, op0, op1):
                return dve.scalar_tensor_tensor(out=o, in0=x, scalar=s, in1=y, op0=op0, op1=op1)

            def ada(l, half):
                q = 2 * l + half
                if q == 0:
                    dve.wait_ge(s_consts, 16 * 9)
                ps = product("ada", l, half)[:, 0:2 * HALF_TILES].rearrange("p (n s) -> p n s", s=2)
                bias = b_ada[:, q, :].rearrange("p (n a) -> p n a", a=1).to_broadcast([P, HALF_TILES, 2])
                take(tt(mod[:, q, :, :], ps, bias, ALU.add), "ada", l, half)
                wait_taken("ada", l, half)
                g = gains[:, q, :].rearrange("p (n a) -> p n a", a=1).to_broadcast([P, KD, 2])
                stt(gain1[:, q, :, :], mod[:, q, KD:2 * KD, :], 1.0, g, ALU.add, ALU.mult).then_inc(s_mod, 1)
                dve.wait_ge(s_mod, q + 1)

            rms_n = [0]

            def inverse(dst):
                rms_n[0] += 1
                dve.wait_ge(s_rms, rms_n[0])
                dve.reciprocal(dst, rms[:, :]).then_inc(s_rstd, 1)
                dve.wait_ge(s_rstd, rms_n[0])

            def norm(q):
                inverse(rstd[:, :])
                if q == 0:
                    dve.wait_ge(s_x, 16)
                for k in range(KD):
                    tt(hT[:, k, :], xT[:, k, :], rstd[:, :], ALU.mult).then_inc(s_norm, 1)
                for k in range(KD):
                    dve.wait_ge(s_norm, q * KD + k + 1)
                    dve.tensor_scalar(hT[:, k, TP:T], hT[:, k, TP:T], gain1[:, q, k, 1:2], mod[:, q, k, 1:2],
                                      ALU.mult, ALU.add).then_inc(s_hs, 1)

            def residual(l, half, d, src):
                q = 2 * l + half
                stt(xT[:, d, 0:TP], src[:, 0:TP], mod[:, q, 2 * KD + d, 0:1], xT[:, d, 0:TP], ALU.mult, ALU.add)
                stt(xT[:, d, TP:T], src[:, TP:T], mod[:, q, 2 * KD + d, 1:2], xT[:, d, TP:T], ALU.mult, ALU.add)\
                    .then_inc(s_res, 1)

            ada(0, 0)
            norm(0)

            for j in range(NQ + NKV):
                dst = q_a[:, j, :] if j < NQ else ckvT[:, j - NQ, 0:T]
                take(dve.tensor_copy(dst, product("ev_in", j)[:, 0:T]), "ev_in", j)
            ps = product("ev_in", 5)
            tt(rope_t[NOPE:QK, :], ps[NOPE:QK, 0:T], rope[NOPE:QK, :], ALU.mult)
            take(tt(k_rope[NOPE:QK, :], ps[QK:P, 0:T], rope[QK:P, :], ALU.mult), "ev_in", 5)
            wait_taken("ev_in", 5)
            tt(k_rope[NOPE:QK, :], k_rope[NOPE:QK, :], rope_t[NOPE:QK, :], ALU.add).then_inc(s_krope, 1)
            inverse(q_rstd)
            for j in range(NQ):
                stt(q_a[:, j, :], q_a[:, j, :], qkv_g[:, j:j + 1], q_rstd, ALU.mult, ALU.mult).then_inc(s_qn, 1)
            inverse(rstd[:, :])
            for j in range(NKV):
                stt(ckvT[:, j, 0:T], ckvT[:, j, 0:T], qkv_g[:, NQ + j:NQ + j + 1], rstd[:, :], ALU.mult,
                    ALU.mult).then_inc(s_kn, 1)
            dve.wait_ge(s_ones, 3)
            U = T + 4
            for j in range(4):
                wait_taken("ev_in", 6 + 2 * j)
                ps = product("ev_in", 7 + 2 * j)
                tt(u_pad[:, j, 1:1 + TP], ps[:, 0:TP], c_gate[:, j, 0:TP], ALU.mult)
                take(tt(u_pad[:, j, TP + 3:U - 1], ps[:, TP:T], c_gate[:, j, TP:T], ALU.mult), "ev_in", 7 + 2 * j)
            for j in range(4):
                wait_taken("ev_in", 7 + 2 * j)
                if j > 0:
                    wait_taken("ev_in", 13 + j)
                u = u_pad[:, j, :]
                t = conv_t[:, 1:U - 1]
                step(dve.tensor_scalar(t, u[:, 0:U - 2], conv_w[:, j, 0:1], None, ALU.mult))
                step(stt(t, u[:, 1:U - 1], conv_w[:, j, 1:2], t, ALU.mult, ALU.add))
                step(stt(t, u[:, 2:U], conv_w[:, j, 2:3], t, ALU.mult, ALU.add))
                ps = product("ev_in", 14 + j)
                tt(mixT[:, j, 0:TP], conv_t[:, 1:1 + TP], ps[:, 0:TP], ALU.mult)
                take(tt(mixT[:, j, TP:T], conv_t[:, TP + 3:U - 1], ps[:, TP:T], ALU.mult), "ev_in", 14 + j)
            for h in range(HEADS):
                ps = product("q_up", h)
                tt(qT[NOPE:QK, h, :], ps[NOPE:QK, 0:T], rope[NOPE:QK, :], ALU.mult)
                dve.wait_ge(s_qnope, h + 1)
                if h > 0:
                    dve.wait_ge(s_qrope, h)
                take(tt(rope_t[NOPE:QK, :], ps[QK:P, 0:T], rope[QK:P, :], ALU.mult), "q_up", h)
                wait_taken("q_up", h)
                tt(qT[NOPE:QK, h, :], qT[NOPE:QK, h, :], rope_t[NOPE:QK, :], ALU.add).then_inc(s_qrope, 1)
            for j in range(HEADS // 2):
                ps = product("k_up", j)
                dve.wait_ge(s_even_key, j + 1)
                take(dve.tensor_copy(kT[0:NOPE, 2 * j + 1, :], ps[NOPE:P, :]), "k_up", j)

            def maxima(h):
                b = h % 2
                p0, p1 = product("score", h, 0), product("score", h, 1)
                dve.reduce_max(sm_max[:, b, 0:1], p0[:, 0:P], AX.X)
                dve.reduce_max(sm_max[:, b, 1:2], p0[:, P:512], AX.X)
                step(dve.reduce_max(sm_max[:, b, 2:3], p1[:, 0:384], AX.X))
                dve.tensor_scalar(sm_neg[:, b, 0:3], sm_max[:, b, 0:3], -SCALE, None, ALU.mult).then_inc(s_max, 1)

            def normalise(h):
                b = h % 2
                dve.wait_ge(s_exp, 3 * h + 3)
                take(dve.reciprocal(sm_inv[:, b, 0:3], sm_sum[:, b, 0:3]), "score", h, 0)
                wait_taken("score", h, 0)
                for c, (lo, hi) in enumerate([(0, P), (P, 512), (512, 896)]):
                    ins = dve.tensor_scalar(probs[:, b, lo:hi], probs[:, b, lo:hi], sm_inv[:, b, c:c + 1], None, ALU.mult)
                take(ins, "score", h, 1)

            for s in range(HEADS + 2):
                if s < HEADS:
                    maxima(s)
                if 1 <= s <= HEADS:
                    normalise(s - 1)
                if s >= 2:
                    h = s - 2
                    if h >= 2:
                        product("attend", h - 2)
                    take(dve.tensor_copy(probs_t[:, h % 2, 512:896], product("probs_t", h, 1)[:, 0:384]), "probs_t", h, 1)

            def mix_out(l):
                for d in range(KD):
                    residual(l, 0, d, product("mix_out", l, d))

            def route(l):
                wait_taken("router", l)
                step(dve.tensor_scalar(s_score[:, :], s_score[:, :], 1.0, None, ALU.add))
                step(dve.reciprocal(s_score[:, :], s_score[:, :]))
                sc3 = s_score[:, :].rearrange("p (t e) -> p t e", e=NE)
                rb = router_b[:, :].rearrange("p (a e) -> p a e", a=1).to_broadcast([P, NT, NE])
                step(tt(s_sel[:, :].rearrange("p (t e) -> p t e", e=NE), sc3, rb, ALU.add))

                def ranks(score, groups, gt, ge, rank):
                    other = score.rearrange("p (g a j) -> p g a j", a=1, j=4).to_broadcast([P, groups, 4, 4])
                    own = score.rearrange("p (g i a) -> p g i a", i=4, a=1).to_broadcast([P, groups, 4, 4])
                    gt4 = gt[:].rearrange("p (g i) j -> p g i j", i=4)
                    ge4 = ge[:].rearrange("p (g i) j -> p g i j", i=4)
                    first = before[:, :].rearrange("p (a i j) -> p a i j", a=1, j=4).to_broadcast([P, groups, 4, 4])
                    tt(gt4, other, own, ALU.is_gt)
                    step(tt(ge4, other, own, ALU.is_equal))
                    step(tt(ge4, ge4, first, ALU.mult))
                    step(tt(gt4, gt4, ge4, ALU.add))
                    step(dve.tensor_reduce(rank, gt[:], AX.X, ALU.add))

                ranks(s_sel[:, :], NT * NG, s_gt, s_ge, s_top[:, :])
                step(dve.tensor_scalar(s_top[:, :], s_top[:, :], 2.0, None, ALU.is_lt))
                step(tt(s_sel[:, :], s_sel[:, :], s_top[:, :], ALU.mult))
                step(dve.tensor_reduce(s_g[:, :], s_sel[:, :].rearrange("p (g j) -> p g j", j=4), AX.X, ALU.add))
                ranks(s_g[:, :], NT, s_ggt, s_gge, s_g4[:, :])
                step(dve.tensor_scalar(s_g4[:, :], s_g4[:, :], 1.0, None, ALU.is_lt))
                top3 = s_top[:, :].rearrange("p (g j) -> p g j", j=4)
                best = s_g4[:, :].rearrange("p (g a) -> p g a", a=1).to_broadcast([P, NT * NG, 4])
                step(tt(top3, top3, best, ALU.mult))
                step(tt(s_score[:, :], s_score[:, :], s_top[:, :], ALU.mult))
                step(dve.tensor_reduce(s_den[:, :], sc3, AX.X, ALU.add))
                step(dve.reciprocal(s_den[:, :], s_den[:, :]))
                den = s_den[:, :].rearrange("p (t a) -> p t a", a=1).to_broadcast([P, NT, NE])
                tt(combine[:, :, :], sc3, den, ALU.mult).then_inc(s_comb, 1)
                dve.wait_ge(s_comb, l + 1)

            def experts_dve(l):
                dve.memset(moe_out, 0.0).then_inc(s_dt, 1)
                dve.wait_ge(s_dt, l * (NE * NT + 1) + 1)
                with dve.Fori(0, NE // SLOTS) as i:
                    for j in range(SLOTS):
                        e = i * SLOTS + j
                        dve.tensor_copy(weight_e[:, j, :],
                                        combine[:, :, bass.ds(e, 1)].rearrange("p t a -> p (t a)")).then_inc(s_we, 1)
                        dve.wait_ge(s_we, i * SLOTS + l * NE + j + 1)
                        for t in range(NT):
                            n = j * NT + t
                            base = l * NE * NT
                            b = n % 2
                            nth = i * (SLOTS * NT) + base + n
                            dve.wait_ge(s_silu, nth + 1)
                            stt(hidden[:, b, :], silu[:, b, :], weight_e[:, j, t:t + 1], bank[b][:, F:2 * F],
                                ALU.mult, ALU.mult).then_inc(s_hid, 1)
                            dve.wait_ge(s_dn, nth + 1)
                            for c in range(2):
                                ins = tt(moe_out[:, t, c * 512:c * 512 + 512], moe_out[:, t, c * 512:c * 512 + 512],
                                         bank[4 + 2 * b + c][:, :], ALU.add)
                            ins.then_inc(s_dt, 1)
                            dve.wait_ge(s_dt, nth + (l + 2))

            def moe(l):
                route(l)
                experts_dve(l)
                for d in range(KD):
                    residual(l, 1, d, product("moe_t", l, d))

            mix_out(0)
            ada(0, 1)
            norm(1)
            moe(0)
            ada(1, 0)
            norm(2)

            dve.wait_ge(s_odd, 48)
            dve.wait_ge(s_vrms, 1)
            step(dve.reciprocal(ss[:, 3:3 + NT], ss[:, 3:3 + NT]))
            for t in range(NT):
                stt(v_rows[:, t, :], v_rows[:, t, :], ss[:, 3 + t:4 + t], v_gain, ALU.mult, ALU.mult).then_inc(s_vn, 1)
            for g in range(KD):
                ps = product("spatial", g)[:, 0:T].rearrange("p (n q) -> p n q", q=P)
                bias = b_s[:, g, :].rearrange("p (a q) -> p a q", a=1).to_broadcast([P, NT, P])
                take(tt(sg_t[:, g % 2, :].rearrange("p (n q) -> p n q", q=P), ps, bias, ALU.add), "spatial", g)
                wait_taken("spatial", g)
                wait_taken("gm_u", g)
                tt(mixT[:, g, :], sg_t[:, g % 2, :], uT[:, g, :], ALU.mult).then_inc(s_sg, 1)
                dve.wait_ge(s_sg, g + 1)
            mix_out(1)
            ada(1, 1)
            norm(3)
            moe(1)
            inverse(rstd[:, :])
            for k in range(KD):
                stt(hT[:, k, :], xT[:, k, :], gains[:, 4, k:k + 1], rstd[:, :], ALU.mult, ALU.mult).then_inc(s_y, 1)

        @block.tensor
        def _(pe):
            def opened(*key):
                n = PRODUCT_AT[key]
                if n >= BANKS:
                    emptied(PRODUCTS[n - BANKS])
                return bank[n % BANKS]

            def emptied(key):
                if key[0] in RESIDUALS:
                    pe.wait_ge(s_res, residuals(key))
                elif key[0] in ROOTS:
                    pe.wait_ge(s_rms, roots(key))
                else:
                    pe.wait_ge(taken[bank_of(key)[0]], takes(key))

            def closed(ins, *key):
                ins.then_inc(full[bank_of(key)[0]], 1)

            def weights(chunk, columns):
                n = CHUNK_AT[chunk]
                pe.wait_ge(ring_full[n % SLOTS], 16 * (n // SLOTS + 1))
                return ring[:, n % SLOTS, 0:KD * columns].rearrange("p (k n) -> p k n", n=columns)

            def ada(l, half):
                if l == 0 and half == 0:
                    pe.wait_ge(s_csil, 1)
                ps = opened("ada", l, half)
                for c in range(4):
                    w = weights(("ada", (l, half, c)), ADA_COLS)
                    for j in range(ADA_TILES):
                        n = c * ADA_TILES + j
                        for k in range(KD):
                            mm = pe.matmul(ps[:, 2 * n:2 * n + 2], w[:, k, j * P:j * P + P], csil[:, k, :],
                                           start=(k == 0), stop=(k == KD - 1))
                    if c < 3:
                        mm.then_inc(s_ada, 1)
                closed(mm, "ada", l, half)

            sq_n = [0]

            def sum_squares(key, tiles):
                ps = opened(*key)
                for k in range(tiles):
                    sq_n[0] += 1
                    pe.wait_ge(s_sq, sq_n[0])
                    mm = pe.matmul(ps[:, 0:T], ones[:, :], sq[:, sq_at[0] % 4, :], start=(k == 0), stop=(k == tiles - 1))
                    sq_at[0] += 1
                    if k < tiles - 1:
                        mm.then_inc(s_squ, 1)
                closed(mm, *key)

            sq_at = [0]

            def norm(q):
                sq_at[0] = 0
                sum_squares(("norm", q), KD)

            def normed(q):
                pe.wait_ge(s_hs, (q + 1) * KD)
                pe.wait_ge(s_hp, (q + 1) * KD)

            def transposed(key, w, j, x):
                ps = opened(*key)
                for k in range(KD):
                    mm = pe.matmul(ps[:, 0:T], w[:, k, j * P:j * P + P], x[:, k, :], start=(k == 0), stop=(k == KD - 1))
                closed(mm, *key)

            pe.wait_ge(s_ones, 3)
            ada(0, 0)
            norm(0)
            normed(0)

            def ev_in(n):
                transposed(("ev_in", n), weights(("ev_in", n // 6), 768), n % 6, hT)

            for n in range(6):
                ev_in(n)
            sq_at[0] = 0
            sum_squares(("q_norm",), NQ)
            sum_squares(("kv_norm",), NKV)
            for n in range(6, EV_TILES):
                ev_in(n)
            n = CHUNK_AT[("qkv", 0)]
            pe.wait_ge(ring_full[n % SLOTS], 16 * (n // SLOTS + 1))
            w_q = ring[:, n % SLOTS, 0:NQ * HEADS * P].rearrange("p (k n) -> p k n", k=NQ)
            w_kv = ring[:, n % SLOTS, NQ * HEADS * P:NQ * HEADS * P + NKV * 1024].rearrange("p (k n) -> p k n", k=NKV)
            pe.wait_ge(s_qn, NQ)
            for h in range(HEADS):
                ps = opened("q_up", h)
                for k in range(NQ):
                    mm = pe.matmul(ps[:, 0:T], w_q[:, k, h * P:h * P + P], q_a[:, k, :], start=(k == 0), stop=(k == NQ - 1))
                closed(mm, "q_up", h)
            pe.wait_ge(s_kn, NKV)
            pe.wait_ge(s_cache, 32)
            for j in range(HEADS // 2):
                ps = opened("k_up", j)
                for k in range(NKV):
                    mm = pe.matmul(ps[:, :], w_kv[:, k, j * P:j * P + P], ckvT[:, k, :], start=(k == 0), stop=(k == NKV - 1))
                closed(mm, "k_up", j)
            for t in range(NKEY // P):
                ps = opened("v_up", t)
                for k in range(NKV):
                    mm = pe.matmul(ps[:, :], ckvT[:, k, t * P:t * P + P], w_kv[:, k, 512:1024], start=(k == 0), stop=(k == NKV - 1))
                closed(mm, "v_up", t)

            def score(h):
                pe.wait_ge(s_qrope, h + 1)
                if h == 0:
                    pe.wait_ge(s_kropes, 1)
                if h % 2 == 0:
                    pe.wait_ge(s_even_key, h // 2 + 1)
                else:
                    emptied(("k_up", h // 2))
                ps = opened("score", h, 0)
                pe.matmul(ps[:, 0:P], qT[0:QK, h, 0:TP], kT[0:QK, h, 0:TP], start=True, stop=True)
                mm = pe.matmul(ps[:, P:512], qT[0:QK, h, TP:TP + P], kT[0:QK, h, TP:NKEY], start=True, stop=True)
                closed(mm, "score", h, 0)
                ps = opened("score", h, 1)
                mm = pe.matmul(ps[:, 0:384], qT[0:QK, h, TP + P:T], kT[0:QK, h, TP:NKEY], start=True, stop=True)
                closed(mm, "score", h, 1)

            def turn(h):
                emptied(("score", h, 1))
                pr = probs[:, h % 2, :]
                tiles = [0] + [x for kt in range(3) for x in (1 + kt, 4 + kt)]
                for c, part in enumerate((tiles[:4], tiles[4:])):
                    ps = opened("probs_t", h, c)
                    for n, x in enumerate(part):
                        mm = pe.transpose(ps[:, n * P:n * P + P], pr[:, x * P:x * P + P], ident[:, :])
                    closed(mm, "probs_t", h, c)

            def attend(h):
                emptied(("probs_t", h, 0))
                emptied(("probs_t", h, 1))
                if h == 0:
                    for t in range(NKEY // P):
                        emptied(("v_up", t))
                pt = probs_t[:, h % 2, :]
                ps = opened("attend", h)
                pe.matmul(ps[0:VD, 0:TP], values[:, 0, h * VD:h * VD + VD], pt[:, 0:P], start=True, stop=True)
                for kt in range(3):
                    mm = pe.matmul(ps[0:VD, TP:T], values[:, 1 + kt, h * VD:h * VD + VD],
                                   pt[:, P + kt * TS:P + (kt + 1) * TS], start=(kt == 0), stop=(kt == 2))
                closed(mm, "attend", h)

            for s in range(HEADS + 2):
                if s < HEADS:
                    score(s)
                if 1 <= s <= HEADS:
                    turn(s - 1)
                if s >= 2:
                    attend(s - 2)

            def mix_out(l):
                for d in range(KD):
                    transposed(("mix_out", l, d), weights(("ev_out" if l == 0 else "gm_out", d // 4), 512), d % 4, mixT)

            emptied(("ev_in", EV_TILES - 1))
            for h in range(HEADS):
                emptied(("attend", h))
            mix_out(0)

            def router(l):
                ps = opened("router", l)
                if l == 0:
                    pe.wait_ge(s_consts, 16 * 9)
                for t in range(NT):
                    for k in range(KD):
                        mm = pe.matmul(ps[:, t * NE:t * NE + NE], hT[:, k, t * P:t * P + P], router_w[:, k, :],
                                       start=(k == 0), stop=(k == KD - 1))
                closed(mm, "router", l)

            def experts(l):
                for key in PRODUCTS[PRODUCT_AT[("router", l)] - BANKS + 1:PRODUCT_AT[("router", l)] + 1]:
                    emptied(key)
                chunk = CHUNK_AT[("moe", (l, 0))]
                base = l * NE * NT
                with pe.Fori(0, NE // SLOTS) as i:
                    def up(n):
                        j, t = n // NT, n % NT
                        s, turn = (chunk + j) % SLOTS, (chunk + j) // SLOTS
                        if t == 0:
                            pe.wait_ge(ring_full[s], i * 16 + 16 * (turn + 1))
                        for k in range(KD):
                            mm = pe.matmul(bank[n % 2][:, :], hT[:, k, t * P:t * P + P], ring[:, s, k * 512:k * 512 + 512],
                                           start=(k == 0), stop=(k == KD - 1))
                        mm.then_inc(s_up, 1)

                    def down(n):
                        b, s = n % 2, (chunk + n // NT) % SLOTS
                        pe.wait_ge(s_hid, i * (SLOTS * NT) + (base + n + 1))
                        for c in range(2):
                            tr = pe.transpose(bank[2 + b][:, c * P:c * P + P], hidden[:, b, c * P:c * P + P], ident[:, :])
                        tr.then_inc(s_tr, 1)
                        pe.wait_ge(s_ht, i * (SLOTS * NT) + (base + n + 1))
                        if n >= 1:
                            pe.wait_ge(s_dt, i * (SLOTS * NT) + (base + n + l))
                        for half in range(2):
                            for c in range(2):
                                at_ = KD * 512 + c * D + half * 512
                                mm = pe.matmul(bank[4 + 2 * b + half][:, :], hiddenT[:, b, c * P:c * P + P],
                                               ring[:, s, at_:at_ + 512], start=(c == 0), stop=(c == 1))
                        mm.then_inc(s_dn, 1)

                    up(0)
                    for n in range(SLOTS * NT):
                        if n + 1 < SLOTS * NT:
                            up(n + 1)
                        down(n)
                    pe.wait_ge(s_dt, i * (SLOTS * NT) + (base + SLOTS * NT + l))

            def moe(l):
                normed(2 * l + 1)
                router(l)
                experts(l)
                pe.wait_ge(s_dt, (l + 1) * (NE * NT + 1))
                for d in range(KD):
                    ps = opened("moe_t", l, d)
                    for t in range(NT):
                        mm = pe.transpose(ps[:, t * P:t * P + P], moe_out[:, t, d * P:d * P + P], ident[:, :])
                    closed(mm, "moe_t", l, d)

            ada(0, 1)
            norm(1)
            moe(0)
            ada(1, 0)
            norm(2)

            normed(2)
            for c in range(2):
                w = weights(("gm_in", c), 512)
                for t in range(NT):
                    ps = opened("gm_v", t, c)
                    for k in range(KD):
                        mm = pe.matmul(ps[:, :], hT[:, k, t * P:t * P + P], w[:, k, :], start=(k == 0), stop=(k == KD - 1))
                    closed(mm, "gm_v", t, c)
            for j in range(KD):
                transposed(("gm_u", j), weights(("gm_in", 2 + j // 4), 512), j % 4, hT)
            pe.wait_ge(s_vn, NT)
            pe.wait_ge(s_odd, 48)
            for g in range(KD):
                ps = opened("spatial", g)
                for t in range(NT):
                    mm = pe.matmul(ps[:, t * P:t * P + P], v_rows[:, t, g * P:g * P + P], w_sT[:, g, :], start=True, stop=True)
                closed(mm, "spatial", g)
            pe.wait_ge(s_sg, KD)
            mix_out(1)
            ada(1, 1)
            norm(3)
            moe(1)
            norm(4)


_LOADED = ("cvec", "xT", "b_ada", "gains", "conv_w", "qkv_g", "rope", "ident", "router_w", "router_b", "before",
           "cache_ckv", "cache_krope", "v_gain", "b_s", "w_sT", "ada_w", "ev_in", "qkv", "ev_out", "gm_in", "gm_out", "moe")


def tiles_first(w):
    return w.reshape(w.shape[0] // P, P, -1).transpose(1, 0, 2)


def rope_swap(w):
    return w.reshape(*w.shape[:-1], 2, 2, ROPE // 4)[..., ::-1, :].reshape(w.shape)


def laid_out(x_prompt, x_sample, cache_ckv, cache_krope, c, c_ctx, w_ada, b_ada, g_mix, g_ffn, g_final,
             ev_w_in, conv_w, q_norm_g, w_q_up, kv_norm_g, w_kv_up, ev_w_out,
             gm_w_in, gm_v_g, gm_w_s, gm_b_s, gm_w_out, router_w, router_b, moe_w1, moe_w3, moe_w2):
    o = {}
    o["xT"] = tiles_first(np.concatenate([x_prompt[0], x_sample[0]]).T)
    o["cvec"] = tiles_first(np.stack([c_ctx, c[0]], 1))
    cols = lambda v: v.reshape(-1, P).T
    o["b_ada"] = np.stack([cols(b_ada[l, h * 3 * D:(h + 1) * 3 * D]) for l in range(LAYERS) for h in range(2)], 1)
    o["gains"] = np.stack([cols(g) for g in (g_mix[0], g_ffn[0], g_mix[1], g_ffn[1], g_final)], 1)
    o["conv_w"] = conv_w[0].T.reshape(4, P, 3).transpose(1, 0, 2)
    o["qkv_g"] = np.concatenate([cols(q_norm_g[0]), cols(kv_norm_g[0])], 1)
    o["ident"] = np.eye(P, dtype=np.float32)
    o["before"] = np.broadcast_to(np.tril(np.ones((EPG, EPG), np.float32), -1).reshape(1, -1), (P, EPG * EPG))
    pos = np.arange(TS)
    freq = 10000.0 ** (-np.arange(ROPE // 4, dtype=np.float32) / np.float32(ROPE // 4))
    ang = np.stack([(pos // 64)[:, None] * freq, (pos % 64)[:, None] * freq], 1).astype(np.float32)
    cos = np.repeat(np.cos(ang)[:, :, None, :], 2, 2).reshape(TS, ROPE).T
    sin = (np.sin(ang)[:, :, None, :] * np.array([-1.0, 1.0])[None, None, :, None]).reshape(TS, ROPE).T
    rope = np.zeros((P, T), np.float32)
    rope[NOPE:QK, :TP] = 1.0
    rope[NOPE:QK, TP:] = cos
    rope[QK:P, TP:] = sin
    o["rope"] = rope
    o["router_w"] = tiles_first(router_w)
    o["router_b"] = np.broadcast_to(router_b[None], (P, NE))
    o["cache_ckv"] = tiles_first(cache_ckv[0, 0].T)
    o["cache_krope"] = np.broadcast_to(cache_krope[0, 0].T[:, None, :], (ROPE, HEADS, PAST))
    o["v_gain"] = gm_v_g[0][None]
    o["b_s"] = gm_b_s[0][None]
    o["w_sT"] = gm_w_s[0].transpose(2, 0, 1)
    chunked = lambda w, n: np.stack([tiles_first(w[:, i:i + n]).reshape(P, -1) for i in range(0, w.shape[1], n)])
    o["ada_w"] = np.stack([np.stack([chunked(w_ada[l][:, h * 3 * D:(h + 1) * 3 * D], ADA_COLS) for h in range(2)])
                           for l in range(LAYERS)])
    b, cg, v, qa, kva, kr = np.split(ev_w_in[0], [512, 1024, 1536, 1920, 2176], axis=1)
    cv = np.stack([cg.reshape(D, 4, P), v.reshape(D, 4, P)], 2).reshape(D, 1024)
    o["ev_in"] = chunked(np.concatenate([qa, kva, np.zeros((D, NOPE), np.float32), kr, rope_swap(kr), cv, b], 1), 768)
    q = w_q_up[0].reshape(QR, HEADS, QK)
    q = np.concatenate([q, rope_swap(q[..., NOPE:])], -1).reshape(QR, HEADS * P)
    kv = w_kv_up[0].reshape(KVR, HEADS, 2, NOPE).transpose(0, 2, 1, 3).reshape(KVR, 1024)
    o["qkv"] = np.concatenate([tiles_first(q).reshape(P, -1), tiles_first(kv).reshape(P, -1)], 1)[None]
    o["ev_out"] = chunked(ev_w_out[0], 512)
    o["gm_in"] = chunked(np.concatenate([gm_w_in[0][:, D:], gm_w_in[0][:, :D]], 1), 512)
    o["gm_out"] = chunked(gm_w_out[0], 512)
    w13 = np.concatenate([moe_w1, moe_w3], -1).reshape(LAYERS, NE, KD, P, 2 * F).transpose(0, 1, 3, 2, 4)
    w2 = moe_w2.reshape(LAYERS, NE, F // P, P, D).transpose(0, 1, 3, 2, 4)
    o["moe"] = np.concatenate([w13.reshape(LAYERS, NE, P, -1), w2.reshape(LAYERS, NE, P, -1)], -1)
    return o


def kernel(**inputs):
    import concourse.bacc as bacc
    from concourse.bass_utils import run_bass_kernel_spmd

    nc = bacc.Bacc("TRN2", target_bir_lowering=False, num_devices=1)
    host = laid_out(**{k: np.asarray(v) for k, v in inputs.items()})
    arrays, a = {}, {}
    for name in _LOADED:
        x = np.ascontiguousarray(host[name], dtype=np.float32)
        arrays[f"in_{name}"] = x
        a[name] = nc.dram_tensor(f"in_{name}", x.shape, F32, kind="ExternalInput").ap()
    shapes = {"y": (P, KD, T), "state_ckv": (P, NKV, TP), "state_krope": (ROPE, TP)}
    out = {n: nc.dram_tensor(f"out_{n}", s, F32, kind="ExternalOutput").ap() for n, s in shapes.items()}
    build(nc, a, out)
    r = run_bass_kernel_spmd(nc, [arrays], core_ids=[0]).results[0]
    y = np.asarray(r["out_y"]).transpose(2, 1, 0).reshape(T, D)
    ckv = np.asarray(r["out_state_ckv"]).transpose(2, 1, 0).reshape(1, 1, TP, KVR)
    krope = np.asarray(r["out_state_krope"]).T.reshape(1, 1, TP, ROPE)
    return y[None, :TP], y[None, TP:], ckv, krope
```

```python
from contextlib import ExitStack

import numpy as np
import concourse.bass as bass
from concourse import mybir

F32 = mybir.dt.float32
ALU = mybir.AluOpType
ACT = mybir.ActivationFunctionType
AX = mybir.AxisListType

P = 128
D = 1024
KD = D // P
TP, TS = 128, 256
T = TP + TS
NT = T // P
PAST = 128
NKEY = T + PAST
LAYERS = 2
HEADS, NOPE, ROPE, VD = 8, 64, 32, 64
QK = NOPE + ROPE
QR, KVR = 384, 256
NQ, NKV = QR // P, KVR // P
NE, NG, EPG = 16, 4, 4
F = 256
EPS = 1e-6
SCALE = QK ** -0.5

SLOTS = 4
SLOT = 6144
ADA_COLS = 768
ADA_TILES = ADA_COLS // P
HALF_TILES = 3 * KD
EV_TILES = 18
EV_ORDER = (["qa"] * 3 + ["kv"] * 2 + ["rope"] + ["c", "v"] * 4 + ["b"] * 4)

CHUNKS = ([("ada", (0, c)) for c in range(4)] + [("ev_in", c) for c in range(3)] + [("qkv", 0)]
          + [("ev_out", c) for c in range(2)] + [("ada", (q, c)) for q in (1, 2) for c in range(4)]
          + [("moe", (0, e)) for e in range(NE)]
          + [("ada", (3, c)) for c in range(4)] + [("gm_in", c) for c in range(4)]
          + [("gm_out", c) for c in range(2)] + [("moe", (1, e)) for e in range(NE)])
CHUNK_AT = {key: n for n, key in enumerate(CHUNKS)}

def ada_products(q):
    rows = [[("ada_row", q, c, i) for i in range(2)] for c in range(4)]
    turned = [[("ada_t", q, c)] for c in range(4)]
    return rows[0] + rows[1] + turned[0] + rows[2] + turned[1] + rows[3] + turned[2] + turned[3]


def dispatch_products(l):
    return ([("router", l)] + [("h_row", l, t, c) for t in range(NT) for c in range(2)] + [("slots", l)])


PRODUCTS = (
    ada_products(0) + [("norm", 0)] + [("ev_in", n) for n in range(6)] + [("q_norm",), ("kv_norm",)]
    + [("ev_in", n) for n in range(6, EV_TILES)]
    + [("q_up", h) for h in range(HEADS)] + [("k_up", j) for j in range(HEADS // 2)]
    + [("v_up", t) for t in range(NKEY // P)]
    + [key for s in range(HEADS + 2)
       for key in ([("score", s, 0), ("score", s, 1)] if s < HEADS else [])
       + ([("probs_t", s - 1, 0), ("probs_t", s - 1, 1)] if 1 <= s <= HEADS else [])
       + ([("attend", s - 2)] if s >= 2 else [])]
    + [("mix_out", 0, d) for d in range(KD)] + ada_products(1) + [("norm", 1)]
    + dispatch_products(0) + ada_products(2) + ada_products(3)
    + [("moe_t", 0, d) for d in range(KD)] + [("norm", 2)] + [("gm_v", t, c) for c in range(2) for t in range(NT)]
    + [("gm_u", j) for j in range(KD)] + [("spatial", g) for g in range(KD)]
    + [("mix_out", 1, d) for d in range(KD)] + [("norm", 3)] + dispatch_products(1)
    + [("moe_t", 1, d) for d in range(KD)] + [("norm", 4)])
PRODUCT_AT = {key: n for n, key in enumerate(PRODUCTS)}
BANKS = 8


ROOTS = ("norm", "q_norm", "kv_norm")
RESIDUALS = ("mix_out", "moe_t")


def bank_of(key):
    return PRODUCT_AT[key] % BANKS, PRODUCT_AT[key] // BANKS


def takes(key):
    n = PRODUCT_AT[key]
    return sum(k[0] not in ROOTS + RESIDUALS for k in PRODUCTS[n % BANKS:n + 1:BANKS])


def roots(key):
    return sum(k[0] in ROOTS for k in PRODUCTS[:PRODUCT_AT[key] + 1])


def residuals(key):
    return sum(k[0] in RESIDUALS for k in PRODUCTS[:PRODUCT_AT[key] + 1])


def last_user(chunk):
    kind, i = chunk
    if kind == "ada":
        return ("ada_row", i[0], i[1], 1)
    if kind == "ev_in":
        return ("ev_in", 6 * i + 5)
    if kind == "qkv":
        return ("v_up", NKEY // P - 1)
    if kind == "gm_in":
        return ("gm_v", NT - 1, i) if i < 2 else ("gm_u", 4 * (i - 2) + 3)
    return ("mix_out", 0 if kind == "ev_out" else 1, 4 * i + 3)


def build(nc, a, out):
    ctx = ExitStack()
    with ctx:
        def sb(name, shape):
            return ctx.enter_context(nc.sbuf_tensor(name, shape, F32))

        def sem(name):
            return ctx.enter_context(nc.semaphore(name))

        bank = [ctx.enter_context(nc.psum_tensor(f"bank{b}", [P, 512], F32)) for b in range(BANKS)]

        ring = sb("ring", [P, SLOTS, SLOT])
        xT = sb("xT", [P, KD, T])
        hT = sb("hT", [P, KD, T])
        qT = hT
        sq = sb("sq", [P, 4, T])
        rstd = sb("rstd", [P, T])
        rms = sb("rms", [P, T])
        cvec = sb("cvec", [P, KD, 2])
        csil = sb("csil", [P, KD, 2])
        b_ada = sb("b_ada_sb", [P, LAYERS * 2, HALF_TILES])
        gains = sb("gains_sb", [P, 5, KD])
        mod = sb("mod", [P, LAYERS * 2, HALF_TILES, 2])
        gain1 = sb("gain1", [P, LAYERS * 2, KD, 2])
        conv_w = sb("conv_w_sb", [P, 4, 3])
        qkv_g = sb("qkv_g_sb", [P, NQ + NKV])
        rope = sb("rope_sb", [P, T])
        ident = sb("ident_sb", [P, P])
        ones = sb("ones", [P, P])
        eps = sb("eps", [P, 1])
        router_w = sb("router_w_sb", [P, KD, NE])
        router_b = sb("router_b_sb", [P, NE])
        before = sb("before_sb", [P, EPG * EPG])
        work = sb("work", [P, 15744])

        at = [0]

        def carve(*shape):
            n = int(np.prod(shape))
            view = work[:, at[0]:at[0] + n]
            at[0] += n
            if len(shape) == 2:
                view = view.rearrange("p (a b) -> p a b", b=shape[1])
            return view

        mixT = carve(KD, T)
        q_a = carve(NQ, T)
        ckvT = carve(NKV, NKEY)
        k_rope = carve(T)
        rope_t = carve(T)
        values = carve(NKEY // P, 512)
        probs = carve(2, 7 * P)
        probs_t = carve(2, 7 * P)
        keys_at = at[0]
        kT = carve(HEADS, NKEY)
        at[0] = keys_at
        c_gate = carve(4, T)
        u_pad = carve(4, T + 4)
        conv_t = carve(T + 4)
        q_rstd = carve(T)
        at[0] = KD * T
        v_rows = carve(NT, D)
        uT = carve(KD, T)
        sg_t = carve(2, T)
        at[0] = 12672
        v_gain = carve(D)
        b_s = carve(KD, P)
        w_sT = carve(KD, P)
        at[0] = 0
        moe_out = carve(NT, D)
        silu = carve(2, F)
        hidden = carve(2, F)
        hiddenT = carve(2, F)
        weight_e = carve(SLOTS, NT)
        h_rows = moe_out
        h_slot = carve(2, D)
        h_slotT = carve(2, D)
        y_slot = carve(2, D)
        second = work[:, 3072 + 3 * 2 * F + SLOTS * NT:3072 + 3 * 2 * F + SLOTS * NT + NT * D]\
            .rearrange("p (t n) -> p t n", n=D)
        zero = sb("zero", [P, D // 4])
        ada_row = sb("ada_row", [2, 2, ADA_COLS])
        ss = sb("ss", [P, 8])
        s_slot = sb("s_slot", [P, NT * NE])
        s_tmp = sb("s_tmp", [P, NT * NE])
        s_eq = sb("s_eq", [P, NT * NE])
        s_first = sb("s_first", [P, 2, NT])
        weight = sb("weight", [P, LAYERS, 2, NT])
        index = ctx.enter_context(nc.sbuf_tensor("index", [P, LAYERS, 2, NT], mybir.dt.uint32))
        most = sb("most", [P, 1])
        most_i = ctx.enter_context(nc.sbuf_tensor("most_i", [P, LAYERS], mybir.dt.int32))
        expert_base = sb("expert_base_sb", [P, NT * NE])
        earlier = sb("earlier_sb", [P, P])
        h_slots = nc.dram_tensor("h_slots", [NE * P, D], F32).ap()
        y_slots = nc.dram_tensor("y_slots", [NE * P, D], F32).ap()
        s_score = sb("s_score", [P, NT * NE])
        s_sel = sb("s_sel", [P, NT * NE])
        s_gt = sb("s_gt", [P, NT * NE, EPG])
        s_ge = sb("s_ge", [P, NT * NE, EPG])
        s_top = sb("s_top", [P, NT * NE])
        s_g = sb("s_g", [P, NT * NG])
        s_ggt = sb("s_ggt", [P, NT * NG, NG])
        s_gge = sb("s_gge", [P, NT * NG, NG])
        s_den = sb("s_den", [P, NT])
        s_g4 = sb("s_g4", [P, NT * NG])
        combine = sb("combine", [P, NT, NE])
        sm_max = sb("sm_max", [P, 2, 4])
        sm_neg = sb("sm_neg", [P, 2, 4])
        sm_sum = sb("sm_sum", [P, 2, 4])
        sm_inv = sb("sm_inv", [P, 2, 4])

        ring_full = [sem(f"ring_full{s}") for s in range(SLOTS)]
        full = [sem(f"bank_full{b}") for b in range(BANKS)]
        taken = [sem(f"bank_taken{b}") for b in range(BANKS)]
        s_c, s_consts, s_x, s_cache, s_odd = (sem(n) for n in ("c_in", "consts_in", "x_in", "cache_in", "odd_in"))
        s_ones, s_csil = sem("ones_set"), sem("silu_c")
        s_mod = sem("mod_ready")
        s_sq, s_squ = sem("square_ready"), sem("square_used")
        s_rms, s_rstd, s_norm, s_hs, s_hp = (sem(n) for n in ("rms_ready", "rstd_ready", "norm_ready", "h_sample", "h_prompt"))
        s_qn, s_kn = sem("q_normed"), sem("kv_normed")
        s_qnope, s_qrope, s_krope, s_kropes = (sem(n) for n in ("q_nope", "q_rope", "k_rope_ready", "k_rope_spread"))
        s_even_key = sem("even_key")
        s_max, s_exp, s_prob = sem("neg_max"), sem("exp_done"), sem("probs_ready")
        s_res = sem("residual")
        s_vss, s_vrms, s_vn, s_sg = sem("v_squares"), sem("v_rms"), sem("v_normed"), sem("spatial_gated")
        s_comb, s_mask, s_index, s_zeroed = sem("combine_ready"), sem("mask_ready"), sem("index_ready"), sem("slots_zeroed")
        def layered(name):
            return [sem(f"{name}{l}") for l in range(LAYERS)]

        s_expert = layered("expert_done")
        s_we, s_dup, s_dsilu, s_dhid, s_dtr, s_dht, s_dn, s_dt = (layered(n) for n in (
            "all_weight", "all_up", "all_silu", "all_hidden", "all_hidden_t", "all_copied", "all_down", "all_summed"))
        s_spread, s_turn0, s_turn1, s_copy0, s_copy1 = (layered(n) for n in (
            "h_spread", "h_turned0", "h_turned1", "h_copied0", "h_copied1"))
        s_up, s_silu, s_hid, s_tr, s_ht, s_y0, s_y1, s_back, s_scaled, s_sum = (layered(n) for n in (
            "up_ready", "silu_ready", "hidden_ready", "hidden_t", "hidden_copied", "y_taken0", "y_taken1",
            "y_gathered", "first_scaled", "sum_ready"))
        s_h = [[sem(f"h_loaded{l}_{b}") for b in range(2)] for l in range(LAYERS)]
        s_yst = [[sem(f"y_stored{l}_{b}") for b in range(2)] for l in range(LAYERS)]
        s_chain = sem("vector_step")
        s_achain = sem("scalar_step")
        s_out = sem("stored")
        s_y = sem("y_ready")

        TOK = [(0, 0, TP), (1, TP, T)]

        def slot(chunk):
            return CHUNK_AT[chunk] % SLOTS, CHUNK_AT[chunk] // SLOTS

        def wait(eng, s, value):
            if not (isinstance(value, int) and value <= 0):
                eng.wait_ge(s, value)

        def rounds(eng, body):
            last = NE // SLOTS - 1
            body(0, True)
            with eng.Fori(1, last) as i:
                body(i, False)
            body(last, True)

        block = ctx.enter_context(nc.Block())

        @block.sync
        def _(sp):
            def wait_used(n):
                kind, i = CHUNKS[n - SLOTS]
                if kind == "moe":
                    sp.wait_ge(s_expert[i[0]], i[1] + 1)
                else:
                    b, turn = bank_of(last_user((kind, i)))
                    sp.wait_ge(full[b], turn + 1)

            def load(n):
                kind, i = CHUNKS[n]
                src = a["ada_w"][i[0], i[1]] if kind == "ada" else a["moe"][i[0], i[1]] if kind == "moe" else a[kind][i]
                if n >= SLOTS:
                    wait_used(n)
                sp.dma_start(ring[:, n % SLOTS, 0:src.shape[-1]], src).then_inc(ring_full[n % SLOTS], 16)

            def load_experts(l):
                base = CHUNK_AT[("moe", (l, 0))]
                for n in range(base, base + SLOTS):
                    load(n)
                with sp.Fori(0, NE // SLOTS - 1) as i:
                    for j in range(SLOTS):
                        s = (base + j) % SLOTS
                        sp.wait_ge(s_expert[l], i * SLOTS + (j + 1))
                        sp.dma_start(ring[:, s, :], a["moe"][l, i * SLOTS + (SLOTS + j)]).then_inc(ring_full[s], 16)

            for l in range(LAYERS):
                first = 0 if l == 0 else CHUNK_AT[("moe", (0, NE - 1))] + 1
                for n in range(first, CHUNK_AT[("moe", (l, 0))]):
                    load(n)
                load_experts(l)

        @block.gpsimd
        def _(pool):
            pool.memset(ones[:, :], 1.0).then_inc(s_ones, 1)
            pool.memset(eps[:, :], EPS).then_inc(s_ones, 1)
            pool.memset(u_pad, 0.0).then_inc(s_ones, 1)
            pool.memset(zero[:, :], 0.0).then_inc(s_ones, 1)
            pool.wait_ge(s_ones, 4)
            b, turn = bank_of(("q_norm",))
            pool.wait_ge(full[b], turn + 1)
            pool.dma_start(h_slots.rearrange("(p e) (c d) -> p (e c) d", p=P, c=4),
                           zero[:, :].rearrange("p (a d) -> p a d", a=1).to_broadcast([P, NE * 4, D // 4])).then_inc(s_zeroed, 16)
            pool.wait_ge(s_zeroed, 16)

            def spread(l):
                for t in range(NT):
                    for c in range(2):
                        key = ("h_row", l, t, c)
                        pool.wait_ge(taken[bank_of(key)[0]], takes(key))
                    for c in range(2):
                        pool.indirect_dma_start(h_slots, bass.IndirectOffsetOnAxis(ap=index[:, l, c, t:t + 1], axis=0),
                                                h_rows[:, t, :], None).then_inc(s_spread[l], 16)
                pool.wait_ge(s_spread[l], 16 * 2 * NT)

            def fetch(l, i, e):
                j = e % SLOTS
                wait(pool, s_turn1[l], i * SLOTS + (j - 1))
                pool.dma_start(h_slot[:, j % 2, :], h_slots[bass.ds(i * (SLOTS * P) + j * P, P), :])\
                    .then_inc(s_h[l][j % 2], 16)

            def gather(l):
                for b in range(2):
                    pool.wait_ge(s_yst[l][b], 16 * NE // 2)
                for t in range(NT):
                    for c, dst in ((0, moe_out), (1, second)):
                        pool.indirect_dma_start(dst[:, t, :], None, y_slots,
                                                bass.IndirectOffsetOnAxis(ap=index[:, l, c, t:t + 1], axis=0))\
                            .then_inc(s_back[l], 16)

            for l in range(LAYERS):
                pool.wait_ge(s_index, l + 1)
                count = pool.value_load(most_i[0:1, l:l + 1], min_val=0, max_val=T)
                with pool.If(count < P + 1):
                    spread(l)
                    rounds(pool, lambda i, static: [fetch(l, i, j) for j in range(SLOTS)])
                    gather(l)
                    pool.wait_ge(s_back[l], 16 * 2 * NT)

        @block.scalar
        def _(act):
            chain = [0]

            def step(ins):
                ins.then_inc(s_achain, 1)
                chain[0] += 1
                act.wait_ge(s_achain, chain[0])

            def product(*key):
                b, turn = bank_of(key)
                act.wait_ge(full[b], turn + 1)
                return bank[b]

            def take(ins, *key):
                ins.then_inc(taken[bank_of(key)[0]], 1)

            def wait_taken(*key):
                act.wait_ge(taken[bank_of(key)[0]], takes(key))

            act.dma_start(cvec[:], a["cvec"]).then_inc(s_c, 16)
            act.dma_start(xT[:], a["xT"]).then_inc(s_x, 16)
            smalls = [(b_ada, "b_ada"), (gains, "gains"), (conv_w, "conv_w"), (qkv_g, "qkv_g"), (rope, "rope"),
                      (ident, "ident"), (router_w, "router_w"), (router_b, "router_b"), (before, "before"),
                      (expert_base, "expert_base"), (earlier, "earlier")]
            for tile, name in smalls:
                act.dma_start(tile[:], a[name]).then_inc(s_consts, 16)
            act.dma_start(ckvT[:, :, T:NKEY], a["cache_ckv"]).then_inc(s_cache, 16)

            act.wait_ge(s_c, 16)
            act.activation(csil[:], cvec[:], ACT.Silu).then_inc(s_csil, 1)

            def squares(q):
                for k in range(KD):
                    if q == 0 and k == 0:
                        act.wait_ge(s_x, 16)
                    elif q > 0:
                        act.wait_ge(s_res, (q - 1) * KD + k + 1)
                    if k >= 4:
                        act.wait_ge(s_squ, squ_n[0] + k - 3)
                    act.activation(sq[:, k % 4, :], xT[:, k, :], ACT.Square).then_inc(s_sq, 1)
                squ_n[0] += KD - 1

            def root(key, width):
                ps = product(*key)
                rms_n[0] += 1
                if rms_n[0] > 1:
                    act.wait_ge(s_rstd, rms_n[0] - 1)
                act.activation(rms[:, :], ps[:, 0:T], ACT.Sqrt, bias=eps[:, 0:1], scale=1.0 / width).then_inc(s_rms, 1)
                act.wait_ge(s_rms, rms_n[0])

            squ_n, rms_n = [0], [0]

            def norm(q):
                squares(q)
                if q == 0:
                    act.wait_ge(s_ones, 3)
                root(("norm", q), D)

            def modulate(q):
                act.wait_ge(s_mod, q + 1)
                for k in range(KD):
                    act.wait_ge(s_norm, q * KD + k + 1)
                    act.activation(hT[:, k, 0:TP], hT[:, k, 0:TP], ACT.Identity, bias=mod[:, q, k, 0:1],
                                   scale=gain1[:, q, k, 0:1]).then_inc(s_hp, 1)

            def ada(q):
                for c in range(4):
                    if c >= 2:
                        product("ada_t", q, c - 2)
                    for i in range(2):
                        take(act.activation(ada_row[:, c % 2, i * 384:i * 384 + 384],
                                            product("ada_row", q, c, i)[0:2, 0:384], ACT.Identity), "ada_row", q, c, i)

            ada(0)
            norm(0)
            modulate(0)

            act.wait_ge(s_consts, 16 * len(smalls))
            for j in range(NQ + NKV):
                wait_taken("ev_in", j)
                src = q_a[:, j, :] if j < NQ else ckvT[:, j - NQ, 0:T]
                if j == 4:
                    act.wait_ge(s_squ, squ_n[0] + 1)
                act.activation(sq[:, j % 4, :], src, ACT.Square).then_inc(s_sq, 1)
            squ_n[0] += NQ - 1 + NKV - 1
            root(("q_norm",), QR)
            root(("kv_norm",), KVR)
            act.wait_ge(s_kn, NKV)
            act.dma_start(out["state_ckv"], ckvT[:, :, 0:TP]).then_inc(s_out, 16)
            act.wait_ge(s_krope, 1)
            act.dma_start(out["state_krope"], k_rope[NOPE:QK, 0:TP]).then_inc(s_out, 16)
            for j in range(4):
                n = 6 + 2 * j
                take(act.activation(c_gate[:, j, :], product("ev_in", n)[:, 0:T], ACT.Identity), "ev_in", n)
            for h in range(HEADS):
                ps = product("q_up", h)
                act.activation(qT[0:NOPE, h, :], ps[0:NOPE, 0:T], ACT.Identity).then_inc(s_qnope, 1)
            wait_taken("ev_in", EV_TILES - 1)
            act.dma_start(kT[NOPE:QK, :, T:NKEY], a["cache_krope"]).then_inc(s_cache, 16)
            act.activation(kT[NOPE:QK, :, 0:T],
                           k_rope[NOPE:QK, :].rearrange("p (a t) -> p a t", a=1).to_broadcast([ROPE, HEADS, T]),
                           ACT.Identity).then_inc(s_kropes, 1)
            for j in range(HEADS // 2):
                ps = product("k_up", j)
                act.activation(kT[0:NOPE, 2 * j, :], ps[0:NOPE, :], ACT.Identity).then_inc(s_even_key, 1)
            for t in range(NKEY // P):
                take(act.activation(values[:, t, :], product("v_up", t)[:, :], ACT.Identity), "v_up", t)

            def exps(h):
                b = h % 2
                act.wait_ge(s_max, h + 1)
                if h >= 2:
                    product("probs_t", h - 2, 1)
                p0, p1 = product("score", h, 0), product("score", h, 1)
                for c, (ps, lo, hi, dst) in enumerate([(p0, 0, P, 0), (p0, P, 512, P), (p1, 0, 384, 512)]):
                    act.activation(probs[:, b, dst:dst + hi - lo], ps[:, lo:hi], ACT.Exp, bias=sm_neg[:, b, c:c + 1],
                                   scale=SCALE, accum_out=sm_sum[:, b, c:c + 1]).then_inc(s_exp, 1)

            for s in range(HEADS + 3):
                if s < HEADS:
                    exps(s)
                if 2 <= s < HEADS + 2:
                    h = s - 2
                    if h >= 2:
                        product("attend", h - 2)
                    take(act.activation(probs_t[:, h % 2, 0:512], product("probs_t", h, 0)[:, :], ACT.Identity),
                         "probs_t", h, 0)
                if s >= 3:
                    h = s - 3
                    take(act.activation(mixT[(h % 2) * VD:(h % 2) * VD + VD, 4 + h // 2, :],
                                        product("attend", h)[0:VD, 0:T], ACT.Identity), "attend", h)

            def experts_all(l):
                with act.Fori(0, NE // SLOTS) as i:
                    for n in range(SLOTS * NT):
                        b = n % 2
                        act.wait_ge(s_dup[l], i * (SLOTS * NT) + (n + 1))
                        act.activation(silu[:, b, :], bank[b][:, 0:F], ACT.Silu).then_inc(s_dsilu[l], 1)
                        act.wait_ge(s_dtr[l], i * (SLOTS * NT) + (n + 1))
                        act.activation(hiddenT[:, b, :], bank[2 + b][:, 0:F], ACT.Identity).then_inc(s_dht[l], 1)

            def copy_h(l, i, e):
                b = e % 2
                act.wait_ge(s_turn0[l], i * SLOTS + (e + 1))
                act.activation(h_slotT[:, b, 0:512], bank[2][:, :], ACT.Identity).then_inc(s_copy0[l], 1)

            def silus(l, i, e):
                act.wait_ge(s_up[l], i * SLOTS + (e + 1))
                act.activation(silu[:, e % 2, :], bank[e % 2][:, 0:F], ACT.Silu).then_inc(s_silu[l], 1)

            def experts_routed(l):
                for e in range(2):
                    copy_h(l, 0, e)
                silus(l, 0, 0)

                def round_(i, static):
                    for j in range(SLOTS):
                        b = j % 2
                        last = static and i > 0
                        act.wait_ge(s_tr[l], i * SLOTS + (j + 1))
                        act.activation(hiddenT[:, b, :], bank[6 + b][:, 0:F], ACT.Identity).then_inc(s_ht[l], 1)
                        if not (last and j == SLOTS - 1):
                            silus(l, i, j + 1)
                        if not (last and j >= SLOTS - 2):
                            copy_h(l, i, j + 2)
                        act.wait_ge(s_expert[l], i * SLOTS + (j + 1))
                        wait(act, s_yst[l][b], i * 32 + 16 * (j // 2))
                        act.activation(y_slot[:, b, 0:512], bank[4][:, :], ACT.Identity).then_inc(s_y0[l], 1)
                        act.wait_ge(s_y0[l], i * SLOTS + (j + 1))
                        act.wait_ge(s_y1[l], i * SLOTS + (j + 1))
                        act.dma_start(y_slots[bass.ds(i * (SLOTS * P) + j * P, P), :], y_slot[:, b, :])\
                            .then_inc(s_yst[l][b], 16)

                rounds(act, round_)
                act.wait_ge(s_back[l], 16 * 2 * NT)
                for t in range(NT):
                    act.activation(moe_out[:, t, :], moe_out[:, t, :], ACT.Identity, scale=weight[:, l, 0, t:t + 1])\
                        .then_inc(s_scaled[l], 1)

            def dispatch(l):
                take(act.activation(s_score[:, :], product("router", l)[:, 0:NT * NE], ACT.Exp, scale=-1.0), "router", l)
                for t in range(NT):
                    key = ("h_row", l, t, 0)
                    take(act.activation(h_rows[:, t, 0:512], product(*key)[:, :], ACT.Identity), *key)

            def moe(l):
                act.wait_ge(s_index, l + 1)
                count = act.value_load(most_i[0:1, l:l + 1], min_val=0, max_val=T)
                with act.If(count < P + 1):
                    experts_routed(l)
                with act.Else():
                    experts_all(l)

            ada(1)
            norm(1)
            modulate(1)
            product("mix_out", 0, KD - 1)
            act.dma_start(v_gain, a["v_gain"].to_broadcast([P, D])).then_inc(s_odd, 16)
            act.dma_start(b_s, a["b_s"].to_broadcast([P, KD, P])).then_inc(s_odd, 16)
            act.dma_start(w_sT, a["w_sT"]).then_inc(s_odd, 16)
            dispatch(0)
            ada(2)
            moe(0)
            ada(3)
            norm(2)
            modulate(2)

            for c in range(2):
                for t in range(NT):
                    take(act.activation(v_rows[:, t, c * 512:c * 512 + 512], product("gm_v", t, c)[:, :], ACT.Gelu),
                         "gm_v", t, c)
            for j in range(KD):
                take(act.activation(uT[:, j, :], product("gm_u", j)[:, 0:T], ACT.Gelu), "gm_u", j)
                if j == 0:
                    wait_taken("gm_v", NT - 1, 1)
                    for t in range(NT):
                        step(act.activation(sq[:, :, :].rearrange("p a b -> p (a b)")[:, 0:D], v_rows[:, t, :],
                                            ACT.Square, accum_out=ss[:, t:t + 1]))
                    act.activation(ss[:, 3:3 + NT], ss[:, 0:NT], ACT.Sqrt, bias=eps[:, 0:1],
                                   scale=1.0 / D).then_inc(s_vrms, 1)

            norm(3)
            modulate(3)
            dispatch(1)
            moe(1)
            norm(4)
            for k in range(KD):
                act.wait_ge(s_y, k + 1)
                act.dma_start(out["y"][:, k, :], hT[:, k, :]).then_inc(s_out, 16)
            act.wait_ge(s_out, 16 * (KD + 2))

        @block.vector
        def _(dve):
            chain = [0]

            def step(ins):
                ins.then_inc(s_chain, 1)
                chain[0] += 1
                dve.wait_ge(s_chain, chain[0])

            def product(*key):
                b, turn = bank_of(key)
                dve.wait_ge(full[b], turn + 1)
                return bank[b]

            def take(ins, *key):
                ins.then_inc(taken[bank_of(key)[0]], 1)

            def wait_taken(*key):
                dve.wait_ge(taken[bank_of(key)[0]], takes(key))

            def tt(o, x, y, op):
                return dve.tensor_tensor(o, x, y, op)

            def stt(o, x, s, y, op0, op1):
                return dve.scalar_tensor_tensor(out=o, in0=x, scalar=s, in1=y, op0=op0, op1=op1)

            def ada(q):
                if q == 0:
                    dve.wait_ge(s_consts, 16 * 11)
                for c in range(4):
                    tiles = slice(c * ADA_TILES, (c + 1) * ADA_TILES)
                    ps = product("ada_t", q, c)[:, 0:2 * ADA_TILES].rearrange("p (n s) -> p n s", s=2)
                    bias = b_ada[:, q, tiles].rearrange("p (n a) -> p n a", a=1).to_broadcast([P, ADA_TILES, 2])
                    take(tt(mod[:, q, tiles, :], ps, bias, ALU.add), "ada_t", q, c)
                wait_taken("ada_t", q, 3)
                g = gains[:, q, :].rearrange("p (n a) -> p n a", a=1).to_broadcast([P, KD, 2])
                stt(gain1[:, q, :, :], mod[:, q, KD:2 * KD, :], 1.0, g, ALU.add, ALU.mult).then_inc(s_mod, 1)
                dve.wait_ge(s_mod, q + 1)

            rms_n = [0]

            def inverse(dst):
                rms_n[0] += 1
                dve.wait_ge(s_rms, rms_n[0])
                dve.reciprocal(dst, rms[:, :]).then_inc(s_rstd, 1)
                dve.wait_ge(s_rstd, rms_n[0])

            def norm(q):
                inverse(rstd[:, :])
                if q == 0:
                    dve.wait_ge(s_x, 16)
                for k in range(KD):
                    tt(hT[:, k, :], xT[:, k, :], rstd[:, :], ALU.mult).then_inc(s_norm, 1)
                for k in range(KD):
                    dve.wait_ge(s_norm, q * KD + k + 1)
                    dve.tensor_scalar(hT[:, k, TP:T], hT[:, k, TP:T], gain1[:, q, k, 1:2], mod[:, q, k, 1:2],
                                      ALU.mult, ALU.add).then_inc(s_hs, 1)

            def residual(l, half, d, src):
                q = 2 * l + half
                stt(xT[:, d, 0:TP], src[:, 0:TP], mod[:, q, 2 * KD + d, 0:1], xT[:, d, 0:TP], ALU.mult, ALU.add)
                stt(xT[:, d, TP:T], src[:, TP:T], mod[:, q, 2 * KD + d, 1:2], xT[:, d, TP:T], ALU.mult, ALU.add)\
                    .then_inc(s_res, 1)

            ada(0)
            norm(0)

            for j in range(NQ + NKV):
                dst = q_a[:, j, :] if j < NQ else ckvT[:, j - NQ, 0:T]
                take(dve.tensor_copy(dst, product("ev_in", j)[:, 0:T]), "ev_in", j)
            ps = product("ev_in", 5)
            tt(rope_t[NOPE:QK, :], ps[NOPE:QK, 0:T], rope[NOPE:QK, :], ALU.mult)
            take(tt(k_rope[NOPE:QK, :], ps[QK:P, 0:T], rope[QK:P, :], ALU.mult), "ev_in", 5)
            wait_taken("ev_in", 5)
            tt(k_rope[NOPE:QK, :], k_rope[NOPE:QK, :], rope_t[NOPE:QK, :], ALU.add).then_inc(s_krope, 1)
            inverse(q_rstd)
            for j in range(NQ):
                stt(q_a[:, j, :], q_a[:, j, :], qkv_g[:, j:j + 1], q_rstd, ALU.mult, ALU.mult).then_inc(s_qn, 1)
            inverse(rstd[:, :])
            for j in range(NKV):
                stt(ckvT[:, j, 0:T], ckvT[:, j, 0:T], qkv_g[:, NQ + j:NQ + j + 1], rstd[:, :], ALU.mult,
                    ALU.mult).then_inc(s_kn, 1)
            dve.wait_ge(s_ones, 3)
            U = T + 4
            for j in range(4):
                wait_taken("ev_in", 6 + 2 * j)
                ps = product("ev_in", 7 + 2 * j)
                tt(u_pad[:, j, 1:1 + TP], ps[:, 0:TP], c_gate[:, j, 0:TP], ALU.mult)
                take(tt(u_pad[:, j, TP + 3:U - 1], ps[:, TP:T], c_gate[:, j, TP:T], ALU.mult), "ev_in", 7 + 2 * j)
            for j in range(4):
                wait_taken("ev_in", 7 + 2 * j)
                if j > 0:
                    wait_taken("ev_in", 13 + j)
                u = u_pad[:, j, :]
                t = conv_t[:, 1:U - 1]
                step(dve.tensor_scalar(t, u[:, 0:U - 2], conv_w[:, j, 0:1], None, ALU.mult))
                step(stt(t, u[:, 1:U - 1], conv_w[:, j, 1:2], t, ALU.mult, ALU.add))
                step(stt(t, u[:, 2:U], conv_w[:, j, 2:3], t, ALU.mult, ALU.add))
                ps = product("ev_in", 14 + j)
                tt(mixT[:, j, 0:TP], conv_t[:, 1:1 + TP], ps[:, 0:TP], ALU.mult)
                take(tt(mixT[:, j, TP:T], conv_t[:, TP + 3:U - 1], ps[:, TP:T], ALU.mult), "ev_in", 14 + j)
            for h in range(HEADS):
                ps = product("q_up", h)
                tt(qT[NOPE:QK, h, :], ps[NOPE:QK, 0:T], rope[NOPE:QK, :], ALU.mult)
                dve.wait_ge(s_qnope, h + 1)
                if h > 0:
                    dve.wait_ge(s_qrope, h)
                take(tt(rope_t[NOPE:QK, :], ps[QK:P, 0:T], rope[QK:P, :], ALU.mult), "q_up", h)
                wait_taken("q_up", h)
                tt(qT[NOPE:QK, h, :], qT[NOPE:QK, h, :], rope_t[NOPE:QK, :], ALU.add).then_inc(s_qrope, 1)
            for j in range(HEADS // 2):
                ps = product("k_up", j)
                dve.wait_ge(s_even_key, j + 1)
                take(dve.tensor_copy(kT[0:NOPE, 2 * j + 1, :], ps[NOPE:P, :]), "k_up", j)

            def maxima(h):
                b = h % 2
                p0, p1 = product("score", h, 0), product("score", h, 1)
                dve.reduce_max(sm_max[:, b, 0:1], p0[:, 0:P], AX.X)
                dve.reduce_max(sm_max[:, b, 1:2], p0[:, P:512], AX.X)
                step(dve.reduce_max(sm_max[:, b, 2:3], p1[:, 0:384], AX.X))
                dve.tensor_scalar(sm_neg[:, b, 0:3], sm_max[:, b, 0:3], -SCALE, None, ALU.mult).then_inc(s_max, 1)

            def normalise(h):
                b = h % 2
                dve.wait_ge(s_exp, 3 * h + 3)
                take(dve.reciprocal(sm_inv[:, b, 0:3], sm_sum[:, b, 0:3]), "score", h, 0)
                wait_taken("score", h, 0)
                for c, (lo, hi) in enumerate([(0, P), (P, 512), (512, 896)]):
                    ins = dve.tensor_scalar(probs[:, b, lo:hi], probs[:, b, lo:hi], sm_inv[:, b, c:c + 1], None, ALU.mult)
                take(ins, "score", h, 1)

            for s in range(HEADS + 2):
                if s < HEADS:
                    maxima(s)
                if 1 <= s <= HEADS:
                    normalise(s - 1)
                if s >= 2:
                    h = s - 2
                    if h >= 2:
                        product("attend", h - 2)
                    take(dve.tensor_copy(probs_t[:, h % 2, 512:896], product("probs_t", h, 1)[:, 0:384]), "probs_t", h, 1)

            def mix_out(l):
                for d in range(KD):
                    residual(l, 0, d, product("mix_out", l, d))

            def route(l):
                wait_taken("router", l)
                step(dve.tensor_scalar(s_score[:, :], s_score[:, :], 1.0, None, ALU.add))
                step(dve.reciprocal(s_score[:, :], s_score[:, :]))
                sc3 = s_score[:, :].rearrange("p (t e) -> p t e", e=NE)
                rb = router_b[:, :].rearrange("p (a e) -> p a e", a=1).to_broadcast([P, NT, NE])
                step(tt(s_sel[:, :].rearrange("p (t e) -> p t e", e=NE), sc3, rb, ALU.add))

                def ranks(score, groups, gt, ge, rank):
                    other = score.rearrange("p (g a j) -> p g a j", a=1, j=4).to_broadcast([P, groups, 4, 4])
                    own = score.rearrange("p (g i a) -> p g i a", i=4, a=1).to_broadcast([P, groups, 4, 4])
                    gt4 = gt[:].rearrange("p (g i) j -> p g i j", i=4)
                    ge4 = ge[:].rearrange("p (g i) j -> p g i j", i=4)
                    first = before[:, :].rearrange("p (a i j) -> p a i j", a=1, j=4).to_broadcast([P, groups, 4, 4])
                    tt(gt4, other, own, ALU.is_gt)
                    step(tt(ge4, other, own, ALU.is_equal))
                    step(tt(ge4, ge4, first, ALU.mult))
                    step(tt(gt4, gt4, ge4, ALU.add))
                    step(dve.tensor_reduce(rank, gt[:], AX.X, ALU.add))

                ranks(s_sel[:, :], NT * NG, s_gt, s_ge, s_top[:, :])
                step(dve.tensor_scalar(s_top[:, :], s_top[:, :], 2.0, None, ALU.is_lt))
                step(tt(s_sel[:, :], s_sel[:, :], s_top[:, :], ALU.mult))
                step(dve.tensor_reduce(s_g[:, :], s_sel[:, :].rearrange("p (g j) -> p g j", j=4), AX.X, ALU.add))
                ranks(s_g[:, :], NT, s_ggt, s_gge, s_g4[:, :])
                step(dve.tensor_scalar(s_g4[:, :], s_g4[:, :], 1.0, None, ALU.is_lt))
                top3 = s_top[:, :].rearrange("p (g j) -> p g j", j=4)
                best = s_g4[:, :].rearrange("p (g a) -> p g a", a=1).to_broadcast([P, NT * NG, 4])
                step(tt(top3, top3, best, ALU.mult))
                dve.tensor_scalar(s_top[:, :], s_top[:, :], 1.0, None, ALU.mult).then_inc(s_mask, 1)
                dve.wait_ge(s_mask, l + 1)
                step(tt(s_score[:, :], s_score[:, :], s_top[:, :], ALU.mult))
                step(dve.tensor_reduce(s_den[:, :], sc3, AX.X, ALU.add))
                step(dve.reciprocal(s_den[:, :], s_den[:, :]))
                den = s_den[:, :].rearrange("p (t a) -> p t a", a=1).to_broadcast([P, NT, NE])
                tt(combine[:, :, :], sc3, den, ALU.mult).then_inc(s_comb, 1)
                dve.wait_ge(s_comb, l + 1)

            def place(l):
                for t in range(NT):
                    key = ("h_row", l, t, 1)
                    take(dve.tensor_copy(h_rows[:, t, 512:D], product(*key)[:, :]), *key)
                ps = product("slots", l)
                step(dve.reduce_max(most[:, 0:1], ps[:, NT * NE:NT * NE + NE], AX.X))
                dve.tensor_copy(most_i[:, l:l + 1], most[:, 0:1])
                take(tt(s_slot[:, :], ps[:, 0:NT * NE], expert_base[:, :], ALU.add), "slots", l)
                wait_taken("slots", l)
                three = lambda x: x[:, :].rearrange("p (t e) -> p t e", e=NE)
                spread = lambda x: x.rearrange("p (t a) -> p t a", a=1).to_broadcast([P, NT, NE])
                step(stt(s_tmp[:, :], s_top[:, :], -4096.0, s_slot[:, :], ALU.mult, ALU.add))
                step(dve.tensor_reduce(s_first[:, 0, :], three(s_tmp), AX.X, ALU.min))
                step(dve.tensor_scalar(s_first[:, 0, :], s_first[:, 0, :], 4096.0, None, ALU.add))
                step(tt(s_tmp[:, :], s_top[:, :], s_slot[:, :], ALU.mult))
                step(dve.tensor_reduce(s_first[:, 1, :], three(s_tmp), AX.X, ALU.max))
                for c in range(2):
                    step(tt(three(s_eq), three(s_slot), spread(s_first[:, c, :]), ALU.is_equal))
                    step(tt(three(s_eq), three(s_eq), combine[:, :, :], ALU.mult))
                    step(dve.tensor_reduce(weight[:, l, c, :], three(s_eq), AX.X, ALU.add))
                dve.tensor_copy(index[:, l, :, :], s_first[:, :, :]).then_inc(s_index, 1)
                dve.wait_ge(s_index, l + 1)

            def experts_all(l):
                dve.memset(moe_out, 0.0).then_inc(s_dt[l], 1)
                dve.wait_ge(s_dt[l], 1)
                with dve.Fori(0, NE // SLOTS) as i:
                    for j in range(SLOTS):
                        e = i * SLOTS + j
                        dve.tensor_copy(weight_e[:, j, :],
                                        combine[:, :, bass.ds(e, 1)].rearrange("p t a -> p (t a)")).then_inc(s_we[l], 1)
                        dve.wait_ge(s_we[l], i * SLOTS + (j + 1))
                        for t in range(NT):
                            n = j * NT + t
                            b = n % 2
                            dve.wait_ge(s_dsilu[l], i * (SLOTS * NT) + (n + 1))
                            stt(hidden[:, b, :], silu[:, b, :], weight_e[:, j, t:t + 1], bank[b][:, F:2 * F],
                                ALU.mult, ALU.mult).then_inc(s_dhid[l], 1)
                            if t < NT - 1:
                                dve.wait_ge(s_dn[l], i * (SLOTS * (NT - 1)) + (j * (NT - 1) + t + 1))
                            else:
                                dve.wait_ge(s_expert[l], i * SLOTS + (j + 1))
                            for c in range(2):
                                ins = tt(moe_out[:, t, c * 512:c * 512 + 512], moe_out[:, t, c * 512:c * 512 + 512],
                                         bank[4 + 2 * b + c][:, :], ALU.add)
                            ins.then_inc(s_dt[l], 1)
                            dve.wait_ge(s_dt[l], i * (SLOTS * NT) + (n + 2))

            def copy_h(l, i, e):
                dve.wait_ge(s_turn1[l], i * SLOTS + (e + 1))
                dve.tensor_copy(h_slotT[:, e % 2, 512:D], bank[3][:, :]).then_inc(s_copy1[l], 1)

            def gate(l, i, e):
                dve.wait_ge(s_silu[l], i * SLOTS + (e + 1))
                tt(hidden[:, e % 2, :], silu[:, e % 2, :], bank[e % 2][:, F:2 * F], ALU.mult).then_inc(s_hid[l], 1)

            def experts_routed(l):
                for e in range(2):
                    copy_h(l, 0, e)
                gate(l, 0, 0)

                def round_(i, static):
                    for j in range(SLOTS):
                        last = static and i > 0
                        if not (last and j >= SLOTS - 2):
                            copy_h(l, i, j + 2)
                        if not (last and j == SLOTS - 1):
                            gate(l, i, j + 1)
                        dve.wait_ge(s_expert[l], i * SLOTS + (j + 1))
                        wait(dve, s_yst[l][j % 2], i * 32 + 16 * (j // 2))
                        dve.tensor_copy(y_slot[:, j % 2, 512:D], bank[5][:, :]).then_inc(s_y1[l], 1)

                rounds(dve, round_)
                for t in range(NT):
                    dve.wait_ge(s_scaled[l], t + 1)
                    stt(moe_out[:, t, :], second[:, t, :], weight[:, l, 1, t:t + 1], moe_out[:, t, :],
                        ALU.mult, ALU.add).then_inc(s_sum[l], 1)

            def dispatch(l):
                route(l)
                place(l)

            def moe(l):
                count = dve.value_load(most_i[0:1, l:l + 1], min_val=0, max_val=T)
                with dve.If(count < P + 1):
                    experts_routed(l)
                with dve.Else():
                    experts_all(l)

            def moe_add(l):
                for d in range(KD):
                    residual(l, 1, d, product("moe_t", l, d))

            mix_out(0)
            ada(1)
            norm(1)
            dispatch(0)
            ada(2)
            moe(0)
            ada(3)
            moe_add(0)
            norm(2)

            dve.wait_ge(s_odd, 48)
            dve.wait_ge(s_vrms, 1)
            step(dve.reciprocal(ss[:, 3:3 + NT], ss[:, 3:3 + NT]))
            for t in range(NT):
                stt(v_rows[:, t, :], v_rows[:, t, :], ss[:, 3 + t:4 + t], v_gain, ALU.mult, ALU.mult).then_inc(s_vn, 1)
            for g in range(KD):
                ps = product("spatial", g)[:, 0:T].rearrange("p (n q) -> p n q", q=P)
                bias = b_s[:, g, :].rearrange("p (a q) -> p a q", a=1).to_broadcast([P, NT, P])
                take(tt(sg_t[:, g % 2, :].rearrange("p (n q) -> p n q", q=P), ps, bias, ALU.add), "spatial", g)
                wait_taken("spatial", g)
                wait_taken("gm_u", g)
                tt(mixT[:, g, :], sg_t[:, g % 2, :], uT[:, g, :], ALU.mult).then_inc(s_sg, 1)
                dve.wait_ge(s_sg, g + 1)
            mix_out(1)
            norm(3)
            dispatch(1)
            moe(1)
            moe_add(1)
            inverse(rstd[:, :])
            for k in range(KD):
                stt(hT[:, k, :], xT[:, k, :], gains[:, 4, k:k + 1], rstd[:, :], ALU.mult, ALU.mult).then_inc(s_y, 1)

        @block.tensor
        def _(pe):
            def opened(*key):
                n = PRODUCT_AT[key]
                if n >= BANKS:
                    emptied(PRODUCTS[n - BANKS])
                return bank[n % BANKS]

            def emptied(key):
                if key[0] in RESIDUALS:
                    pe.wait_ge(s_res, residuals(key))
                elif key[0] in ROOTS:
                    pe.wait_ge(s_rms, roots(key))
                else:
                    pe.wait_ge(taken[bank_of(key)[0]], takes(key))

            def closed(ins, *key):
                ins.then_inc(full[bank_of(key)[0]], 1)

            def weights(chunk, columns):
                n = CHUNK_AT[chunk]
                pe.wait_ge(ring_full[n % SLOTS], 16 * (n // SLOTS + 1))
                return ring[:, n % SLOTS, 0:KD * columns].rearrange("p (k n) -> p k n", n=columns)

            def ada(q):
                if q == 0:
                    pe.wait_ge(s_csil, 1)

                def rows(c):
                    w = weights(("ada", (q, c)), ADA_COLS)
                    for i in range(2):
                        ps = opened("ada_row", q, c, i)
                        for k in range(KD):
                            mm = pe.matmul(ps[0:2, 0:384], csil[:, k, :], w[:, k, i * 384:i * 384 + 384],
                                           start=(k == 0), stop=(k == KD - 1))
                        closed(mm, "ada_row", q, c, i)

                def turned(c):
                    emptied(("ada_row", q, c, 0))
                    emptied(("ada_row", q, c, 1))
                    ps = opened("ada_t", q, c)
                    for j in range(ADA_TILES):
                        mm = pe.transpose(ps[:, 2 * j:2 * j + 2], ada_row[0:2, c % 2, j * P:j * P + P], ident[0:2, 0:2])
                    closed(mm, "ada_t", q, c)

                if q == 0:
                    pe.wait_ge(s_consts, 16 * 11)
                rows(0)
                rows(1)
                turned(0)
                rows(2)
                turned(1)
                rows(3)
                turned(2)
                turned(3)

            sq_n = [0]

            def sum_squares(key, tiles):
                ps = opened(*key)
                for k in range(tiles):
                    sq_n[0] += 1
                    pe.wait_ge(s_sq, sq_n[0])
                    mm = pe.matmul(ps[:, 0:T], ones[:, :], sq[:, sq_at[0] % 4, :], start=(k == 0), stop=(k == tiles - 1))
                    sq_at[0] += 1
                    if k < tiles - 1:
                        mm.then_inc(s_squ, 1)
                closed(mm, *key)

            sq_at = [0]

            def norm(q):
                sq_at[0] = 0
                sum_squares(("norm", q), KD)

            def normed(q):
                pe.wait_ge(s_hs, (q + 1) * KD)
                pe.wait_ge(s_hp, (q + 1) * KD)

            def transposed(key, w, j, x):
                ps = opened(*key)
                for k in range(KD):
                    mm = pe.matmul(ps[:, 0:T], w[:, k, j * P:j * P + P], x[:, k, :], start=(k == 0), stop=(k == KD - 1))
                closed(mm, *key)

            pe.wait_ge(s_ones, 3)
            ada(0)
            norm(0)
            normed(0)

            def ev_in(n):
                transposed(("ev_in", n), weights(("ev_in", n // 6), 768), n % 6, hT)

            for n in range(6):
                ev_in(n)
            sq_at[0] = 0
            sum_squares(("q_norm",), NQ)
            sum_squares(("kv_norm",), NKV)
            for n in range(6, EV_TILES):
                ev_in(n)
            n = CHUNK_AT[("qkv", 0)]
            pe.wait_ge(ring_full[n % SLOTS], 16 * (n // SLOTS + 1))
            w_q = ring[:, n % SLOTS, 0:NQ * HEADS * P].rearrange("p (k n) -> p k n", k=NQ)
            w_kv = ring[:, n % SLOTS, NQ * HEADS * P:NQ * HEADS * P + NKV * 1024].rearrange("p (k n) -> p k n", k=NKV)
            pe.wait_ge(s_qn, NQ)
            for h in range(HEADS):
                ps = opened("q_up", h)
                for k in range(NQ):
                    mm = pe.matmul(ps[:, 0:T], w_q[:, k, h * P:h * P + P], q_a[:, k, :], start=(k == 0), stop=(k == NQ - 1))
                closed(mm, "q_up", h)
            pe.wait_ge(s_kn, NKV)
            pe.wait_ge(s_cache, 32)
            for j in range(HEADS // 2):
                ps = opened("k_up", j)
                for k in range(NKV):
                    mm = pe.matmul(ps[:, :], w_kv[:, k, j * P:j * P + P], ckvT[:, k, :], start=(k == 0), stop=(k == NKV - 1))
                closed(mm, "k_up", j)
            for t in range(NKEY // P):
                ps = opened("v_up", t)
                for k in range(NKV):
                    mm = pe.matmul(ps[:, :], ckvT[:, k, t * P:t * P + P], w_kv[:, k, 512:1024], start=(k == 0), stop=(k == NKV - 1))
                closed(mm, "v_up", t)

            def score(h):
                pe.wait_ge(s_qrope, h + 1)
                if h == 0:
                    pe.wait_ge(s_kropes, 1)
                if h % 2 == 0:
                    pe.wait_ge(s_even_key, h // 2 + 1)
                else:
                    emptied(("k_up", h // 2))
                ps = opened("score", h, 0)
                pe.matmul(ps[:, 0:P], qT[0:QK, h, 0:TP], kT[0:QK, h, 0:TP], start=True, stop=True)
                mm = pe.matmul(ps[:, P:512], qT[0:QK, h, TP:TP + P], kT[0:QK, h, TP:NKEY], start=True, stop=True)
                closed(mm, "score", h, 0)
                ps = opened("score", h, 1)
                mm = pe.matmul(ps[:, 0:384], qT[0:QK, h, TP + P:T], kT[0:QK, h, TP:NKEY], start=True, stop=True)
                closed(mm, "score", h, 1)

            def turn(h):
                emptied(("score", h, 1))
                pr = probs[:, h % 2, :]
                tiles = [0] + [x for kt in range(3) for x in (1 + kt, 4 + kt)]
                for c, part in enumerate((tiles[:4], tiles[4:])):
                    ps = opened("probs_t", h, c)
                    for n, x in enumerate(part):
                        mm = pe.transpose(ps[:, n * P:n * P + P], pr[:, x * P:x * P + P], ident[:, :])
                    closed(mm, "probs_t", h, c)

            def attend(h):
                emptied(("probs_t", h, 0))
                emptied(("probs_t", h, 1))
                if h == 0:
                    for t in range(NKEY // P):
                        emptied(("v_up", t))
                pt = probs_t[:, h % 2, :]
                ps = opened("attend", h)
                pe.matmul(ps[0:VD, 0:TP], values[:, 0, h * VD:h * VD + VD], pt[:, 0:P], start=True, stop=True)
                for kt in range(3):
                    mm = pe.matmul(ps[0:VD, TP:T], values[:, 1 + kt, h * VD:h * VD + VD],
                                   pt[:, P + kt * TS:P + (kt + 1) * TS], start=(kt == 0), stop=(kt == 2))
                closed(mm, "attend", h)

            for s in range(HEADS + 2):
                if s < HEADS:
                    score(s)
                if 1 <= s <= HEADS:
                    turn(s - 1)
                if s >= 2:
                    attend(s - 2)

            def mix_out(l):
                for d in range(KD):
                    transposed(("mix_out", l, d), weights(("ev_out" if l == 0 else "gm_out", d // 4), 512), d % 4, mixT)

            emptied(("ev_in", EV_TILES - 1))
            for h in range(HEADS):
                emptied(("attend", h))
            mix_out(0)

            def dispatch(l):
                normed(2 * l + 1)
                ps = opened("router", l)
                for t in range(NT):
                    for k in range(KD):
                        mm = pe.matmul(ps[:, t * NE:t * NE + NE], hT[:, k, t * P:t * P + P], router_w[:, k, :],
                                       start=(k == 0), stop=(k == KD - 1))
                closed(mm, "router", l)
                for t in range(NT):
                    for c in range(2):
                        ps = opened("h_row", l, t, c)
                        for k in range(4):
                            mm = pe.transpose(ps[:, k * P:k * P + P], hT[:, 4 * c + k, t * P:t * P + P], ident[:, :])
                        closed(mm, "h_row", l, t, c)
                pe.wait_ge(s_mask, l + 1)
                ps = opened("slots", l)
                for t in range(NT):
                    for u in range(t + 1):
                        pe.matmul(ps[:, t * NE:t * NE + NE], earlier[:, :] if u == t else ones[:, :],
                                  s_top[:, u * NE:u * NE + NE], start=(u == 0), stop=(u == t))
                for t in range(NT):
                    mm = pe.matmul(ps[:, NT * NE:NT * NE + NE], ones[:, :], s_top[:, t * NE:t * NE + NE],
                                   start=(t == 0), stop=(t == NT - 1))
                closed(mm, "slots", l)

            def experts_all(l):
                chunk = CHUNK_AT[("moe", (l, 0))]
                with pe.Fori(0, NE // SLOTS) as i:
                    def up(n, tiles):
                        j, t = n // NT, n % NT
                        s, turn = (chunk + j) % SLOTS, (chunk + j) // SLOTS
                        if t == 0 and 0 in tiles:
                            pe.wait_ge(ring_full[s], i * 16 + 16 * (turn + 1))
                        for k in tiles:
                            mm = pe.matmul(bank[n % 2][:, :], hT[:, k, t * P:t * P + P], ring[:, s, k * 512:k * 512 + 512],
                                           start=(k == 0), stop=(k == KD - 1))
                        if KD - 1 in tiles:
                            mm.then_inc(s_dup[l], 1)

                    def turned(n):
                        b = n % 2
                        pe.wait_ge(s_dhid[l], i * (SLOTS * NT) + (n + 1))
                        for c in range(2):
                            tr = pe.transpose(bank[2 + b][:, c * P:c * P + P], hidden[:, b, c * P:c * P + P], ident[:, :])
                        tr.then_inc(s_dtr[l], 1)

                    def down(n):
                        b, s = n % 2, (chunk + n // NT) % SLOTS
                        pe.wait_ge(s_dht[l], i * (SLOTS * NT) + (n + 1))
                        if n >= 1:
                            pe.wait_ge(s_dt[l], i * (SLOTS * NT) + n)
                        mm = down_matmuls(bank[4 + 2 * b:6 + 2 * b], b, s)
                        mm.then_inc(s_expert[l] if n % NT == NT - 1 else s_dn[l], 1)

                    up(0, range(KD))
                    for n in range(SLOTS * NT):
                        if n + 1 < SLOTS * NT:
                            up(n + 1, range(KD // 2))
                        turned(n)
                        if n + 1 < SLOTS * NT:
                            up(n + 1, range(KD // 2, KD))
                        down(n)
                    pe.wait_ge(s_dt[l], i * (SLOTS * NT) + SLOTS * NT)
                pe.wait_ge(s_dt[l], NE * NT + 1)

            def down_matmuls(ps, b, s):
                for half in range(2):
                    for c in range(2):
                        at_ = KD * 2 * F + c * D + half * 512
                        mm = pe.matmul(ps[half][:, :], hiddenT[:, b, c * P:c * P + P], ring[:, s, at_:at_ + 512],
                                       start=(c == 0), stop=(c == 1))
                return mm

            def experts_routed(l):
                chunk = CHUNK_AT[("moe", (l, 0))]

                def turn_h(i, e):
                    b = e % 2
                    pe.wait_ge(s_h[l][b], i * 32 + 16 * (e // 2 + 1))
                    wait(pe, s_copy0[l], i * SLOTS + e)
                    for k in range(4):
                        tr = pe.transpose(bank[2][:, k * P:k * P + P], h_slot[:, b, k * P:k * P + P], ident[:, :])
                    tr.then_inc(s_turn0[l], 1)
                    wait(pe, s_copy1[l], i * SLOTS + e)
                    for k in range(4, 8):
                        tr = pe.transpose(bank[3][:, (k - 4) * P:(k - 3) * P], h_slot[:, b, k * P:k * P + P], ident[:, :])
                    tr.then_inc(s_turn1[l], 1)

                def up(i, e, tiles):
                    s, turn = (chunk + e) % SLOTS, (chunk + e) // SLOTS
                    if 0 in tiles:
                        pe.wait_ge(ring_full[s], i * 16 + 16 * (turn + 1))
                        pe.wait_ge(s_copy0[l], i * SLOTS + (e + 1))
                        wait(pe, s_hid[l], i * SLOTS + (e - 1))
                    if 4 in tiles:
                        pe.wait_ge(s_copy1[l], i * SLOTS + (e + 1))
                    for k in tiles:
                        mm = pe.matmul(bank[e % 2][:, :], h_slotT[:, e % 2, k * P:k * P + P],
                                       ring[:, s, k * 512:k * 512 + 512], start=(k == 0), stop=(k == KD - 1))
                    if KD - 1 in tiles:
                        mm.then_inc(s_up[l], 1)

                turn_h(0, 0)
                turn_h(0, 1)
                up(0, 0, range(KD))

                def round_(i, static):
                    for j in range(SLOTS):
                        b = j % 2
                        last = static and i > 0
                        more = not (last and j == SLOTS - 1)
                        if more:
                            up(i, j + 1, range(KD // 2))
                        pe.wait_ge(s_hid[l], i * SLOTS + (j + 1))
                        for c in range(2):
                            tr = pe.transpose(bank[6 + b][:, c * P:c * P + P], hidden[:, b, c * P:c * P + P], ident[:, :])
                        tr.then_inc(s_tr[l], 1)
                        if more:
                            up(i, j + 1, range(KD // 2, KD))
                        if not (last and j >= SLOTS - 2):
                            turn_h(i, j + 2)
                        pe.wait_ge(s_ht[l], i * SLOTS + (j + 1))
                        wait(pe, s_y0[l], i * SLOTS + j)
                        wait(pe, s_y1[l], i * SLOTS + j)
                        down_matmuls(bank[4:6], b, (chunk + j) % SLOTS).then_inc(s_expert[l], 1)

                rounds(pe, round_)

            def moe(l):
                n = PRODUCT_AT[("ada_t", 2, 3)] if l == 0 else PRODUCT_AT[("slots", 1)]
                for key in PRODUCTS[n - BANKS + 1:n + 1]:
                    emptied(key)
                pe.wait_ge(s_index, l + 1)
                count = pe.value_load(most_i[0:1, l:l + 1], min_val=0, max_val=T)
                with pe.If(count < P + 1):
                    experts_routed(l)
                    pe.wait_ge(s_y0[l], NE)
                    pe.wait_ge(s_y1[l], NE)
                    if l == 0:
                        ada(3)
                    pe.wait_ge(s_sum[l], NT)
                with pe.Else():
                    experts_all(l)
                    if l == 0:
                        ada(3)

            def moe_add(l):
                for d in range(KD):
                    ps = opened("moe_t", l, d)
                    for t in range(NT):
                        mm = pe.transpose(ps[:, t * P:t * P + P], moe_out[:, t, d * P:d * P + P], ident[:, :])
                    closed(mm, "moe_t", l, d)

            ada(1)
            norm(1)
            dispatch(0)
            ada(2)
            moe(0)
            moe_add(0)
            norm(2)

            normed(2)
            for c in range(2):
                w = weights(("gm_in", c), 512)
                for t in range(NT):
                    ps = opened("gm_v", t, c)
                    for k in range(KD):
                        mm = pe.matmul(ps[:, :], hT[:, k, t * P:t * P + P], w[:, k, :], start=(k == 0), stop=(k == KD - 1))
                    closed(mm, "gm_v", t, c)
            for j in range(KD):
                transposed(("gm_u", j), weights(("gm_in", 2 + j // 4), 512), j % 4, hT)
            pe.wait_ge(s_vn, NT)
            pe.wait_ge(s_odd, 48)
            for g in range(KD):
                ps = opened("spatial", g)
                for t in range(NT):
                    mm = pe.matmul(ps[:, t * P:t * P + P], v_rows[:, t, g * P:g * P + P], w_sT[:, g, :], start=True, stop=True)
                closed(mm, "spatial", g)
            pe.wait_ge(s_sg, KD)
            mix_out(1)
            norm(3)
            dispatch(1)
            moe(1)
            moe_add(1)
            norm(4)


_LOADED = ("cvec", "xT", "b_ada", "gains", "conv_w", "qkv_g", "rope", "ident", "router_w", "router_b", "before", "expert_base", "earlier",
           "cache_ckv", "cache_krope", "v_gain", "b_s", "w_sT", "ada_w", "ev_in", "qkv", "ev_out", "gm_in", "gm_out", "moe")


def tiles_first(w):
    return w.reshape(w.shape[0] // P, P, -1).transpose(1, 0, 2)


def rope_swap(w):
    return w.reshape(*w.shape[:-1], 2, 2, ROPE // 4)[..., ::-1, :].reshape(w.shape)


def laid_out(x_prompt, x_sample, cache_ckv, cache_krope, c, c_ctx, w_ada, b_ada, g_mix, g_ffn, g_final,
             ev_w_in, conv_w, q_norm_g, w_q_up, kv_norm_g, w_kv_up, ev_w_out,
             gm_w_in, gm_v_g, gm_w_s, gm_b_s, gm_w_out, router_w, router_b, moe_w1, moe_w3, moe_w2):
    o = {}
    o["xT"] = tiles_first(np.concatenate([x_prompt[0], x_sample[0]]).T)
    o["cvec"] = tiles_first(np.stack([c_ctx, c[0]], 1))
    cols = lambda v: v.reshape(-1, P).T
    o["b_ada"] = np.stack([cols(b_ada[l, h * 3 * D:(h + 1) * 3 * D]) for l in range(LAYERS) for h in range(2)], 1)
    o["gains"] = np.stack([cols(g) for g in (g_mix[0], g_ffn[0], g_mix[1], g_ffn[1], g_final)], 1)
    o["conv_w"] = conv_w[0].T.reshape(4, P, 3).transpose(1, 0, 2)
    o["qkv_g"] = np.concatenate([cols(q_norm_g[0]), cols(kv_norm_g[0])], 1)
    o["ident"] = np.eye(P, dtype=np.float32)
    o["before"] = np.broadcast_to(np.tril(np.ones((EPG, EPG), np.float32), -1).reshape(1, -1), (P, EPG * EPG))
    o["expert_base"] = np.broadcast_to(np.tile(np.arange(NE, dtype=np.float32) * P, NT)[None], (P, NT * NE))
    o["earlier"] = np.triu(np.ones((P, P), np.float32), 1)
    pos = np.arange(TS)
    freq = 10000.0 ** (-np.arange(ROPE // 4, dtype=np.float32) / np.float32(ROPE // 4))
    ang = np.stack([(pos // 64)[:, None] * freq, (pos % 64)[:, None] * freq], 1).astype(np.float32)
    cos = np.repeat(np.cos(ang)[:, :, None, :], 2, 2).reshape(TS, ROPE).T
    sin = (np.sin(ang)[:, :, None, :] * np.array([-1.0, 1.0])[None, None, :, None]).reshape(TS, ROPE).T
    rope = np.zeros((P, T), np.float32)
    rope[NOPE:QK, :TP] = 1.0
    rope[NOPE:QK, TP:] = cos
    rope[QK:P, TP:] = sin
    o["rope"] = rope
    o["router_w"] = tiles_first(router_w)
    o["router_b"] = np.broadcast_to(router_b[None], (P, NE))
    o["cache_ckv"] = tiles_first(cache_ckv[0, 0].T)
    o["cache_krope"] = np.broadcast_to(cache_krope[0, 0].T[:, None, :], (ROPE, HEADS, PAST))
    o["v_gain"] = gm_v_g[0][None]
    o["b_s"] = gm_b_s[0][None]
    o["w_sT"] = gm_w_s[0].transpose(2, 0, 1)
    chunked = lambda w, n: np.stack([tiles_first(w[:, i:i + n]).reshape(P, -1) for i in range(0, w.shape[1], n)])
    o["ada_w"] = np.stack([chunked(w_ada[l][:, h * 3 * D:(h + 1) * 3 * D], ADA_COLS)
                           for l in range(LAYERS) for h in range(2)])
    b, cg, v, qa, kva, kr = np.split(ev_w_in[0], [512, 1024, 1536, 1920, 2176], axis=1)
    cv = np.stack([cg.reshape(D, 4, P), v.reshape(D, 4, P)], 2).reshape(D, 1024)
    o["ev_in"] = chunked(np.concatenate([qa, kva, np.zeros((D, NOPE), np.float32), kr, rope_swap(kr), cv, b], 1), 768)
    q = w_q_up[0].reshape(QR, HEADS, QK)
    q = np.concatenate([q, rope_swap(q[..., NOPE:])], -1).reshape(QR, HEADS * P)
    kv = w_kv_up[0].reshape(KVR, HEADS, 2, NOPE).transpose(0, 2, 1, 3).reshape(KVR, 1024)
    o["qkv"] = np.concatenate([tiles_first(q).reshape(P, -1), tiles_first(kv).reshape(P, -1)], 1)[None]
    o["ev_out"] = chunked(ev_w_out[0], 512)
    o["gm_in"] = chunked(np.concatenate([gm_w_in[0][:, D:], gm_w_in[0][:, :D]], 1), 512)
    o["gm_out"] = chunked(gm_w_out[0], 512)
    w13 = np.concatenate([moe_w1, moe_w3], -1).reshape(LAYERS, NE, KD, P, 2 * F).transpose(0, 1, 3, 2, 4)
    w2 = moe_w2.reshape(LAYERS, NE, F // P, P, D).transpose(0, 1, 3, 2, 4)
    o["moe"] = np.concatenate([w13.reshape(LAYERS, NE, P, -1), w2.reshape(LAYERS, NE, P, -1)], -1)
    return o


def kernel(**inputs):
    import concourse.bacc as bacc
    from concourse.bass_utils import run_bass_kernel_spmd

    nc = bacc.Bacc("TRN2", target_bir_lowering=False, num_devices=1)
    host = laid_out(**{k: np.asarray(v) for k, v in inputs.items()})
    arrays, a = {}, {}
    for name in _LOADED:
        x = np.ascontiguousarray(host[name], dtype=np.float32)
        arrays[f"in_{name}"] = x
        a[name] = nc.dram_tensor(f"in_{name}", x.shape, F32, kind="ExternalInput").ap()
    shapes = {"y": (P, KD, T), "state_ckv": (P, NKV, TP), "state_krope": (ROPE, TP)}
    out = {n: nc.dram_tensor(f"out_{n}", s, F32, kind="ExternalOutput").ap() for n, s in shapes.items()}
    build(nc, a, out)
    r = run_bass_kernel_spmd(nc, [arrays], core_ids=[0]).results[0]
    y = np.asarray(r["out_y"]).transpose(2, 1, 0).reshape(T, D)
    ckv = np.asarray(r["out_state_ckv"]).transpose(2, 1, 0).reshape(1, 1, TP, KVR)
    krope = np.asarray(r["out_state_krope"]).T.reshape(1, 1, TP, ROPE)
    return y[None, :TP], y[None, TP:], ckv, krope
```

```python
from contextlib import ExitStack

import numpy as np
import concourse.bass as bass
from concourse import mybir

F32 = mybir.dt.float32
ALU = mybir.AluOpType
ACT = mybir.ActivationFunctionType
AX = mybir.AxisListType

P = 128
D = 1024
KD = D // P
TP, TS = 128, 256
T = TP + TS
NT = T // P
PAST = 128
NKEY = T + PAST
LAYERS = 2
HEADS, NOPE, ROPE, VD = 8, 64, 32, 64
QK = NOPE + ROPE
QR, KVR = 384, 256
NQ, NKV = QR // P, KVR // P
NE, NG, EPG = 16, 4, 4
F = 256
EPS = 1e-6
SCALE = QK ** -0.5

SLOTS = 4
SLOT = 6144
ADA_COLS = 768
ADA_TILES = ADA_COLS // P
HALF_TILES = 3 * KD
EV_TILES = 18

CHUNKS = ([("ada", n) for n in range(3)] + [("ev_in", c) for c in range(3)] + [("qkv", 0)]
          + [("ada", n) for n in range(3, 8)] + [("ev_out", c) for c in range(2)]
          + [("ada", n) for n in range(8, 11)] + [("moe", (0, e)) for e in range(NE)]
          + [("ada", n) for n in range(11, 14)] + [("gm_in", c) for c in range(4)]
          + [("gm_out", c) for c in range(2)] + [("ada", n) for n in (14, 15)] + [("moe", (1, e)) for e in range(NE)])
CHUNK_AT = {key: n for n, key in enumerate(CHUNKS)}


def ada_products(turned, rows):
    rows = [("ada_row", n) for n in rows]
    turned = [("ada_t", n) for n in turned]
    return [key for n in range(max(len(rows), len(turned))) for key in rows[n:n + 1] + turned[n:n + 1]]


def attention_ada(s):
    return [s + 1] if 2 <= s <= 6 else [], [s] if 3 <= s <= 7 else []


def dispatch_products(l):
    return ([("router", l), ("logits", l)] + [("h_row", l, t, c) for t in range(NT) for c in range(2)]
            + (ada_products([8], [9]) if l == 0 else []) + [("slots", l)]
            + [("table", l, 0)] + (ada_products([9], [10]) if l == 0 else ada_products([], [15]))
            + [("table", l, g) for g in range(1, NE // SLOTS)] + [("ada_t", 10 if l == 0 else 15)])


PRODUCTS = (
    [("norm", 0), ("ada_row", 0), ("ada_row", 1), ("ada_t", 0), ("ada_t", 1), ("ada_row", 2), ("ada_t", 2)] + [("ev_in", n) for n in range(6)]
    + [("q_norm",), ("kv_norm",)] + [("ev_in", n) for n in range(6, EV_TILES)]
    + [("v_up", t) for t in range(NKEY // P)]
    + [("q_up", h) for h in range(HEADS)] + [("k_up", j) for j in range(HEADS // 2)]
    + [key for s in range(HEADS + 2)
       for key in ([("score", s, 0), ("score", s, 1)] if s < HEADS else [])
       + [("ada_row", n) for n in attention_ada(s)[0]] + [("ada_t", n) for n in attention_ada(s)[1]]
       + ([("probs_t", s - 1, 0), ("probs_t", s - 1, 1)] if 1 <= s <= HEADS else [])
       + ([("attend", s // 2 - 1)] if s >= 3 and s % 2 else [])]
    + [("mix_out", 0, d) for d in range(KD)] + [("norm", 1), ("ada_row", 8)]
    + dispatch_products(0) + [("ada_row", 11), ("ada_row", 12), ("ada_t", 11), ("ada_t", 12)]
    + [("moe_t", 0, d) for d in range(KD)] + [("norm", 2), ("ada_row", 13)]
    + [("gm_v", t, 0) for t in range(NT)] + [("ada_t", 13)] + [("gm_v", t, 1) for t in range(NT)]
    + [("gm_u", j) for j in range(KD)] + [("spatial", g) for g in range(KD)]
    + [("mix_out", 1, d) for d in range(KD)] + [("ada_row", 14), ("norm", 3), ("ada_t", 14)] + dispatch_products(1)
    + [("moe_t", 1, d) for d in range(KD)] + [("norm", 4)])
PRODUCT_AT = {key: n for n, key in enumerate(PRODUCTS)}
BANKS = 8
SENT = 3

SMALLS = (("b_ada", (LAYERS * 2, HALF_TILES)), ("gains", (5, KD)), ("conv_w", (4, 3)), ("qkv_g", (NQ + NKV,)), ("rope", (T,)),
          ("ident", (P,)), ("router_w", (KD, 32)), ("router_b", (NE,)), ("threshold", (EPG * EPG,)),
          ("expert_base", (NT * NE,)), ("earlier", (P,)), ("token", (NT,)), ("place", (P,)))

ADDED = (1, 3)
RESIDUALS = ("mix_out", "moe_t")
SCORES = ("score",)


def bank_of(key):
    return PRODUCT_AT[key] % BANKS, PRODUCT_AT[key] // BANKS


def takes(key):
    n = PRODUCT_AT[key]
    return sum(k[0] not in RESIDUALS + SCORES for k in PRODUCTS[n % BANKS:n + 1:BANKS])


def squares_before(q):
    return q * KD + (NQ + NKV if q > 0 else 0)


def residuals(key):
    return sum(k[0] in RESIDUALS for k in PRODUCTS[:PRODUCT_AT[key] + 1])


def last_user(chunk):
    kind, i = chunk
    if kind == "ada":
        return ("ada_row", i)
    if kind == "ev_in":
        return ("ev_in", 6 * i + 5)
    if kind == "qkv":
        return ("k_up", HEADS // 2 - 1)
    if kind == "gm_in":
        return ("gm_v", NT - 1, i) if i < 2 else ("gm_u", 4 * (i - 2) + 3)
    return ("mix_out", 0 if kind == "ev_out" else 1, 4 * i + 3)


def build(nc, a, out):
    ctx = ExitStack()
    with ctx:
        def sb(name, shape):
            return ctx.enter_context(nc.sbuf_tensor(name, shape, F32))

        def sem(name):
            return ctx.enter_context(nc.semaphore(name))

        bank = [ctx.enter_context(nc.psum_tensor(f"bank{b}", [P, 512], F32)) for b in range(BANKS)]

        ring = sb("ring", [P, SLOTS, SLOT])
        xT = sb("xT", [P, KD, T])
        hT = sb("hT", [P, KD, T])
        qT = hT
        sq = sb("sq", [P, 4, T])
        rstd = sb("rstd", [P, T])
        logit_t = sb("logit_t", [P, T])
        acc = sb("acc", [P, T])
        smalls = sb("smalls", [P, sum(int(np.prod(shape)) for _, shape in SMALLS)])
        small, n = {}, 0
        for name, shape in SMALLS:
            size = int(np.prod(shape))
            view = smalls[:, n:n + size]
            small[name] = view.rearrange("p (a b) -> p a b", b=shape[1]) if len(shape) == 2 else view
            n += size
        (b_ada, gains, conv_w, qkv_g, rope, ident, router_w, router_b, threshold, expert_base, earlier,
         token, place_no) = (
            small[name] for name, _ in SMALLS)
        cvec = sb("cvec", [P, KD, 2])
        csil = sb("csil", [P, KD, 32])
        ones_b = ctx.enter_context(nc.sbuf_tensor("ones_b", [P, P], mybir.dt.bfloat16))
        earlier_b = ctx.enter_context(nc.sbuf_tensor("earlier_b", [P, P], mybir.dt.bfloat16))
        top_b = ctx.enter_context(nc.sbuf_tensor("top_b", [P, NT * NE], mybir.dt.bfloat16))
        mod = sb("mod", [P, LAYERS * 2, HALF_TILES, 2])
        gain1 = sb("gain1", [P, LAYERS * 2, KD, 2])
        eps = sb("eps", [P, 1])
        share = sb("share", [P, 3, P])
        work = sb("work", [P, 15744])

        at = [0]

        def carve(*shape):
            n = int(np.prod(shape))
            view = work[:, at[0]:at[0] + n]
            at[0] += n
            if len(shape) == 2:
                view = view.rearrange("p (a b) -> p a b", b=shape[1])
            return view

        mixT = carve(KD, T)
        q_a = carve(NQ, T)
        ckvT = carve(NKV, NKEY)
        k_rope = carve(T)
        rope_t = carve(T)
        values = carve(NKEY // P, 512)
        probs = carve(2, 7 * P)
        probs_t = carve(2, 7 * P)
        keys_at = at[0]
        kT = carve(HEADS, NKEY)
        at[0] = keys_at
        c_gate = carve(4, T)
        u_pad = carve(4, T + 4)
        conv_t = carve(T + 4)
        q_rstd = carve(T)
        at[0] = KD * T
        v_rows = carve(NT, D)
        uT = carve(KD, T)
        sg_t = carve(2, T)
        at[0] = 12672
        v_gain = carve(D)
        b_s = carve(KD, P)
        w_sT = carve(KD, P)
        at[0] = 0
        moe_out = carve(NT, D)
        silu = carve(2, F)
        hidden = carve(2, F)
        hiddenT = carve(2, F)
        weight_e = carve(SLOTS, NT)
        h_rows = moe_out
        second_at = at[0]
        h_slot = carve(2, D)
        chosen_at = at[0]
        h_slotT = carve(2, D)
        y_slot = carve(2, D)
        second = work[:, second_at:second_at + NT * D].rearrange("p (t n) -> p t n", n=D)
        chosen = work[:, chosen_at:chosen_at + NT * NE * P // 2].bitcast(mybir.dt.float16)\
            .rearrange("p (g t j n) -> p g t j n", g=NE // SLOTS, t=NT, j=SLOTS)
        token_h = ctx.enter_context(nc.sbuf_tensor("token_h", [P, NT], mybir.dt.float16))
        table = ctx.enter_context(nc.sbuf_tensor("table", [P, LAYERS, NE], mybir.dt.uint32))
        ada_row = sb("ada_row", [P, 2, 2 * P])
        ss = sb("ss", [P, 8])
        s_slot = sb("s_slot", [P, NT * NE])
        s_tmp = sb("s_tmp", [P, NT * NE])
        s_last = sb("s_last", [P, NT * NE])
        s_eq = sb("s_eq", [P, NT * NE])
        s_first = sb("s_first", [P, 2, NT])
        weight = sb("weight", [P, LAYERS, 2, NT])
        index = ctx.enter_context(nc.sbuf_tensor("index", [P, LAYERS, 2, NT], mybir.dt.uint32))
        most = sb("most", [P, 1])
        scrap = sb("scrap", [1, 1])
        most_i = ctx.enter_context(nc.sbuf_tensor("most_i", [P, LAYERS], mybir.dt.int32))
        h_all = nc.dram_tensor("h_all", [T, D], F32).ap()
        y_slots = nc.dram_tensor("y_slots", [NE * P, D], F32).ap()
        s_score = sb("s_score", [P, NT * NE])
        s_sel = sb("s_sel", [P, NT * NE])
        s_gt = sb("s_gt", [P, NT * NE, EPG])
        s_top = sb("s_top", [P, NT * NE])
        s_g = sb("s_g", [P, NT * NG])
        s_ggt = sb("s_ggt", [P, NT * NG, NG])
        s_den = sb("s_den", [P, NT])
        s_g4 = sb("s_g4", [P, NT * NG])
        combine = sb("combine", [P, NT, NE])
        sm_max = sb("sm_max", [P, 2, 4])
        sm_neg = sb("sm_neg", [P, 2, 4])
        sm_sum = sb("sm_sum", [P, 2, 4])
        sm_inv = sb("sm_inv", [P, 2, 4])

        ring_full = [sem(f"ring_full{s}") for s in range(SLOTS)]
        full = [sem(f"bank_full{b}") for b in range(BANKS)]
        taken = [sem(f"bank_taken{b}") for b in range(BANKS)]
        s_c, s_consts, s_x, s_cache, s_odd = (sem(n) for n in ("c_in", "consts_in", "x_in", "cache_in", "odd_in"))
        s_zeroc, s_ones, s_csil = sem("silu_c_zeroed"), sem("constants_set"), sem("silu_c")
        s_mod = sem("mod_ready")
        s_sq, s_squ = sem("square_ready"), sem("square_used")
        s_norm, s_hs, s_hp = (sem(n) for n in ("norm_ready", "h_sample", "h_prompt"))
        s_qn, s_kn = sem("q_normed"), sem("kv_normed")
        s_qnope, s_qrope, s_krope, s_kropes = (sem(n) for n in ("q_nope", "q_rope", "k_rope_ready", "k_rope_spread"))
        s_even_key = sem("even_key")
        s_max, s_exp, s_prob = sem("neg_max"), sem("exp_done"), sem("probs_ready")
        s_res = sem("residual")
        s_vss, s_vrms, s_vn, s_sg = sem("v_squares"), sem("v_rms"), sem("v_normed"), sem("spatial_gated")
        s_sent, s_acc = sem("rows_sent"), sem("squares_added")
        s_prefix, s_rexp, s_weight = sem("prefix_ready"), sem("router_exp"), sem("weight_ready")
        s_comb, s_mask, s_index, s_hstored = sem("combine_ready"), sem("mask_ready"), sem("index_ready"), sem("h_stored")
        s_chosen, s_most = sem("chosen_ready"), sem("most_ready")
        def layered(name):
            return [sem(f"{name}{l}") for l in range(LAYERS)]

        s_expert = layered("expert_done")
        s_we, s_dup, s_dsilu, s_dhid, s_dtr, s_dht, s_dn, s_dt = (layered(n) for n in (
            "all_weight", "all_up", "all_silu", "all_hidden", "all_hidden_t", "all_copied", "all_down", "all_summed"))
        s_turn0, s_turn1, s_copy0, s_copy1 = (layered(n) for n in (
            "h_turned0", "h_turned1", "h_copied0", "h_copied1"))
        s_up, s_silu, s_hid, s_tr, s_ht, s_y0, s_y1, s_scaled, s_sum = (layered(n) for n in (
            "up_ready", "silu_ready", "hidden_ready", "hidden_t", "hidden_copied", "y_taken0", "y_taken1",
            "first_scaled", "sum_ready"))
        s_back = [[[sem(f"y_gathered{l}_{c}_{t}") for t in range(NT)] for c in range(2)] for l in range(LAYERS)]
        s_h = [[sem(f"h_loaded{l}_{b}") for b in range(2)] for l in range(LAYERS)]
        s_yst = [[sem(f"y_stored{l}_{b}") for b in range(2)] for l in range(LAYERS)]
        s_chain = sem("vector_step")
        s_out = sem("stored")
        s_y = sem("y_ready")

        TOK = [(0, 0, TP), (1, TP, T)]

        def slot(chunk):
            return CHUNK_AT[chunk] % SLOTS, CHUNK_AT[chunk] // SLOTS

        def wait(eng, s, value):
            if not (isinstance(value, int) and value <= 0):
                eng.wait_ge(s, value)

        def rounds(eng, body):
            last = NE // SLOTS - 1
            body(0, True)
            with eng.Fori(1, last) as i:
                body(i, False)
            body(last, True)

        block = ctx.enter_context(nc.Block())

        @block.sync
        def _(sp):
            def wait_used(n):
                kind, i = CHUNKS[n - SLOTS]
                if kind == "moe":
                    sp.wait_ge(s_expert[i[0]], i[1] + 1)
                else:
                    b, turn = bank_of(last_user((kind, i)))
                    sp.wait_ge(full[b], turn + 1)

            sp.dma_start(cvec[:], a["cvec"]).then_inc(s_c, 16)
            sp.dma_start(smalls[:], a["smalls"]).then_inc(s_consts, 16)
            sp.dma_start(xT[:], a["xT"]).then_inc(s_x, 16)

            def load(n):
                kind, i = CHUNKS[n]
                if kind == "moe" and i[1] in (2, 3):
                    sp.wait_ge(s_sent, SENT * i[0] + i[1] - 1)
                if (kind, i) == ("ada", 13):
                    sp.wait_ge(s_sent, SENT)
                src = a["ada_w"][i // 4, i % 4] if kind == "ada" else a["moe"][i[0], i[1]] if kind == "moe" else a[kind][i]
                if n >= SLOTS:
                    wait_used(n)
                sp.dma_start(ring[:, n % SLOTS, 0:src.shape[-1]], src).then_inc(ring_full[n % SLOTS], 16)

            def load_experts(l):
                base = CHUNK_AT[("moe", (l, 0))]
                for n in range(base, base + SLOTS):
                    load(n)
                with sp.Fori(0, NE // SLOTS - 1) as i:
                    for j in range(SLOTS):
                        s = (base + j) % SLOTS
                        sp.wait_ge(s_expert[l], i * SLOTS + (j + 1))
                        sp.dma_start(ring[:, s, :], a["moe"][l, i * SLOTS + (SLOTS + j)]).then_inc(ring_full[s], 16)

            for l in range(LAYERS):
                first = 0 if l == 0 else CHUNK_AT[("moe", (0, NE - 1))] + 1
                for n in range(first, CHUNK_AT[("moe", (l, 0))]):
                    load(n)
                load_experts(l)

        @block.gpsimd
        def _(pool):
            pool.memset(csil[:, :, :], 0.0).then_inc(s_zeroc, 1)
            for n, width in enumerate((D, QR, KVR)):
                pool.memset(share[:, n, :], 1.0 / width).then_inc(s_ones, 1)
            pool.memset(eps[:, :], EPS).then_inc(s_ones, 1)
            pool.memset(ones_b[:, :], 1.0).then_inc(s_ones, 1)
            pool.memset(u_pad, 0.0).then_inc(s_ones, 1)

            def sent(l, n):
                if SENT * l + n > 0:
                    pool.wait_ge(s_sent, SENT * l + n)
                pool.memset(scrap[:, :], 0.0).then_inc(s_sent, 1)

            def fetch(l, e):
                if e % SLOTS == 0:
                    key = ("table", l, e // SLOTS)
                    pool.wait_ge(taken[bank_of(key)[0]], takes(key))
                if e >= 2:
                    pool.wait_ge(s_turn1[l], e - 1)
                pool.indirect_dma_start(h_slot[:, e % 2, :], None, h_all,
                                        bass.IndirectOffsetOnAxis(ap=table[:, l, e:e + 1], axis=0))\
                    .then_inc(s_h[l][e % 2], 16)

            def gather(l):
                stored = 16 * NE // 2
                pool.wait_ge(s_index, l + 1)
                pool.wait_ge(s_yst[l][0], stored)
                pool.wait_ge(s_yst[l][1], stored - 16)
                for c, dst in ((0, moe_out), (1, second)):
                    if c == 1:
                        pool.wait_ge(s_yst[l][1], stored)
                    for t in range(NT):
                        pool.indirect_dma_start(dst[:, t, :], None, y_slots[0:(NE - 1 + c) * P, :],
                                                bass.IndirectOffsetOnAxis(ap=index[:, l, c, t:t + 1], axis=0))\
                            .then_inc(s_back[l][c][t], 16)

            for l in range(LAYERS):
                pool.wait_ge(s_hstored, 16 * NT * (l + 1))
                pool.wait_ge(s_most, l + 1)
                count = pool.value_load(most_i[0:1, l:l + 1], min_val=0, max_val=T)
                with pool.If(count < P + 1):
                    for e in range(NE):
                        fetch(l, e)
                        if e in (2, 3):
                            sent(l, e - 2)
                    gather(l)
                    sent(l, 2)
                    for c in range(2):
                        for t in range(NT):
                            pool.wait_ge(s_back[l][c][t], 16)
                with pool.Else():
                    for n in range(SENT):
                        sent(l, n)

        @block.scalar
        def _(act):
            def product(*key):
                b, turn = bank_of(key)
                act.wait_ge(full[b], turn + 1)
                return bank[b]

            def take(ins, *key):
                ins.then_inc(taken[bank_of(key)[0]], 1)

            def wait_taken(*key):
                act.wait_ge(taken[bank_of(key)[0]], takes(key))

            act.dma_start(ckvT[:, :, T:NKEY], a["cache_ckv"]).then_inc(s_cache, 16)

            act.wait_ge(s_c, 16)
            act.wait_ge(s_zeroc, 1)
            act.activation(csil[:, :, 0:2], cvec[:], ACT.Silu).then_inc(s_csil, 1)

            def squares(q):
                for k in range(KD):
                    if q == 0 and k == 0:
                        act.wait_ge(s_x, 16)
                    elif q > 0:
                        act.wait_ge(s_res, (q - 1) * KD + k + 1)
                    if k >= 4 and q in ADDED:
                        act.wait_ge(s_acc, ADDED.index(q) * (KD - 1) + max(k - 4, 1))
                    elif k >= 4:
                        act.wait_ge(s_squ, squ_n[0] + k - 3)
                    act.activation(sq[:, k % 4, :], xT[:, k, :], ACT.Square).then_inc(s_sq, 1)
                if q not in ADDED:
                    squ_n[0] += KD - 1

            squ_n = [0]

            def root(dst, *key):
                take(act.activation(dst, product(*key)[:, 0:T], ACT.Sqrt, bias=eps[:, 0:1]), *key)

            def modulate(q):
                act.wait_ge(s_mod, q + 1)
                for k in range(KD):
                    act.wait_ge(s_norm, q * KD + k + 1)
                    act.activation(hT[:, k, 0:TP], hT[:, k, 0:TP], ACT.Identity, bias=mod[:, q, k, 0:1],
                                   scale=gain1[:, q, k, 0:1]).then_inc(s_hp, 1)

            def ada(*chunks):
                for n in chunks:
                    if n >= 2:
                        product("ada_t", n - 2)
                    take(act.activation(ada_row[:, n % 2, :], product("ada_row", n)[:, 0:2 * P], ACT.Identity), "ada_row", n)

            squares(0)
            act.wait_ge(s_ones, 4)
            root(rstd[:, :], "norm", 0)
            ada(0, 1, 2)
            act.wait_ge(s_consts, 16)
            act.activation(earlier_b[:, :], earlier, ACT.Identity).then_inc(s_prefix, 1)
            act.activation(token_h[:, :], token, ACT.Identity).then_inc(s_prefix, 1)
            modulate(0)

            for j in range(NQ + NKV):
                wait_taken("ev_in", j)
                src = q_a[:, j, :] if j < NQ else ckvT[:, j - NQ, 0:T]
                if j == 4:
                    act.wait_ge(s_squ, squ_n[0] + 1)
                act.activation(sq[:, j % 4, :], src, ACT.Square).then_inc(s_sq, 1)
            squ_n[0] += NQ - 1 + NKV - 1
            root(q_rstd, "q_norm")
            root(rstd[:, :], "kv_norm")
            act.wait_ge(s_kn, NKV)
            act.dma_start(out["state_ckv"], ckvT[:, :, 0:TP]).then_inc(s_out, 16)
            act.wait_ge(s_krope, 1)
            act.dma_start(out["state_krope"], k_rope[NOPE:QK, 0:TP]).then_inc(s_out, 16)
            for j in range(4):
                n = 6 + 2 * j
                take(act.activation(c_gate[:, j, :], product("ev_in", n)[:, 0:T], ACT.Identity), "ev_in", n)
            for t in range(NKEY // P):
                take(act.activation(values[:, t, :], product("v_up", t)[:, :], ACT.Identity), "v_up", t)
            for h in range(HEADS):
                ps = product("q_up", h)
                act.activation(qT[0:NOPE, h, :], ps[0:NOPE, 0:T], ACT.Identity).then_inc(s_qnope, 1)
            wait_taken("ev_in", EV_TILES - 1)
            act.dma_start(kT[NOPE:QK, :, T:NKEY], a["cache_krope"]).then_inc(s_cache, 16)
            act.activation(kT[NOPE:QK, :, 0:T],
                           k_rope[NOPE:QK, :].rearrange("p (a t) -> p a t", a=1).to_broadcast([ROPE, HEADS, T]),
                           ACT.Identity).then_inc(s_kropes, 1)
            for j in range(HEADS // 2):
                ps = product("k_up", j)
                act.activation(kT[0:NOPE, 2 * j, :], ps[0:NOPE, :], ACT.Identity).then_inc(s_even_key, 1)

            def exps(h):
                b = h % 2
                act.wait_ge(s_max, h + 1)
                if h >= 2:
                    product("probs_t", h - 2, 1)
                p0, p1 = product("score", h, 0), product("score", h, 1)
                for c, (ps, lo, hi, dst) in enumerate([(p0, 0, P, 0), (p0, P, 512, P), (p1, 0, 384, 512)]):
                    act.activation(probs[:, b, dst:dst + hi - lo], ps[:, lo:hi], ACT.Exp, bias=sm_neg[:, b, c:c + 1],
                                   scale=SCALE, accum_out=sm_sum[:, b, c:c + 1]).then_inc(s_exp, 1)

            for s in range(HEADS + 3):
                if 2 <= s < HEADS + 2:
                    h = s - 2
                    if h >= 2:
                        product("attend", h // 2 - 1)
                    take(act.activation(probs_t[:, h % 2, 0:512], product("probs_t", h, 0)[:, :], ACT.Identity),
                         "probs_t", h, 0)
                if s < HEADS:
                    exps(s)
                if s >= 4 and s % 2 == 0:
                    pair = s // 2 - 2
                    take(act.activation(mixT[:, 4 + pair, :], product("attend", pair)[:, 0:T], ACT.Identity), "attend", pair)
                ada(*attention_ada(s)[0])

            def experts_all(l):
                with act.Fori(0, NE // SLOTS) as i:
                    for n in range(SLOTS * NT):
                        b = n % 2
                        act.wait_ge(s_dup[l], i * (SLOTS * NT) + (n + 1))
                        act.activation(silu[:, b, :], bank[b][:, 0:F], ACT.Silu).then_inc(s_dsilu[l], 1)
                        act.wait_ge(s_dtr[l], i * (SLOTS * NT) + (n + 1))
                        act.activation(hiddenT[:, b, :], bank[2 + b][:, 0:F], ACT.Identity).then_inc(s_dht[l], 1)

            def copy_h(l, i, e):
                b = e % 2
                act.wait_ge(s_turn0[l], i * SLOTS + (e + 1))
                act.activation(h_slotT[:, b, 0:512], bank[2][:, :], ACT.Identity).then_inc(s_copy0[l], 1)

            def silus(l, i, e):
                act.wait_ge(s_up[l], i * SLOTS + (e + 1))
                act.activation(silu[:, e % 2, :], bank[e % 2][:, 0:F], ACT.Silu).then_inc(s_silu[l], 1)

            def experts_routed(l):
                for e in range(2):
                    copy_h(l, 0, e)
                silus(l, 0, 0)

                def round_(i, static):
                    for j in range(SLOTS):
                        b = j % 2
                        last = static and i > 0
                        act.wait_ge(s_tr[l], i * SLOTS + (j + 1))
                        act.activation(hiddenT[:, b, :], bank[6 + b][:, 0:F], ACT.Identity).then_inc(s_ht[l], 1)
                        if not (last and j == SLOTS - 1):
                            silus(l, i, j + 1)
                        if not (last and j >= SLOTS - 2):
                            copy_h(l, i, j + 2)
                        act.wait_ge(s_expert[l], i * SLOTS + (j + 1))
                        wait(act, s_yst[l][b], i * 32 + 16 * (j // 2))
                        act.activation(y_slot[:, b, 0:512], bank[4][:, :], ACT.Identity).then_inc(s_y0[l], 1)
                        act.wait_ge(s_y0[l], i * SLOTS + (j + 1))
                        act.wait_ge(s_y1[l], i * SLOTS + (j + 1))
                        act.dma_start(y_slots[bass.ds(i * (SLOTS * P) + j * P, P), :], y_slot[:, b, :])\
                            .then_inc(s_yst[l][b], 16)

                rounds(act, round_)
                if l == 0:
                    ada(11)
                act.wait_ge(s_weight, 2 * l + 2)
                for t in range(NT):
                    act.wait_ge(s_back[l][0][t], 16)
                    act.activation(moe_out[:, t, :], moe_out[:, t, :], ACT.Identity, scale=weight[:, l, 0, t:t + 1])\
                        .then_inc(s_scaled[l], 1)
                if l == 0:
                    ada(12)

            def dispatch(l):
                take(act.activation(logit_t[:, :], product("router", l)[:, 0:T], ACT.Identity), "router", l)
                wait_taken("logits", l)
                act.activation(s_score[:, :], s_score[:, :], ACT.Exp, scale=-1.0).then_inc(s_rexp, 1)
                for t in range(NT):
                    for c in range(2):
                        key = ("h_row", l, t, c)
                        take(act.activation(h_rows[:, t, c * 512:c * 512 + 512], product(*key)[:, :], ACT.Identity), *key)
                    for c in range(2):
                        wait_taken("h_row", l, t, c)
                    act.dma_start(h_all[t * P:t * P + P, :], h_rows[:, t, :]).then_inc(s_hstored, 16)

            def moe(l):
                act.wait_ge(s_most, l + 1)
                count = act.value_load(most_i[0:1, l:l + 1], min_val=0, max_val=T)
                with act.If(count < P + 1):
                    experts_routed(l)
                with act.Else():
                    experts_all(l)
                    if l == 0:
                        ada(11, 12)

            squares(1)
            root(rstd[:, :], "norm", 1)
            modulate(1)
            ada(8)
            product("mix_out", 0, KD - 1)
            act.dma_start(v_gain, a["v_gain"].to_broadcast([P, D])).then_inc(s_odd, 16)
            act.dma_start(b_s, a["b_s"].to_broadcast([P, KD, P])).then_inc(s_odd, 16)
            act.dma_start(w_sT, a["w_sT"]).then_inc(s_odd, 16)
            dispatch(0)
            ada(9, 10)
            moe(0)
            squares(2)
            root(rstd[:, :], "norm", 2)
            modulate(2)
            ada(13)

            for c in range(2):
                for t in range(NT):
                    take(act.activation(v_rows[:, t, c * 512:c * 512 + 512], product("gm_v", t, c)[:, :], ACT.Gelu),
                         "gm_v", t, c)
            for j in range(KD):
                take(act.activation(uT[:, j, :], product("gm_u", j)[:, 0:T], ACT.Gelu), "gm_u", j)
                if j == 0:
                    wait_taken("gm_v", NT - 1, 1)
                    for t in range(NT):
                        act.activation(sq[:, :, :].rearrange("p a b -> p (a b)")[:, 0:D], v_rows[:, t, :],
                                       ACT.Square, accum_out=ss[:, t:t + 1]).then_inc(s_vss, 1)
                        act.wait_ge(s_vss, t + 1)
                    act.activation(ss[:, 3:3 + NT], ss[:, 0:NT], ACT.Sqrt, bias=eps[:, 0:1],
                                   scale=1.0 / D).then_inc(s_vrms, 1)

            squares(3)
            ada(14)
            root(rstd[:, :], "norm", 3)
            modulate(3)
            dispatch(1)
            ada(15)
            moe(1)
            squares(4)
            root(rstd[:, :], "norm", 4)
            for k in range(KD):
                act.wait_ge(s_y, k + 1)
                act.dma_start(out["y"][:, k, :], hT[:, k, :]).then_inc(s_out, 16)
            act.wait_ge(s_out, 16 * (KD + 2))

        @block.vector
        def _(dve):
            chain = [0]

            def step(ins):
                ins.then_inc(s_chain, 1)
                chain[0] += 1
                dve.wait_ge(s_chain, chain[0])

            def product(*key):
                b, turn = bank_of(key)
                dve.wait_ge(full[b], turn + 1)
                return bank[b]

            def take(ins, *key):
                ins.then_inc(taken[bank_of(key)[0]], 1)

            def wait_taken(*key):
                dve.wait_ge(taken[bank_of(key)[0]], takes(key))

            def tt(o, x, y, op):
                return dve.tensor_tensor(o, x, y, op)

            def stt(o, x, s, y, op0, op1):
                return dve.scalar_tensor_tensor(out=o, in0=x, scalar=s, in1=y, op0=op0, op1=op1)

            def ada(*chunks):
                for n in chunks:
                    q, at_ = n // 4, n % 4 * ADA_TILES
                    four, two = (product("ada_t", n)[:, i * P:i * P + P].rearrange("p (g s) -> p g s", s=32)[:, :, 0:2]
                                 for i in range(2))
                    bias = b_ada[:, q, at_:at_ + ADA_TILES].rearrange("p (n a) -> p n a", a=1).to_broadcast([P, ADA_TILES, 2])
                    tt(mod[:, q, at_:at_ + 4, :], four, bias[:, 0:4, :], ALU.add)
                    step(tt(mod[:, q, at_ + 4:at_ + 6, :], two[:, 0:2, :], bias[:, 4:6, :], ALU.add))
                    take(tt(mod[:, q, at_ + 4:at_ + 6, :], two[:, 2:4, :], mod[:, q, at_ + 4:at_ + 6, :], ALU.add), "ada_t", n)
                    wait_taken("ada_t", n)
                    if n % 4 == 2:
                        g = gains[:, q, :].rearrange("p (n a) -> p n a", a=1).to_broadcast([P, KD, 2])
                        stt(gain1[:, q, :, :], mod[:, q, KD:2 * KD, :], 1.0, g, ALU.add, ALU.mult).then_inc(s_mod, 1)
                        dve.wait_ge(s_mod, q + 1)

            def inverse(rms, *key):
                wait_taken(*key)
                step(dve.reciprocal(rms, rms))

            def normalised(q, k):
                tt(hT[:, k, :], xT[:, k, :], rstd[:, :], ALU.mult).then_inc(s_norm, 1)

            def modulated(q, k):
                dve.wait_ge(s_norm, q * KD + k + 1)
                dve.tensor_scalar(hT[:, k, TP:T], hT[:, k, TP:T], gain1[:, q, k, 1:2], mod[:, q, k, 1:2],
                                  ALU.mult, ALU.add).then_inc(s_hs, 1)

            def norm(q):
                inverse(rstd[:, :], "norm", q)
                if q == 0:
                    for k in range(KD):
                        normalised(q, k)
                    dve.wait_ge(s_consts, 16)
                    ada(0, 1, 2)
                    for k in range(KD):
                        modulated(q, k)
                else:
                    if q == 3:
                        ada(14)
                    for k in range(KD):
                        normalised(q, k)
                        if k > 0:
                            modulated(q, k - 1)
                    modulated(q, KD - 1)

            def residual(l, half, d, src):
                q = 2 * l + half
                stt(xT[:, d, 0:TP], src[:, 0:TP], mod[:, q, 2 * KD + d, 0:1], xT[:, d, 0:TP], ALU.mult, ALU.add)
                stt(xT[:, d, TP:T], src[:, TP:T], mod[:, q, 2 * KD + d, 1:2], xT[:, d, TP:T], ALU.mult, ALU.add)\
                    .then_inc(s_res, 1)

            dve.wait_ge(s_x, 16)
            norm(0)

            for j in range(NQ + NKV):
                dst = q_a[:, j, :] if j < NQ else ckvT[:, j - NQ, 0:T]
                take(dve.tensor_copy(dst, product("ev_in", j)[:, 0:T]), "ev_in", j)
            ps = product("ev_in", 5)
            tt(rope_t[NOPE:QK, :], ps[NOPE:QK, 0:T], rope[NOPE:QK, :], ALU.mult)
            take(tt(k_rope[NOPE:QK, :], ps[QK:P, 0:T], rope[QK:P, :], ALU.mult), "ev_in", 5)
            wait_taken("ev_in", 5)
            tt(k_rope[NOPE:QK, :], k_rope[NOPE:QK, :], rope_t[NOPE:QK, :], ALU.add).then_inc(s_krope, 1)
            inverse(q_rstd, "q_norm")
            for j in range(NQ):
                stt(q_a[:, j, :], q_a[:, j, :], qkv_g[:, j:j + 1], q_rstd, ALU.mult, ALU.mult).then_inc(s_qn, 1)
            inverse(rstd[:, :], "kv_norm")
            for j in range(NKV):
                stt(ckvT[:, j, 0:T], ckvT[:, j, 0:T], qkv_g[:, NQ + j:NQ + j + 1], rstd[:, :], ALU.mult,
                    ALU.mult).then_inc(s_kn, 1)
            dve.wait_ge(s_ones, 6)
            U = T + 4
            for j in range(4):
                wait_taken("ev_in", 6 + 2 * j)
                ps = product("ev_in", 7 + 2 * j)
                tt(u_pad[:, j, 1:1 + TP], ps[:, 0:TP], c_gate[:, j, 0:TP], ALU.mult)
                take(tt(u_pad[:, j, TP + 3:U - 1], ps[:, TP:T], c_gate[:, j, TP:T], ALU.mult), "ev_in", 7 + 2 * j)
            for j in range(4):
                wait_taken("ev_in", 7 + 2 * j)
                if j > 0:
                    wait_taken("ev_in", 13 + j)
                u = u_pad[:, j, :]
                t = conv_t[:, 1:U - 1]
                step(dve.tensor_scalar(t, u[:, 0:U - 2], conv_w[:, j, 0:1], None, ALU.mult))
                step(stt(t, u[:, 1:U - 1], conv_w[:, j, 1:2], t, ALU.mult, ALU.add))
                step(stt(t, u[:, 2:U], conv_w[:, j, 2:3], t, ALU.mult, ALU.add))
                ps = product("ev_in", 14 + j)
                tt(mixT[:, j, 0:TP], conv_t[:, 1:1 + TP], ps[:, 0:TP], ALU.mult)
                take(tt(mixT[:, j, TP:T], conv_t[:, TP + 3:U - 1], ps[:, TP:T], ALU.mult), "ev_in", 14 + j)
            for h in range(HEADS):
                ps = product("q_up", h)
                tt(qT[NOPE:QK, h, :], ps[NOPE:QK, 0:T], rope[NOPE:QK, :], ALU.mult)
                dve.wait_ge(s_qnope, h + 1)
                if h > 0:
                    dve.wait_ge(s_qrope, h)
                take(tt(rope_t[NOPE:QK, :], ps[QK:P, 0:T], rope[QK:P, :], ALU.mult), "q_up", h)
                wait_taken("q_up", h)
                tt(qT[NOPE:QK, h, :], qT[NOPE:QK, h, :], rope_t[NOPE:QK, :], ALU.add).then_inc(s_qrope, 1)
            for j in range(HEADS // 2):
                ps = product("k_up", j)
                dve.wait_ge(s_even_key, j + 1)
                take(dve.tensor_copy(kT[0:NOPE, 2 * j + 1, :], ps[NOPE:P, :]), "k_up", j)

            def maxima(h):
                b = h % 2
                p0, p1 = product("score", h, 0), product("score", h, 1)
                dve.reduce_max(sm_max[:, b, 0:1], p0[:, 0:P], AX.X)
                dve.reduce_max(sm_max[:, b, 1:2], p0[:, P:512], AX.X)
                step(dve.reduce_max(sm_max[:, b, 2:3], p1[:, 0:384], AX.X))
                dve.tensor_scalar(sm_neg[:, b, 0:3], sm_max[:, b, 0:3], -SCALE, None, ALU.mult).then_inc(s_max, 1)

            def normalise(h):
                b = h % 2
                dve.wait_ge(s_exp, 3 * h + 3)
                step(dve.reciprocal(sm_inv[:, b, 0:3], sm_sum[:, b, 0:3]))
                for c, (lo, hi) in enumerate([(0, P), (P, 512), (512, 896)]):
                    ins = dve.tensor_scalar(probs[:, b, lo:hi], probs[:, b, lo:hi], sm_inv[:, b, c:c + 1], None, ALU.mult)
                ins.then_inc(s_prob, 1)

            for s in range(HEADS + 2):
                if s >= 2:
                    h = s - 2
                    if h >= 2:
                        product("attend", h // 2 - 1)
                    take(dve.tensor_copy(probs_t[:, h % 2, 512:896], product("probs_t", h, 1)[:, 0:384]), "probs_t", h, 1)
                if 1 <= s <= HEADS:
                    normalise(s - 1)
                if s < HEADS:
                    maxima(s)
                ada(*attention_ada(s)[1])

            def add_square(q, k):
                dve.wait_ge(s_sq, squares_before(q) + k + 1)
                n = ADDED.index(q) * (KD - 1) + k
                if k > 1:
                    dve.wait_ge(s_acc, n - 1)
                tt(acc[:, :], sq[:, 0, :] if k == 1 else acc[:, :], sq[:, k % 4, :], ALU.add).then_inc(s_acc, 1)

            def mix_out(l):
                for d in range(KD):
                    residual(l, 0, d, product("mix_out", l, d))
                    if d >= 2:
                        add_square(2 * l + 1, d - 1)
                add_square(2 * l + 1, KD - 1)

            def route(l):
                ps = product("logits", l)[:, 0:T].rearrange("p (t g e) -> p t e g", g=4, e=32)[:, :, 0:NE, :]
                take(dve.tensor_reduce(s_score[:, :].rearrange("p (t e) -> p t e", e=NE), ps, AX.X, ALU.add), "logits", l)
                dve.wait_ge(s_rexp, l + 1)
                step(dve.tensor_scalar(s_score[:, :], s_score[:, :], 1.0, None, ALU.add))
                step(dve.reciprocal(s_score[:, :], s_score[:, :]))
                sc3 = s_score[:, :].rearrange("p (t e) -> p t e", e=NE)
                rb = router_b.rearrange("p (a e) -> p a e", a=1).to_broadcast([P, NT, NE])
                step(tt(s_sel[:, :].rearrange("p (t e) -> p t e", e=NE), sc3, rb, ALU.add))

                def ranks(score, groups, gt, rank):
                    other = score.rearrange("p (g a j) -> p g a j", a=1, j=4).to_broadcast([P, groups, 4, 4])
                    own = score.rearrange("p (g i a) -> p g i a", i=4, a=1).to_broadcast([P, groups, 4, 4])
                    gt4 = gt[:].rearrange("p (g i) j -> p g i j", i=4)
                    least = threshold.rearrange("p (a i j) -> p a i j", a=1, j=4).to_broadcast([P, groups, 4, 4])
                    step(tt(gt4, other, own, ALU.subtract))
                    step(tt(gt4, gt4, least, ALU.is_ge))
                    step(dve.tensor_reduce(rank, gt[:], AX.X, ALU.add))

                ranks(s_sel[:, :], NT * NG, s_gt, s_top[:, :])
                step(stt(s_sel[:, :], s_top[:, :], 2.0, s_sel[:, :], ALU.is_lt, ALU.mult))
                dve.tensor_scalar(s_top[:, :], s_top[:, :], 2.0, None, ALU.is_lt)
                step(dve.tensor_reduce(s_g[:, :], s_sel[:, :].rearrange("p (g j) -> p g j", j=4), AX.X, ALU.add))
                ranks(s_g[:, :], NT, s_ggt, s_g4[:, :])
                four = lambda x: x[:, :].rearrange("p (g j) -> p g j", j=4)
                best = s_g4[:, :].rearrange("p (g a) -> p g a", a=1).to_broadcast([P, NT * NG, 4])
                stt(four(top_b), best, 1.0, four(s_top), ALU.is_lt, ALU.mult).then_inc(s_mask, 1)
                dve.wait_ge(s_mask, l + 1)
                step(stt(four(s_top), best, 1.0, four(s_top), ALU.is_lt, ALU.mult))
                step(tt(s_score[:, :], s_score[:, :], s_top[:, :], ALU.mult))
                step(dve.tensor_reduce(s_den[:, :], sc3, AX.X, ALU.add))
                step(dve.reciprocal(s_den[:, :], s_den[:, :]))
                den = s_den[:, :].rearrange("p (t a) -> p t a", a=1).to_broadcast([P, NT, NE])
                tt(combine[:, :, :], sc3, den, ALU.mult).then_inc(s_comb, 1)
                dve.wait_ge(s_comb, l + 1)

            three = lambda x: x[:, :].rearrange("p (t e) -> p t e", e=NE)

            def place(l):
                ps = product("slots", l)
                dve.reduce_max(most[:, 0:1], ps[:, NT * NE:NT * NE + NE], AX.X)
                stt(s_tmp[:, :], ps[:, 0:NT * NE], 1.0, s_top[:, :], ALU.add, ALU.mult)
                take(tt(s_slot[:, :], ps[:, 0:NT * NE], expert_base, ALU.add), "slots", l)
                wait_taken("slots", l)
                dve.tensor_copy(most_i[:, l:l + 1], most[:, 0:1]).then_inc(s_most, 1)
                places = place_no.rearrange("p (a b n) -> p a b n", a=1, b=1).to_broadcast([P, NT, SLOTS, P])

                def tokens(g):
                    take(dve.tensor_copy(table[:, l, g * SLOTS:g * SLOTS + SLOTS], product("table", l, g)[:, 0:SLOTS]),
                         "table", l, g)

                for g in range(NE // SLOTS):
                    own = three(s_tmp)[:, :, g * SLOTS:g * SLOTS + SLOTS].rearrange("p t (j a) -> p t j a", a=1)
                    tt(chosen[:, g, :, :, :], places, own.to_broadcast([P, NT, SLOTS, P]), ALU.is_equal)\
                        .then_inc(s_chosen, 1)
                    if g != 1:
                        tokens(max(g - 1, 0))
                tokens(NE // SLOTS - 1)

            def index_rows(l):
                spread = lambda x: x.rearrange("p (t a) -> p t a", a=1).to_broadcast([P, NT, NE])
                dve.wait_ge(s_chosen, NE // SLOTS * (l + 1))
                stt(s_tmp[:, :], s_top[:, :], -4096.0, s_slot[:, :], ALU.mult, ALU.add)
                step(tt(s_last[:, :], s_top[:, :], s_slot[:, :], ALU.mult))
                dve.tensor_reduce(s_first[:, 0, :], three(s_tmp), AX.X, ALU.min)
                step(dve.tensor_reduce(s_first[:, 1, :], three(s_last), AX.X, ALU.max))
                dve.tensor_scalar(index[:, l, 0, :], s_first[:, 0, :], 4096.0, None, ALU.add)
                dve.tensor_copy(index[:, l, 1, :], s_first[:, 1, :]).then_inc(s_index, 1)
                dve.wait_ge(s_index, l + 1)
                step(dve.tensor_scalar(s_first[:, 0, :], s_first[:, 0, :], 4096.0, None, ALU.add))
                for c in range(2):
                    step(tt(three(s_eq), three(s_slot), spread(s_first[:, c, :]), ALU.is_equal))
                    step(tt(three(s_eq), three(s_eq), combine[:, :, :], ALU.mult))
                    dve.tensor_reduce(weight[:, l, c, :], three(s_eq), AX.X, ALU.add).then_inc(s_weight, 1)
                    dve.wait_ge(s_weight, 2 * l + c + 1)

            def experts_all(l):
                dve.wait_ge(s_hstored, 16 * NT * (l + 1))
                dve.memset(moe_out, 0.0).then_inc(s_dt[l], 1)
                dve.wait_ge(s_dt[l], 1)
                with dve.Fori(0, NE // SLOTS) as i:
                    for j in range(SLOTS):
                        e = i * SLOTS + j
                        dve.tensor_copy(weight_e[:, j, :],
                                        combine[:, :, bass.ds(e, 1)].rearrange("p t a -> p (t a)")).then_inc(s_we[l], 1)
                        dve.wait_ge(s_we[l], i * SLOTS + (j + 1))
                        for t in range(NT):
                            n = j * NT + t
                            b = n % 2
                            dve.wait_ge(s_dsilu[l], i * (SLOTS * NT) + (n + 1))
                            stt(hidden[:, b, :], silu[:, b, :], weight_e[:, j, t:t + 1], bank[b][:, F:2 * F],
                                ALU.mult, ALU.mult).then_inc(s_dhid[l], 1)
                            if t < NT - 1:
                                dve.wait_ge(s_dn[l], i * (SLOTS * (NT - 1)) + (j * (NT - 1) + t + 1))
                            else:
                                dve.wait_ge(s_expert[l], i * SLOTS + (j + 1))
                            for c in range(2):
                                ins = tt(moe_out[:, t, c * 512:c * 512 + 512], moe_out[:, t, c * 512:c * 512 + 512],
                                         bank[4 + 2 * b + c][:, :], ALU.add)
                            ins.then_inc(s_dt[l], 1)
                            dve.wait_ge(s_dt[l], i * (SLOTS * NT) + (n + 2))

            def copy_h(l, i, e):
                dve.wait_ge(s_turn1[l], i * SLOTS + (e + 1))
                dve.tensor_copy(h_slotT[:, e % 2, 512:D], bank[3][:, :]).then_inc(s_copy1[l], 1)

            def gate(l, i, e):
                dve.wait_ge(s_silu[l], i * SLOTS + (e + 1))
                tt(hidden[:, e % 2, :], silu[:, e % 2, :], bank[e % 2][:, F:2 * F], ALU.mult).then_inc(s_hid[l], 1)

            def experts_routed(l):
                for e in range(2):
                    copy_h(l, 0, e)
                gate(l, 0, 0)

                def round_(i, static):
                    for j in range(SLOTS):
                        last = static and i > 0
                        if not (last and j >= SLOTS - 2):
                            copy_h(l, i, j + 2)
                        if not (last and j == SLOTS - 1):
                            gate(l, i, j + 1)
                        dve.wait_ge(s_expert[l], i * SLOTS + (j + 1))
                        wait(dve, s_yst[l][j % 2], i * 32 + 16 * (j // 2))
                        dve.tensor_copy(y_slot[:, j % 2, 512:D], bank[5][:, :]).then_inc(s_y1[l], 1)

                round_(0, True)
                index_rows(l)
                with dve.Fori(1, NE // SLOTS - 1) as i:
                    round_(i, False)
                round_(NE // SLOTS - 1, True)
                if l == 0:
                    ada(11, 12)
                for t in range(NT):
                    dve.wait_ge(s_scaled[l], t + 1)
                    dve.wait_ge(s_back[l][1][t], 16)
                    stt(moe_out[:, t, :], second[:, t, :], weight[:, l, 1, t:t + 1], moe_out[:, t, :],
                        ALU.mult, ALU.add).then_inc(s_sum[l], 1)

            def dispatch(l):
                route(l)
                place(l)

            def moe(l):
                count = dve.value_load(most_i[0:1, l:l + 1], min_val=0, max_val=T)
                steps = chain[0]
                with dve.If(count < P + 1):
                    experts_routed(l)
                chain[0] = steps
                with dve.Else():
                    index_rows(l)
                    experts_all(l)
                    if l == 0:
                        ada(11, 12)

            def moe_add(l):
                for d in range(KD):
                    residual(l, 1, d, product("moe_t", l, d))

            mix_out(0)
            norm(1)
            dispatch(0)
            ada(8, 9, 10)
            moe(0)
            moe_add(0)
            norm(2)
            ada(13)

            dve.wait_ge(s_odd, 48)
            dve.wait_ge(s_vrms, 1)
            step(dve.reciprocal(ss[:, 3:3 + NT], ss[:, 3:3 + NT]))
            for t in range(NT):
                stt(v_rows[:, t, :], v_rows[:, t, :], ss[:, 3 + t:4 + t], v_gain, ALU.mult, ALU.mult).then_inc(s_vn, 1)
            for g in range(KD):
                ps = product("spatial", g)[:, 0:T].rearrange("p (n q) -> p n q", q=P)
                bias = b_s[:, g, :].rearrange("p (a q) -> p a q", a=1).to_broadcast([P, NT, P])
                take(tt(sg_t[:, g % 2, :].rearrange("p (n q) -> p n q", q=P), ps, bias, ALU.add), "spatial", g)
                wait_taken("spatial", g)
                wait_taken("gm_u", g)
                tt(mixT[:, g, :], sg_t[:, g % 2, :], uT[:, g, :], ALU.mult).then_inc(s_sg, 1)
                dve.wait_ge(s_sg, g + 1)
            mix_out(1)
            norm(3)
            dispatch(1)
            ada(15)
            moe(1)
            moe_add(1)
            inverse(rstd[:, :], "norm", 4)
            for k in range(KD):
                stt(hT[:, k, :], xT[:, k, :], gains[:, 4, k:k + 1], rstd[:, :], ALU.mult, ALU.mult).then_inc(s_y, 1)

        @block.tensor
        def _(pe):
            def opened(*key):
                n = PRODUCT_AT[key]
                if n >= BANKS:
                    emptied(PRODUCTS[n - BANKS])
                return bank[n % BANKS]

            def emptied(key):
                if key[0] in RESIDUALS:
                    pe.wait_ge(s_res, residuals(key))
                elif key[0] in SCORES:
                    pe.wait_ge(s_exp, 3 * key[1] + 2 + key[2])
                else:
                    pe.wait_ge(taken[bank_of(key)[0]], takes(key))

            def closed(ins, *key):
                ins.then_inc(full[bank_of(key)[0]], 1)

            def weights(chunk, columns):
                n = CHUNK_AT[chunk]
                pe.wait_ge(ring_full[n % SLOTS], 16 * (n // SLOTS + 1))
                return ring[:, n % SLOTS, 0:KD * columns].rearrange("p (k n) -> p k n", n=columns)

            def ada_rows(n):
                w = weights(("ada", n), ADA_COLS)
                ps = opened("ada_row", n)
                for k in range(KD):
                    for g in range(4):
                        pe.matmul(ps[32 * g:32 * g + 32, 0:P], csil[:, k, :], w[:, k, g * P:g * P + P],
                                  start=(k == 0), stop=(k == KD - 1))
                for i in range(KD // 2):
                    for g in range(4):
                        k, at_ = i + KD // 2 * (g // 2), (4 + g % 2) * P
                        mm = pe.matmul(ps[32 * g:32 * g + 32, P:2 * P], csil[:, k, :], w[:, k, at_:at_ + P],
                                       start=(i == 0), stop=(i == KD // 2 - 1))
                closed(mm, "ada_row", n)

            def ada_turned(n):
                emptied(("ada_row", n))
                ps = opened("ada_t", n)
                for i in range(2):
                    mm = pe.transpose(ps[:, i * P:i * P + P], ada_row[:, n % 2, i * P:i * P + P], ident[:, :])
                closed(mm, "ada_t", n)

            def ada(turned, rows):
                for n in range(max(len(rows), len(turned))):
                    if n < len(rows):
                        ada_rows(rows[n])
                    if n < len(turned):
                        ada_turned(turned[n])

            sq_n = [0]

            def mean_squares(key, tiles, n):
                ps = opened(*key)
                for k in range(tiles):
                    sq_n[0] += 1
                    pe.wait_ge(s_sq, sq_n[0])
                    mm = pe.matmul(ps[:, 0:T], share[:, n, :], sq[:, sq_at[0] % 4, :], start=(k == 0), stop=(k == tiles - 1))
                    sq_at[0] += 1
                    if k < tiles - 1:
                        mm.then_inc(s_squ, 1)
                closed(mm, *key)

            sq_at = [0]

            def norm(q):
                if q in ADDED:
                    sq_n[0] += KD
                    pe.wait_ge(s_acc, (ADDED.index(q) + 1) * (KD - 1))
                    mm = pe.matmul(opened("norm", q)[:, 0:T], share[:, 0, :], acc[:, :], start=True, stop=True)
                    closed(mm, "norm", q)
                else:
                    sq_at[0] = 0
                    mean_squares(("norm", q), KD, 0)

            def normed(q, k):
                pe.wait_ge(s_hs, q * KD + k + 1)
                pe.wait_ge(s_hp, q * KD + k + 1)

            def transposed(key, w, j, x, ready=None):
                ps = opened(*key)
                for k in range(KD):
                    if ready is not None:
                        ready(k)
                    mm = pe.matmul(ps[:, 0:T], w[:, k, j * P:j * P + P], x[:, k, :], start=(k == 0), stop=(k == KD - 1))
                closed(mm, *key)

            pe.wait_ge(s_ones, 4)
            norm(0)
            pe.wait_ge(s_csil, 1)
            ada_rows(0)
            ada_rows(1)
            pe.wait_ge(s_consts, 16)
            ada([0, 1], [])
            ada([2], [2])

            def ev_in(n):
                transposed(("ev_in", n), weights(("ev_in", n // 6), 768), n % 6, hT,
                           (lambda k: normed(0, k)) if n == 0 else None)

            for n in range(6):
                ev_in(n)
            sq_at[0] = 0
            mean_squares(("q_norm",), NQ, 1)
            mean_squares(("kv_norm",), NKV, 2)
            for n in range(6, EV_TILES):
                ev_in(n)
            n = CHUNK_AT[("qkv", 0)]
            pe.wait_ge(ring_full[n % SLOTS], 16 * (n // SLOTS + 1))
            w_q = ring[:, n % SLOTS, 0:NQ * HEADS * P].rearrange("p (k n) -> p k n", k=NQ)
            w_kv = ring[:, n % SLOTS, NQ * HEADS * P:NQ * HEADS * P + NKV * 1024].rearrange("p (k n) -> p k n", k=NKV)
            pe.wait_ge(s_kn, NKV)
            pe.wait_ge(s_cache, 16)
            for t in range(NKEY // P):
                ps = opened("v_up", t)
                for k in range(NKV):
                    mm = pe.matmul(ps[:, :], ckvT[:, k, t * P:t * P + P], w_kv[:, k, 512:1024], start=(k == 0), stop=(k == NKV - 1))
                closed(mm, "v_up", t)
            pe.wait_ge(s_qn, NQ)
            for h in range(HEADS):
                ps = opened("q_up", h)
                for k in range(NQ):
                    mm = pe.matmul(ps[:, 0:T], w_q[:, k, h * P:h * P + P], q_a[:, k, :], start=(k == 0), stop=(k == NQ - 1))
                closed(mm, "q_up", h)
            for j in range(HEADS // 2):
                ps = opened("k_up", j)
                for k in range(NKV):
                    mm = pe.matmul(ps[:, :], w_kv[:, k, j * P:j * P + P], ckvT[:, k, :], start=(k == 0), stop=(k == NKV - 1))
                closed(mm, "k_up", j)

            def score(h):
                pe.wait_ge(s_qrope, h + 1)
                if h == 0:
                    pe.wait_ge(s_kropes, 1)
                    pe.wait_ge(s_cache, 32)
                if h % 2 == 0:
                    pe.wait_ge(s_even_key, h // 2 + 1)
                else:
                    emptied(("k_up", h // 2))
                ps = opened("score", h, 0)
                pe.matmul(ps[:, 0:P], qT[0:QK, h, 0:TP], kT[0:QK, h, 0:TP], start=True, stop=True)
                mm = pe.matmul(ps[:, P:512], qT[0:QK, h, TP:TP + P], kT[0:QK, h, TP:NKEY], start=True, stop=True)
                closed(mm, "score", h, 0)
                ps = opened("score", h, 1)
                mm = pe.matmul(ps[:, 0:384], qT[0:QK, h, TP + P:T], kT[0:QK, h, TP:NKEY], start=True, stop=True)
                closed(mm, "score", h, 1)

            def turn(h):
                pe.wait_ge(s_prob, h + 1)
                pr = probs[:, h % 2, :]
                tiles = [0] + [x for kt in range(3) for x in (1 + kt, 4 + kt)]
                for c, part in enumerate((tiles[:4], tiles[4:])):
                    ps = opened("probs_t", h, c)
                    for n, x in enumerate(part):
                        mm = pe.transpose(ps[:, n * P:n * P + P], pr[:, x * P:x * P + P], ident[:, :])
                    closed(mm, "probs_t", h, c)

            def attend(pair):
                for h in (2 * pair, 2 * pair + 1):
                    emptied(("probs_t", h, 0))
                    emptied(("probs_t", h, 1))
                if pair == 0:
                    for t in range(NKEY // P):
                        emptied(("v_up", t))
                ps = opened("attend", pair)

                def half(c, key_tile, queries, probs, start, stop):
                    at_ = (2 * pair + c) * VD
                    return pe.matmul(ps[c * VD:c * VD + VD, queries], values[:, key_tile, at_:at_ + VD],
                                     probs_t[:, c, probs], start=start, stop=stop)

                for c in range(2):
                    half(c, 0, slice(0, TP), slice(0, P), True, True)
                for kt in range(3):
                    for c in range(2):
                        mm = half(c, 1 + kt, slice(TP, T), slice(P + kt * TS, P + (kt + 1) * TS), kt == 0, kt == 2)
                closed(mm, "attend", pair)

            for s in range(HEADS + 2):
                if s < HEADS:
                    score(s)
                ada(attention_ada(s)[1], attention_ada(s)[0])
                if 1 <= s <= HEADS:
                    turn(s - 1)
                if s >= 3 and s % 2:
                    attend(s // 2 - 1)

            def mixed(l):
                def even(k):
                    if k < 4:
                        emptied(("ev_in", 14 + k))
                    else:
                        emptied(("attend", k - 4))

                return even if l == 0 else lambda k: pe.wait_ge(s_sg, k + 1)

            def mix_out(l):
                for d in range(KD):
                    transposed(("mix_out", l, d), weights(("ev_out" if l == 0 else "gm_out", d // 4), 512), d % 4, mixT,
                               mixed(l) if d == 0 else None)

            mix_out(0)

            def dispatch(l):
                ps = opened("router", l)
                for k in range(KD):
                    g = k % 4
                    normed(2 * l + 1, k)
                    mm = pe.matmul(ps[32 * g:32 * g + 32, 0:T], router_w[:, k, :], hT[:, k, :], start=(k < 4), stop=(k >= 4))
                closed(mm, "router", l)
                emptied(("router", l))
                ps = opened("logits", l)
                for t in range(NT):
                    mm = pe.transpose(ps[:, t * P:t * P + P], logit_t[:, t * P:t * P + P], ident[:, :])
                closed(mm, "logits", l)
                for t in range(NT):
                    for c in range(2):
                        ps = opened("h_row", l, t, c)
                        for k in range(4):
                            mm = pe.transpose(ps[:, k * P:k * P + P], hT[:, 4 * c + k, t * P:t * P + P], ident[:, :])
                        closed(mm, "h_row", l, t, c)
                if l == 0:
                    ada([8], [9])
                pe.wait_ge(s_mask, l + 1)
                pe.wait_ge(s_prefix, 2)
                ps = opened("slots", l)
                pe.matmul(ps[:, 0:NT * NE], earlier_b[:, :], top_b[:, :], start=True, stop=False)
                for u in range(1, NT):
                    pe.matmul(ps[:, u * NE:NT * NE], ones_b[:, :], top_b[:, 0:(NT - u) * NE], start=False, stop=(u == NT - 1))
                for t in range(NT):
                    mm = pe.matmul(ps[:, NT * NE:NT * NE + NE], ones_b[:, :], top_b[:, t * NE:t * NE + NE],
                                   start=(t == 0), stop=(t == NT - 1))
                closed(mm, "slots", l)
                pe.wait_ge(s_most, l + 1)
                count = pe.value_load(most_i[0:1, l:l + 1], min_val=0, max_val=T)
                for g in range(NE // SLOTS):
                    if g == 1:
                        ada([9] if l == 0 else [], [10 if l == 0 else 15])
                    pe.wait_ge(s_chosen, NE // SLOTS * l + g + 1)
                    ps = opened("table", l, g)
                    for j in range(SLOTS):
                        for t in range(NT):
                            mm = pe.matmul(ps[:, j:j + 1], chosen[:, g, t, j, :], token_h[:, t:t + 1],
                                           start=(t == 0), stop=(t == NT - 1))
                    closed(mm, "table", l, g)
                ada_turned(10 if l == 0 else 15)
                return count

            def experts_all(l):
                chunk = CHUNK_AT[("moe", (l, 0))]
                with pe.Fori(0, NE // SLOTS) as i:
                    def up(n, tiles):
                        j, t = n // NT, n % NT
                        s, turn = (chunk + j) % SLOTS, (chunk + j) // SLOTS
                        if t == 0 and 0 in tiles:
                            pe.wait_ge(ring_full[s], i * 16 + 16 * (turn + 1))
                        for k in tiles:
                            mm = pe.matmul(bank[n % 2][:, :], hT[:, k, t * P:t * P + P], ring[:, s, k * 512:k * 512 + 512],
                                           start=(k == 0), stop=(k == KD - 1))
                        if KD - 1 in tiles:
                            mm.then_inc(s_dup[l], 1)

                    def turned(n):
                        b = n % 2
                        pe.wait_ge(s_dhid[l], i * (SLOTS * NT) + (n + 1))
                        for c in range(2):
                            tr = pe.transpose(bank[2 + b][:, c * P:c * P + P], hidden[:, b, c * P:c * P + P], ident[:, :])
                        tr.then_inc(s_dtr[l], 1)

                    def down(n):
                        b, s = n % 2, (chunk + n // NT) % SLOTS
                        pe.wait_ge(s_dht[l], i * (SLOTS * NT) + (n + 1))
                        if n >= 1:
                            pe.wait_ge(s_dt[l], i * (SLOTS * NT) + n)
                        mm = down_matmuls(bank[4 + 2 * b:6 + 2 * b], b, s)
                        mm.then_inc(s_expert[l] if n % NT == NT - 1 else s_dn[l], 1)

                    up(0, range(KD))
                    for n in range(SLOTS * NT):
                        if n + 1 < SLOTS * NT:
                            up(n + 1, range(KD // 2))
                        turned(n)
                        if n + 1 < SLOTS * NT:
                            up(n + 1, range(KD // 2, KD))
                        down(n)
                    pe.wait_ge(s_dt[l], i * (SLOTS * NT) + SLOTS * NT)
                pe.wait_ge(s_dt[l], NE * NT + 1)

            def down_matmuls(ps, b, s):
                for half in range(2):
                    for c in range(2):
                        at_ = KD * 2 * F + c * D + half * 512
                        mm = pe.matmul(ps[half][:, :], hiddenT[:, b, c * P:c * P + P], ring[:, s, at_:at_ + 512],
                                       start=(c == 0), stop=(c == 1))
                return mm

            def experts_routed(l):
                chunk = CHUNK_AT[("moe", (l, 0))]

                def turn_h(i, e):
                    b = e % 2
                    pe.wait_ge(s_h[l][b], i * 32 + 16 * (e // 2 + 1))
                    wait(pe, s_copy0[l], i * SLOTS + e)
                    for k in range(4):
                        tr = pe.transpose(bank[2][:, k * P:k * P + P], h_slot[:, b, k * P:k * P + P], ident[:, :])
                    tr.then_inc(s_turn0[l], 1)
                    wait(pe, s_copy1[l], i * SLOTS + e)
                    for k in range(4, 8):
                        tr = pe.transpose(bank[3][:, (k - 4) * P:(k - 3) * P], h_slot[:, b, k * P:k * P + P], ident[:, :])
                    tr.then_inc(s_turn1[l], 1)

                def up(i, e, tiles):
                    s, turn = (chunk + e) % SLOTS, (chunk + e) // SLOTS
                    if 0 in tiles:
                        pe.wait_ge(ring_full[s], i * 16 + 16 * (turn + 1))
                        pe.wait_ge(s_copy0[l], i * SLOTS + (e + 1))
                        wait(pe, s_hid[l], i * SLOTS + (e - 1))
                    if 4 in tiles:
                        pe.wait_ge(s_copy1[l], i * SLOTS + (e + 1))
                    for k in tiles:
                        mm = pe.matmul(bank[e % 2][:, :], h_slotT[:, e % 2, k * P:k * P + P],
                                       ring[:, s, k * 512:k * 512 + 512], start=(k == 0), stop=(k == KD - 1))
                    if KD - 1 in tiles:
                        mm.then_inc(s_up[l], 1)

                turn_h(0, 0)
                up(0, 0, range(KD // 2))
                turn_h(0, 1)
                up(0, 0, range(KD // 2, KD))

                def round_(i, static):
                    for j in range(SLOTS):
                        b = j % 2
                        last = static and i > 0
                        more = not (last and j == SLOTS - 1)
                        if more:
                            up(i, j + 1, range(KD // 2))
                        pe.wait_ge(s_hid[l], i * SLOTS + (j + 1))
                        for c in range(2):
                            tr = pe.transpose(bank[6 + b][:, c * P:c * P + P], hidden[:, b, c * P:c * P + P], ident[:, :])
                        tr.then_inc(s_tr[l], 1)
                        if more:
                            up(i, j + 1, range(KD // 2, KD))
                        if not (last and j >= SLOTS - 2):
                            turn_h(i, j + 2)
                        pe.wait_ge(s_ht[l], i * SLOTS + (j + 1))
                        wait(pe, s_y0[l], i * SLOTS + j)
                        wait(pe, s_y1[l], i * SLOTS + j)
                        down_matmuls(bank[4:6], b, (chunk + j) % SLOTS).then_inc(s_expert[l], 1)

                rounds(pe, round_)

            def moe(l, count):
                n = PRODUCT_AT[("ada_t", 10 if l == 0 else 15)]
                for key in PRODUCTS[n - BANKS + 1:n + 1]:
                    emptied(key)
                with pe.If(count < P + 1):
                    experts_routed(l)
                    pe.wait_ge(s_y0[l], NE)
                    pe.wait_ge(s_y1[l], NE)
                    if l == 0:
                        ada([], [11, 12])
                        ada([11, 12], [])
                    pe.wait_ge(s_sum[l], NT)
                with pe.Else():
                    experts_all(l)
                    if l == 0:
                        ada([], [11, 12])
                        ada([11, 12], [])

            def moe_add(l):
                for d in range(KD):
                    ps = opened("moe_t", l, d)
                    for t in range(NT):
                        mm = pe.transpose(ps[:, t * P:t * P + P], moe_out[:, t, d * P:d * P + P], ident[:, :])
                    closed(mm, "moe_t", l, d)

            norm(1)
            ada_rows(8)
            moe(0, dispatch(0))
            moe_add(0)
            norm(2)
            ada_rows(13)

            for c in range(2):
                w = weights(("gm_in", c), 512)
                if c == 1:
                    ada_turned(13)
                for t in range(NT):
                    ps = opened("gm_v", t, c)
                    for k in range(KD):
                        if c == 0 and t == 0:
                            normed(2, k)
                        mm = pe.matmul(ps[:, :], hT[:, k, t * P:t * P + P], w[:, k, :], start=(k == 0), stop=(k == KD - 1))
                    closed(mm, "gm_v", t, c)
            for j in range(KD):
                transposed(("gm_u", j), weights(("gm_in", 2 + j // 4), 512), j % 4, hT)
            pe.wait_ge(s_vn, NT)
            pe.wait_ge(s_odd, 48)
            for g in range(KD):
                ps = opened("spatial", g)
                for t in range(NT):
                    mm = pe.matmul(ps[:, t * P:t * P + P], v_rows[:, t, g * P:g * P + P], w_sT[:, g, :], start=True, stop=True)
                closed(mm, "spatial", g)
            mix_out(1)
            ada_rows(14)
            norm(3)
            ada_turned(14)
            moe(1, dispatch(1))
            moe_add(1)
            norm(4)


_LOADED = ("cvec", "xT", "smalls",
           "cache_ckv", "cache_krope", "v_gain", "b_s", "w_sT", "ada_w", "ev_in", "qkv", "ev_out", "gm_in", "gm_out", "moe")


def tiles_first(w):
    return w.reshape(w.shape[0] // P, P, -1).transpose(1, 0, 2)


def rope_swap(w):
    return w.reshape(*w.shape[:-1], 2, 2, ROPE // 4)[..., ::-1, :].reshape(w.shape)


def laid_out(x_prompt, x_sample, cache_ckv, cache_krope, c, c_ctx, w_ada, b_ada, g_mix, g_ffn, g_final,
             ev_w_in, conv_w, q_norm_g, w_q_up, kv_norm_g, w_kv_up, ev_w_out,
             gm_w_in, gm_v_g, gm_w_s, gm_b_s, gm_w_out, router_w, router_b, moe_w1, moe_w3, moe_w2):
    o = {}
    o["xT"] = tiles_first(np.concatenate([x_prompt[0], x_sample[0]]).T)
    o["cvec"] = tiles_first(np.stack([c_ctx, c[0]], 1))
    cols = lambda v: v.reshape(-1, P).T
    o["b_ada"] = np.stack([cols(b_ada[l, h * 3 * D:(h + 1) * 3 * D]) for l in range(LAYERS) for h in range(2)], 1)
    o["gains"] = np.stack([cols(g) for g in (g_mix[0], g_ffn[0], g_mix[1], g_ffn[1], g_final)], 1)
    o["conv_w"] = conv_w[0].T.reshape(4, P, 3).transpose(1, 0, 2)
    o["qkv_g"] = np.concatenate([cols(q_norm_g[0]), cols(kv_norm_g[0])], 1)
    o["ident"] = np.eye(P, dtype=np.float32)
    tiny = np.finfo(np.float32).tiny
    o["threshold"] = np.broadcast_to(np.triu(np.full((EPG, EPG), tiny, np.float32)).reshape(1, -1), (P, EPG * EPG))
    o["expert_base"] = np.broadcast_to(np.tile(np.arange(NE, dtype=np.float32) * P, NT)[None], (P, NT * NE))
    o["token"] = np.arange(T, dtype=np.float32).reshape(NT, P).T
    o["place"] = np.broadcast_to(np.arange(1, P + 1, dtype=np.float32)[None], (P, P))
    o["earlier"] = np.triu(np.ones((P, P), np.float32), 1)
    pos = np.arange(TS)
    freq = 10000.0 ** (-np.arange(ROPE // 4, dtype=np.float32) / np.float32(ROPE // 4))
    ang = np.stack([(pos // 64)[:, None] * freq, (pos % 64)[:, None] * freq], 1).astype(np.float32)
    cos = np.repeat(np.cos(ang)[:, :, None, :], 2, 2).reshape(TS, ROPE).T
    sin = (np.sin(ang)[:, :, None, :] * np.array([-1.0, 1.0])[None, None, :, None]).reshape(TS, ROPE).T
    rope = np.zeros((P, T), np.float32)
    rope[NOPE:QK, :TP] = 1.0
    rope[NOPE:QK, TP:] = cos
    rope[QK:P, TP:] = sin
    o["rope"] = rope
    o["router_w"] = tiles_first(np.concatenate([router_w, np.zeros((D, 32 - NE), np.float32)], 1))
    o["router_b"] = np.broadcast_to(router_b[None], (P, NE))
    o["smalls"] = np.concatenate([np.reshape(o[name], (P, -1)) for name, _ in SMALLS], 1)
    o["cache_ckv"] = tiles_first(cache_ckv[0, 0].T)
    o["cache_krope"] = np.broadcast_to(cache_krope[0, 0].T[:, None, :], (ROPE, HEADS, PAST))
    o["v_gain"] = gm_v_g[0][None]
    o["b_s"] = gm_b_s[0][None]
    o["w_sT"] = gm_w_s[0].transpose(2, 0, 1)
    chunked = lambda w, n: np.stack([tiles_first(w[:, i:i + n]).reshape(P, -1) for i in range(0, w.shape[1], n)])
    o["ada_w"] = np.stack([chunked(w_ada[l][:, h * 3 * D:(h + 1) * 3 * D], ADA_COLS)
                           for l in range(LAYERS) for h in range(2)])
    b, cg, v, qa, kva, kr = np.split(ev_w_in[0], [512, 1024, 1536, 1920, 2176], axis=1)
    cv = np.stack([cg.reshape(D, 4, P), v.reshape(D, 4, P)], 2).reshape(D, 1024)
    o["ev_in"] = chunked(np.concatenate([qa, kva, np.zeros((D, NOPE), np.float32), kr, rope_swap(kr), cv, b], 1), 768)
    q = w_q_up[0].reshape(QR, HEADS, QK)
    q = np.concatenate([q, rope_swap(q[..., NOPE:])], -1).reshape(QR, HEADS * P)
    kv = w_kv_up[0].reshape(KVR, HEADS, 2, NOPE).transpose(0, 2, 1, 3).reshape(KVR, 1024)
    o["qkv"] = np.concatenate([tiles_first(q).reshape(P, -1), tiles_first(kv).reshape(P, -1)], 1)[None]
    o["ev_out"] = chunked(ev_w_out[0], 512)
    o["gm_in"] = chunked(np.concatenate([gm_w_in[0][:, D:], gm_w_in[0][:, :D]], 1), 512)
    o["gm_out"] = chunked(gm_w_out[0], 512)
    w13 = np.concatenate([moe_w1, moe_w3], -1).reshape(LAYERS, NE, KD, P, 2 * F).transpose(0, 1, 3, 2, 4)
    w2 = moe_w2.reshape(LAYERS, NE, F // P, P, D).transpose(0, 1, 3, 2, 4)
    o["moe"] = np.concatenate([w13.reshape(LAYERS, NE, P, -1), w2.reshape(LAYERS, NE, P, -1)], -1)
    return o


def kernel(**inputs):
    import concourse.bacc as bacc
    from concourse.bass_utils import run_bass_kernel_spmd

    nc = bacc.Bacc("TRN2", target_bir_lowering=False, num_devices=1)
    host = laid_out(**{k: np.asarray(v) for k, v in inputs.items()})
    arrays, a = {}, {}
    for name in _LOADED:
        x = np.ascontiguousarray(host[name], dtype=np.float32)
        arrays[f"in_{name}"] = x
        a[name] = nc.dram_tensor(f"in_{name}", x.shape, F32, kind="ExternalInput").ap()
    shapes = {"y": (P, KD, T), "state_ckv": (P, NKV, TP), "state_krope": (ROPE, TP)}
    out = {n: nc.dram_tensor(f"out_{n}", s, F32, kind="ExternalOutput").ap() for n, s in shapes.items()}
    build(nc, a, out)
    r = run_bass_kernel_spmd(nc, [arrays], core_ids=[0]).results[0]
    y = np.asarray(r["out_y"]).transpose(2, 1, 0).reshape(T, D)
    ckv = np.asarray(r["out_state_ckv"]).transpose(2, 1, 0).reshape(1, 1, TP, KVR)
    krope = np.asarray(r["out_state_krope"]).T.reshape(1, 1, TP, ROPE)
    return y[None, :TP], y[None, TP:], ckv, krope
```
